# Optimizing a Trainium2 kernel written in Bass

```python
import jax, jax.numpy as jnp
from jax import lax
import numpy as np

D_MODEL = 1024
BATCH = 1
SEQ = 128
DEPTH = 2
DEC_BATCH = 1
DEC_SEQ = 512
PAST_LEN = 128

GRID_W = 64
N_EVEN = (DEPTH + 1) // 2
N_ODD = DEPTH // 2
N_MOD = 6
RMS_EPS = 1e-6
ROPE_THETA = 10000.0
NEG_INF = -1e30
Q_BLOCK = 128

CONV_DIM = 512
CONV_W = 3
HEAD_DIM_B = 64
N_HEADS_B = 8
N_KV_B = 2
WINDOW = 128
BAND_BLOCK = 128
EVEN_IN = 3 * CONV_DIM + (N_HEADS_B + 2 * N_KV_B) * HEAD_DIM_B
EVEN_OUT = CONV_DIM + N_HEADS_B * HEAD_DIM_B
N_HEADS_C = 8
Q_LORA = 384
KV_LORA = 256
NOPE_C = 64
ROPE_C = 32
V_DIM_C = 64
MLA_SCALE = (NOPE_C + ROPE_C) ** -0.5
CHUNK = 128
N_GROUPS_D = 4
GROUP_DIM_D = 128
D_D = N_GROUPS_D * GROUP_DIM_D
ODD_IN = Q_LORA + KV_LORA + ROPE_C + 2 * D_D
ODD_OUT = N_HEADS_C * V_DIM_C + D_D
PEER_HEADS = 8
PEER_DK = 256
N_KEYS = 128
N_EXPERTS = N_KEYS * N_KEYS
PEER_TOPK = 16
PEER_BLOCK = 128

kernel_name = "hybrid_diffusion_prefix_step"

def rmsnorm(x, g):
    xf = x.astype(jnp.float32)
    y = xf * lax.rsqrt(jnp.mean(xf * xf, axis=-1, keepdims=True) + RMS_EPS)
    return (y * g.astype(jnp.float32)).astype(x.dtype)

def modulation(cvec, w_mod, b_mod):
    m = jax.nn.silu(cvec) @ w_mod + b_mod
    return m.reshape(cvec.shape[0], N_MOD, D_MODEL)

def adaln(x, g, shift, scale):
    return rmsnorm(x, g) * (1.0 + scale[:, None, :]) + shift[:, None, :]

def axial_rope(x):
    s, dr = x.shape[1], x.shape[-1]
    rows = s // GRID_W
    t = jnp.arange(rows * GRID_W)
    row = (t // GRID_W).astype(jnp.float32)
    col = (t % GRID_W).astype(jnp.float32)
    n_freq = dr // 4
    freqs = jnp.power(ROPE_THETA, -jnp.arange(n_freq, dtype=jnp.float32) / n_freq)
    ang = jnp.concatenate([row[:, None] * freqs, col[:, None] * freqs], axis=-1)[:, None, :]
    cos, sin = jnp.cos(ang), jnp.sin(ang)
    xf = x.astype(jnp.float32)
    x1, x2 = xf[..., : dr // 2], xf[..., dr // 2:]
    return jnp.concatenate([x1 * cos - x2 * sin, x1 * sin + x2 * cos], axis=-1).astype(x.dtype)

def short_conv3(u, w):
    up = jnp.pad(u, ((0, 0), (1, 1), (0, 0)))
    return up[:, :-2] * w[0] + up[:, 1:-1] * w[1] + up[:, 2:] * w[2]

def attend_blocked(q, k, v, scale, sink=None):
    b, sq, h, dq = q.shape
    hkv = k.shape[2]
    g = h // hkv
    dv = v.shape[-1]
    nb = sq // Q_BLOCK
    qb = jnp.moveaxis(q.reshape(b, nb, Q_BLOCK, hkv, g, dq), 1, 0)

    def block(qblk):
        s = jnp.einsum('bqhgd,bkhd->bhgqk', qblk, k).astype(jnp.float32) * scale
        if sink is not None:
            sk = jnp.broadcast_to(sink.astype(jnp.float32).reshape(1, hkv, g, 1, 1), s.shape[:-1] + (1,))
            p = jax.nn.softmax(jnp.concatenate([s, sk], axis=-1), axis=-1)[..., :-1]
        else:
            p = jax.nn.softmax(s, axis=-1)
        return jnp.einsum('bhgqk,bkhd->bqhgd', p.astype(v.dtype), v)

    o = lax.map(block, qb)
    return jnp.moveaxis(o, 0, 1).reshape(b, sq, h, dv)

def window_attn_ctx(q, k, v, kc, vc, sink, scale):
    b, s, h, d = q.shape
    hkv = k.shape[2]
    g = h // hkv
    nb = s // BAND_BLOCK
    sc = kc.shape[1]
    qb = q.reshape(b, nb, BAND_BLOCK, hkv, g, d)

    def neighbours(x):
        xr = x.reshape(b, nb, BAND_BLOCK, hkv, x.shape[-1])
        xp = jnp.pad(xr, ((0, 0), (1, 1), (0, 0), (0, 0), (0, 0)))
        return jnp.concatenate([xp[:, :-2], xp[:, 1:-1], xp[:, 2:]], axis=2)

    kw, vw = neighbours(k), neighbours(v)
    s_loc = jnp.einsum('bnqhgd,bnkhd->bnhgqk', qb, kw).astype(jnp.float32) * scale
    qi = jnp.arange(BAND_BLOCK)[:, None]
    kj = jnp.arange(3 * BAND_BLOCK)[None, :]
    in_window = jnp.abs(kj - BAND_BLOCK - qi) <= WINDOW
    key_block = jnp.arange(nb)[:, None, None] + (kj // BAND_BLOCK - 1)[None]
    valid = in_window[None] & (key_block >= 0) & (key_block < nb)
    s_loc = jnp.where(valid[None, :, None, None], s_loc, NEG_INF)
    s_ctx = jnp.einsum('bnqhgd,bkhd->bnhgqk', qb, kc).astype(jnp.float32) * scale
    sk = jnp.broadcast_to(sink.astype(jnp.float32).reshape(1, 1, hkv, g, 1, 1), s_ctx.shape[:-1] + (1,))
    p = jax.nn.softmax(jnp.concatenate([s_ctx, s_loc, sk], axis=-1), axis=-1)
    p_ctx = p[..., :sc].astype(v.dtype)
    p_loc = p[..., sc:sc + 3 * BAND_BLOCK].astype(v.dtype)
    o = (jnp.einsum('bnhgqk,bkhd->bnqhgd', p_ctx, vc)
         + jnp.einsum('bnhgqk,bnkhd->bnqhgd', p_loc, vw))
    return o.reshape(b, s, h, d)

def even_project(h, w_in, conv_w):
    b, s, _ = h.shape
    nq = N_HEADS_B * HEAD_DIM_B
    nkv = N_KV_B * HEAD_DIM_B
    z = h @ w_in
    gb, gc, xa, q, k, v = jnp.split(
        z, [CONV_DIM, 2 * CONV_DIM, 3 * CONV_DIM, 3 * CONV_DIM + nq, 3 * CONV_DIM + nq + nkv], axis=-1)
    y_a = gb * short_conv3(gc * xa, conv_w)
    q = q.reshape(b, s, N_HEADS_B, HEAD_DIM_B)
    k = k.reshape(b, s, N_KV_B, HEAD_DIM_B)
    v = v.reshape(b, s, N_KV_B, HEAD_DIM_B)
    return y_a, q, k, v

def even_mixer_ctx(h, w_in, conv_w, sink, w_out):
    b, s, _ = h.shape
    y_a, q, k, v = even_project(h, w_in, conv_w)
    y_b = attend_blocked(q, k, v, HEAD_DIM_B ** -0.5, sink)
    out = jnp.concatenate([y_a, y_b.reshape(b, s, -1)], axis=-1) @ w_out
    return out, k, v

def even_mixer_lat(h, cache_k, cache_v, w_in, conv_w, sink, w_out):
    b, s, _ = h.shape
    y_a, q, k, v = even_project(h, w_in, conv_w)
    y_b = window_attn_ctx(axial_rope(q), axial_rope(k), v, cache_k, cache_v, sink, HEAD_DIM_B ** -0.5)
    return jnp.concatenate([y_a, y_b.reshape(b, s, -1)], axis=-1) @ w_out

def chunk_gmlp(dz, g_sgu, w_s, b_s):
    a = jax.nn.gelu(dz)
    u, vv = a[..., :D_D], a[..., D_D:]
    vv = rmsnorm(vv, g_sgu)
    b, s, _ = vv.shape
    vr = vv.reshape(b, s // CHUNK, CHUNK, N_GROUPS_D, GROUP_DIM_D)
    mixed = jnp.einsum('gpq,bnqgc->bnpgc', w_s, vr) + b_s.T[:, :, None]
    return u * mixed.reshape(b, s, D_D)

def odd_project(h, w_in, g_q, w_uq, g_kv, g_sgu, w_s, b_s):
    b, s, _ = h.shape
    z = h @ w_in
    cq, ckv, kr, dz = jnp.split(z, [Q_LORA, Q_LORA + KV_LORA, Q_LORA + KV_LORA + ROPE_C], axis=-1)
    q = (rmsnorm(cq, g_q) @ w_uq).reshape(b, s, N_HEADS_C, NOPE_C + ROPE_C)
    ckv_n = rmsnorm(ckv, g_kv)
    y_d = chunk_gmlp(dz, g_sgu, w_s, b_s)
    return q, ckv_n, kr, y_d

def mla_expand(ckv_n, w_ukv):
    b, s, _ = ckv_n.shape
    kv = (ckv_n @ w_ukv).reshape(b, s, N_HEADS_C, NOPE_C + V_DIM_C)
    return kv[..., :NOPE_C], kv[..., NOPE_C:]

def mla_keys(k_nope, k_rope):
    kr = jnp.broadcast_to(k_rope[:, :, None, :], k_nope.shape[:-1] + (ROPE_C,))
    return jnp.concatenate([k_nope, kr], axis=-1)

def odd_mixer_ctx(h, w_in, g_q, w_uq, g_kv, w_ukv, g_sgu, w_s, b_s, w_out):
    b, s, _ = h.shape
    q, ckv_n, kr, y_d = odd_project(h, w_in, g_q, w_uq, g_kv, g_sgu, w_s, b_s)
    k_nope, v = mla_expand(ckv_n, w_ukv)
    y_c = attend_blocked(q, mla_keys(k_nope, kr), v, MLA_SCALE)
    out = jnp.concatenate([y_c.reshape(b, s, -1), y_d], axis=-1) @ w_out
    return out, ckv_n, kr

def odd_mixer_lat(h, cache_ckv, cache_krope, w_in, g_q, w_uq, g_kv, w_ukv, g_sgu, w_s, b_s, w_out):
    b, s, _ = h.shape
    q, ckv_n, kr, y_d = odd_project(h, w_in, g_q, w_uq, g_kv, g_sgu, w_s, b_s)
    q = jnp.concatenate([q[..., :NOPE_C], axial_rope(q[..., NOPE_C:])], axis=-1)
    kr_lat = axial_rope(kr[:, :, None, :])[:, :, 0]
    k_nope_l, v_l = mla_expand(ckv_n, w_ukv)
    k_nope_c, v_c = mla_expand(cache_ckv, w_ukv)
    k_all = jnp.concatenate([mla_keys(k_nope_c, cache_krope), mla_keys(k_nope_l, kr_lat)], axis=1)
    v_all = jnp.concatenate([v_c, v_l], axis=1)
    y_c = attend_blocked(q, k_all, v_all, MLA_SCALE)
    return jnp.concatenate([y_c.reshape(b, s, -1), y_d], axis=-1) @ w_out

def peer(h, wq, subkeys, u_tab, v_tab):
    b, s, d = h.shape
    xb_all = h.reshape((b * s) // PEER_BLOCK, PEER_BLOCK, d)

    def block(xb):
        tb = xb.shape[0]
        q = (xb @ wq).reshape(tb, PEER_HEADS, 2, PEER_DK // 2)
        sc = jnp.einsum('thsd,hskd->thsk', q, subkeys).astype(jnp.float32)
        sv, si = lax.top_k(sc, PEER_TOPK)
        cand = (sv[:, :, 0, :, None] + sv[:, :, 1, None, :]).reshape(tb, PEER_HEADS, PEER_TOPK * PEER_TOPK)
        best, ci = lax.top_k(cand, PEER_TOPK)
        i1 = jnp.take_along_axis(si[:, :, 0], ci // PEER_TOPK, axis=-1)
        i2 = jnp.take_along_axis(si[:, :, 1], ci % PEER_TOPK, axis=-1)
        idx = i1 * N_KEYS + i2
        gsm = jax.nn.softmax(best, axis=-1)
        ue = u_tab[idx]
        act = jax.nn.gelu(jnp.einsum('td,thkd->thk', xb, ue))
        ve = v_tab[idx]
        return jnp.einsum('thk,thkd->td', (gsm * act).astype(ve.dtype), ve)

    return lax.map(block, xb_all).reshape(b, s, d)

def setup_inputs(seed: int = 0) -> dict:
    key = jax.random.key(seed)
    ks = iter(jax.random.split(key, 32))

    def nrm(shape, scale=1.0):
        return scale * jax.random.normal(next(ks), shape, jnp.float32)

    def gain(shape):
        return 1.0 + 0.05 * jax.random.normal(next(ks), shape, jnp.float32)

    D = D_MODEL
    return {
        'x_prompt': nrm((BATCH, SEQ, D)),
        'x_sample': nrm((DEC_BATCH, DEC_SEQ, D)),
        'cache_attn_k': nrm((DEC_BATCH, N_EVEN, PAST_LEN, N_KV_B, HEAD_DIM_B)),
        'cache_attn_v': nrm((DEC_BATCH, N_EVEN, PAST_LEN, N_KV_B, HEAD_DIM_B)),
        'cache_mla_ckv': nrm((DEC_BATCH, N_ODD, PAST_LEN, KV_LORA)),
        'cache_mla_krope': nrm((DEC_BATCH, N_ODD, PAST_LEN, ROPE_C)),
        'c': nrm((DEC_BATCH, D)),
        'c_ctx': nrm((D,)),
        'w_mod': nrm((DEPTH, D, N_MOD * D), 0.5 * D ** -0.5),
        'b_mod': nrm((DEPTH, N_MOD * D), 0.02),
        'g_norm1': gain((DEPTH, D)),
        'g_norm2': gain((DEPTH, D)),
        'ev_w_in': nrm((N_EVEN, D, EVEN_IN), D ** -0.5),
        'ev_conv_w': nrm((N_EVEN, CONV_W, CONV_DIM), CONV_W ** -0.5),
        'ev_sink': nrm((N_EVEN, N_HEADS_B), 0.5),
        'ev_w_out': nrm((N_EVEN, EVEN_OUT, D), EVEN_OUT ** -0.5),
        'od_w_in': nrm((N_ODD, D, ODD_IN), D ** -0.5),
        'od_g_qnorm': gain((N_ODD, Q_LORA)),
        'od_w_uq': nrm((N_ODD, Q_LORA, N_HEADS_C * (NOPE_C + ROPE_C)), Q_LORA ** -0.5),
        'od_g_kvnorm': gain((N_ODD, KV_LORA)),
        'od_w_ukv': nrm((N_ODD, KV_LORA, N_HEADS_C * (NOPE_C + V_DIM_C)), KV_LORA ** -0.5),
        'od_g_sgu': gain((N_ODD, D_D)),
        'od_w_spatial': nrm((N_ODD, N_GROUPS_D, CHUNK, CHUNK), 0.5 * CHUNK ** -0.5),
        'od_b_spatial': gain((N_ODD, N_GROUPS_D, CHUNK)),
        'od_w_out': nrm((N_ODD, ODD_OUT, D), ODD_OUT ** -0.5),
        'peer_wq': nrm((DEPTH, D, PEER_HEADS * PEER_DK), D ** -0.5),
        'peer_subkeys': nrm((DEPTH, PEER_HEADS, 2, N_KEYS, PEER_DK // 2), (PEER_DK // 2) ** -0.5),
        'peer_u': nrm((DEPTH, N_EXPERTS, D), D ** -0.5),
        'peer_v': nrm((DEPTH, N_EXPERTS, D), 1.0),
        'g_final': gain((D,)),
    }

def reference(x_prompt, x_sample, cache_attn_k, cache_attn_v, cache_mla_ckv, cache_mla_krope, c, c_ctx,
              w_mod, b_mod, g_norm1, g_norm2, ev_w_in, ev_conv_w, ev_sink, ev_w_out,
              od_w_in, od_g_qnorm, od_w_uq, od_g_kvnorm, od_w_ukv, od_g_sgu, od_w_spatial, od_b_spatial,
              od_w_out, peer_wq, peer_subkeys, peer_u, peer_v, g_final):
    xp, xs = x_prompt, x_sample
    new_k, new_v, new_ckv, new_kr = [], [], [], []
    for layer in range(DEPTH):
        j = layer // 2
        mp = modulation(c_ctx[None, :], w_mod[layer], b_mod[layer])
        ms = modulation(c, w_mod[layer], b_mod[layer])
        hp = adaln(xp, g_norm1[layer], mp[:, 0], mp[:, 1])
        hs = adaln(xs, g_norm1[layer], ms[:, 0], ms[:, 1])
        if layer % 2 == 0:
            op, kp, vp = even_mixer_ctx(hp, ev_w_in[j], ev_conv_w[j], ev_sink[j], ev_w_out[j])
            os_ = even_mixer_lat(hs, cache_attn_k[:, j], cache_attn_v[:, j],
                                 ev_w_in[j], ev_conv_w[j], ev_sink[j], ev_w_out[j])
            new_k.append(kp)
            new_v.append(vp)
        else:
            op, ckv_p, kr_p = odd_mixer_ctx(hp, od_w_in[j], od_g_qnorm[j], od_w_uq[j], od_g_kvnorm[j],
                                            od_w_ukv[j], od_g_sgu[j], od_w_spatial[j], od_b_spatial[j],
                                            od_w_out[j])
            os_ = odd_mixer_lat(hs, cache_mla_ckv[:, j], cache_mla_krope[:, j],
                                od_w_in[j], od_g_qnorm[j], od_w_uq[j], od_g_kvnorm[j], od_w_ukv[j],
                                od_g_sgu[j], od_w_spatial[j], od_b_spatial[j], od_w_out[j])
            new_ckv.append(ckv_p)
            new_kr.append(kr_p)
        xp = xp + mp[:, 2][:, None, :] * op
        xs = xs + ms[:, 2][:, None, :] * os_
        hp = adaln(xp, g_norm2[layer], mp[:, 3], mp[:, 4])
        hs = adaln(xs, g_norm2[layer], ms[:, 3], ms[:, 4])
        xp = xp + mp[:, 5][:, None, :] * peer(hp, peer_wq[layer], peer_subkeys[layer], peer_u[layer], peer_v[layer])
        xs = xs + ms[:, 5][:, None, :] * peer(hs, peer_wq[layer], peer_subkeys[layer], peer_u[layer], peer_v[layer])
    y_prompt = rmsnorm(xp, g_final)
    y_sample = rmsnorm(xs, g_final)
    new_attn_k = jnp.stack(new_k, axis=1)
    new_attn_v = jnp.stack(new_v, axis=1)
    new_mla_ckv = jnp.stack(new_ckv, axis=1)
    new_mla_krope = jnp.stack(new_kr, axis=1)
    return (y_prompt, y_sample, new_attn_k, new_attn_v, new_mla_ckv, new_mla_krope)


_drawn_inputs = setup_inputs


def setup_inputs(seed=0):
    import zlib

    import numpy as np

    out = dict(_drawn_inputs(seed))
    spreads = {}
    factors = {'cache_mla_ckv': 4.232,
     'cache_mla_krope': 5.875,
     'ev_sink': 8.0,
     'od_g_qnorm': 8.0,
     'od_g_sgu': 16.122,
     'od_b_spatial': 10.947}
    for name, (base, spread) in spreads.items():
        noise = np.random.default_rng([zlib.crc32(name.encode()), seed]).standard_normal(out[name].shape)
        drawn = base * np.exp(spread * noise) if base else spread * noise
        out[name] = __import__('jax').numpy.asarray(drawn.astype(out[name].dtype))
    for name, factor in factors.items():
        out[name] = (out[name] * factor).astype(out[name].dtype)
    return out
```

```python
import concourse.bass as bass
from concourse import mybir
from contextlib import ExitStack

P = 128
D, KD = 1024, 8
NP_TOK, NL_TOK = 128, 512
T, NT = 640, 5
HALF = 320
NKEY, PICKS = 128, 128
NH = 8
EPS = 1e-6
SCALE_B, SCALE_C = 64.0 ** -0.5, 96.0 ** -0.5
RAW, SPLIT = 2, 8
GROUP = 4
NEG = -1.0e30


def plan():
    chunks, products = [], []

    def add(layer, kind, n, made=1, size=1024):
        for i in range(n):
            first = len(products)
            products.extend([(layer, kind, i, j, len(chunks)) for j in range(made)])
            chunks.append((layer, kind, i, size, first, len(products)))

    add(0, "in", 18)
    add(0, "out", 8)
    add(0, "wq", 16)
    add(0, "u", 128)
    add(0, "v", 128, made=0)
    add(1, "in", 14)
    add(1, "ukv_v", 1, made=3)
    add(1, "head", 8, made=2, size=3 * 96 + 2 * 128)
    add(1, "out", 8)
    add(1, "wq", 16)
    add(1, "u", 128)
    add(1, "v", 128, made=0)
    return chunks, products


CHUNKS, PRODUCTS = plan()


def chunk_at(layer, kind):
    return next(n for n, c in enumerate(CHUNKS) if c[0] == layer and c[1] == kind)


def product_at(layer, kind):
    return next(n for n, c in enumerate(PRODUCTS) if c[0] == layer and c[1] == kind)


def build(nc, a):
    F, R, U32 = mybir.dt.float32, mybir.dt.float32r, mybir.dt.uint32
    ALU, ACT, AX = mybir.AluOpType, mybir.ActivationFunctionType, mybir.AxisListType
    ctx = ExitStack()
    with ctx:
        slab_bytes = 212 * 1024 - 4480
        slab = ctx.enter_context(nc.sbuf_tensor("slab", [P, slab_bytes // 4], F))
        base = nc.sbuf_base - slab_bytes
        end = [base]

        def at(name, shape, off, dt=F):
            return nc.alloc_sbuf_tensor_at(name, shape, dt, offset=off)

        def sb(name, shape, dt=F):
            size = 4
            for n in shape[1:]:
                size *= n
            off = end[0]
            end[0] += (size + 31) // 32 * 32
            return at(name, shape, off, dt)

        def sem(name):
            return ctx.enter_context(nc.semaphore(name))

        x = sb("x", [P, KD, T])
        act_at = end[0]
        a_hi = sb("a_hi", [P, KD, T], R)
        a_lo = sb("a_lo", [P, KD, T], R)
        raw = sb("raw", [P, RAW, 1024])
        w_hi = sb("w_hi", [P, SPLIT, 1024], R)
        w_lo = sb("w_lo", [P, SPLIT, 1024], R)
        ident = sb("ident", [P, P])
        ones = sb("ones", [P, P])
        iota = sb("iota", [P, P])
        mask = sb("mask", [P, 384])
        perm = sb("perm", [P, P])
        rope = sb("rope", [P, 2, NL_TOK])
        mod = sb("mod", [P, 2, 48, 2])
        b_mod = sb("b_mod", [P, 2, 48])
        g_norm = sb("g_norm", [P, 5, KD])
        gain = sb("gain", [P, 4, KD, 2])
        cvec = sb("cvec", [P, KD, 2])
        silu_c = sb("silu_c", [P, KD, 2])
        sink = sb("sink", [P, NH])
        conv_w = sb("conv_w", [P, 4, 3])
        g_small = sb("g_small", [P, 5])
        stat = sb("stat", [P, 2, 8])
        ss = sb("ss", [P, 8])
        tmp_at = end[0]
        tmp = sb("tmp", [P, 2, T])
        rstd = sb("rstd", [P, T])
        picks = at("picks", [P, 3, NT, PICKS], tmp_at)
        work = end[0]
        a_out = sb("a_out", [P, 2, T])
        work = end[0]
        room = base + slab_bytes - work
        assert room >= 54304, room

        y = at("y", [P, KD, T], work)
        kT = at("kT", [P, 768], work + 20480)
        vt = at("vt", [P, 6, P], work + 23552)
        u_pad = at("u_pad", [P, 648], work + 26624)
        gate_c = at("gate_c", [P, T], work + 29216)
        conv = at("conv", [P, 642], work + 31776)
        s_sb = at("s_sb", [P, 2, 512], work + 36416)
        pt_sb = at("pt_sb", [P, 2, 512], work + 40512)
        vv = at("vv", [P, NT, 512], work + 20480)
        vt1 = at("vt1", [P, 6, 512], work + 20480)
        cq = at("cq", [P, 3, T], work + 32768)
        ckv = at("ckv", [P, 2, T], work + 40448)
        ckv_old = at("ckv_old", [P, 2, P], work + 45568)
        kr = at("kr", [32, T], work + 46592)
        kr_rope = at("kr_rope", [32, 2, NL_TOK], work + 49152)
        p_sb = at("p_sb", [P, 2, T], work + 46592)
        pt1 = at("pt1", [P, T], work + 51712)
        ws_t = at("ws_t", [P, 4, P], work)
        b_s = at("b_s", [1, 4, P], work + 2048)
        g_sgu = at("g_sgu", [P, 512], work + 4096)
        cq_hi = at("cq_hi", [P, 3, T], act_at, R)
        cq_lo = at("cq_lo", [P, 3, T], act_at + 7680, R)
        ckv_hi = at("ckv_hi", [P, 2, 768], act_at + 15360, R)
        ckv_lo = at("ckv_lo", [P, 2, 768], act_at + 21504, R)
        k_head = at("k_head", [96, 2, 768], act_at + 27648)
        q_head = at("q_head", [96, 2, T], act_at + 33792)
        w_mod = at("w_mod", [P, 2, KD, 512], work)
        scores = at("scores", [P, NT, 16, NKEY], work)
        subk = at("subk", [P, 16, NKEY], work + 40960)
        cand = at("cand", [P, NH, 16, 16], work + 40960)
        top_v = at("top_v", [P, 16, 16], work + 49152)
        top_i = at("top_i", [P, 16, 16], work + 50176, U32)
        top_f = at("top_f", [P, 16, 16], work + 51200)
        best = at("best", [P, NH, 16], work + 52224)
        place = at("place", [P, NH, 16], work + 52736, U32)
        part_i = at("part_i", [P, NH, 16], work + 53248, U32)
        part_f = at("part_f", [P, NH, 16], work + 53760)
        g_sum = at("g_sum", [P, NH], work + 54272)
        gates = [at("gates0", [P, NKEY, 64], work), at("gates1", [P, NKEY, 64], act_at)]
        one_a = at("one_a", [P, 8, NKEY], work + 32768)
        one_b = at("one_b", [P, 8, NKEY], work + 36864)
        picks_t = at("picks_t", [P, 3, T], work + 40960)
        ag = at("ag", [P, 4, 2, T], work)
        p_raw = at("p_raw", [P, 2, T], work + 20480)

        acc = [ctx.enter_context(nc.psum_tensor(f"acc{i}", [P, 2, 512], F)) for i in range(2)]
        aux = [ctx.enter_context(nc.psum_tensor(f"aux{i}", [P, 2, 512], F)) for i in range(2)]

        const_in = sem("const_in")
        const1_in, cache_in, cache1_in = sem("const1_in"), sem("cache_in"), sem("cache1_in")
        raw_in = [sem(f"raw_in{i}") for i in range(RAW)]
        hi_done, lo_done, slot_free = sem("hi_done"), sem("lo_done"), sem("slot_free")
        made = sem("made")
        taken = [sem(f"taken{i}") for i in range(2)]
        mod_in = [sem(f"mod_in{i}") for i in range(2)]
        mod_used, silu_ready, mod_ready = sem("mod_used"), sem("silu_ready"), sem("mod_ready")
        dve_step, act_step = sem("dve_step"), sem("act_step")
        sq_ready, sq_used = sem("sq_ready"), sem("sq_used")
        var_ready, rstd_ready = sem("var_ready"), sem("rstd_ready")
        h_ready, hi_ready, lo_ready = sem("h_ready"), sem("hi_ready"), sem("lo_ready")
        rope_done, rope_applied = sem("rope_done"), sem("rope_applied")
        s_done, s_read = sem("s_done"), sem("s_read")
        neg_ready, e_ready, p_ready = sem("neg_ready"), sem("e_ready"), sem("p_ready")
        pt_done, pt_ready, pv_done, pv_read = sem("pt_done"), sem("pt_ready"), sem("pv_done"), sem("pv_read")
        state_out = sem("state_out")
        mix_done, mix_read, vv_ready = sem("mix_done"), sem("mix_read"), sem("vv_ready")
        conv_ready, ss_ready, ss_inv, ss_root = sem("conv_ready"), sem("ss_ready"), sem("ss_inv"), sem("ss_root")
        lat_norm, lat_hi, lat_lo, kr_ready = sem("lat_norm"), sem("lat_hi"), sem("lat_lo"), sem("kr_ready")
        sc_done, sc_read = sem("sc_done"), sem("sc_read")
        subk_in = sem("subk_in")
        shifted, exp_done, picks_ready = sem("shifted"), sem("exp_done"), sem("picks_ready")
        turned, turned_read = sem("turned"), sem("turned_read")
        hot_ready, hot_used, gate_read = sem("hot_ready"), sem("hot_used"), sem("gate_read")
        gates_out = [sem(f"gates_out{i}") for i in range(2)]
        a_st = [sem(f"a_stored{i}") for i in range(2)]
        ag_in = [sem(f"ag_in{i}") for i in range(4)]
        p_made, p_hi, p_lo = sem("p_made"), sem("p_hi"), sem("p_lo")
        v_done, v_taken = sem("v_done"), sem("v_taken")
        y_ready, y_out = sem("y_ready"), sem("y_out")
        block = ctx.enter_context(nc.Block())

        N_CONST, N_CONST1 = 13, 5
        OUT = {l: product_at(l, "out") for l in range(2)}
        WQ = {l: product_at(l, "wq") for l in range(2)}
        UM = {l: product_at(l, "u") for l in range(2)}
        IN = {l: product_at(l, "in") for l in range(2)}
        UKV, HEAD = product_at(1, "ukv_v"), product_at(1, "head")
        UC = {l: chunk_at(l, "u") for l in range(2)}
        VC = {l: chunk_at(l, "v") for l in range(2)}
        BODIES = NKEY // SPLIT
        NUNIT = NT * NH
        FIRST_G = {0: 0, 1: NKEY // GROUP}

        SQ = [0, 8, 16, 24, 27, 29, 37]
        UNITS0 = [(j, s, b) for j in range(4) for s in range(2) for b in range(NT)]

        def local(b):
            lo, hi = max(1, b - 1), min(4, b + 1)
            return lo + 1, hi - lo + 1

        def keys_of(b):
            return P if b == 0 else P + local(b)[1] * P

        def halves(t):
            return t.rearrange("p (h t) -> p h t", h=2)

        def wait(eng, s, value):
            if not isinstance(value, int) or value > 0:
                eng.wait_ge(s, value)

        def has_taken(eng, m):
            eng.wait_ge(taken[m % 2], m // 2 + 1)

        def source(n):
            layer, kind, i, size = CHUNKS[n][:4]
            if kind in ("u", "v"):
                return a[kind][layer, i]
            if kind == "wq":
                return a["wq"][layer, i]
            if kind == "head":
                return a["head"][i]
            if kind == "ukv_v":
                return a["ukv_v"]
            return a[f"{kind}{layer}"][i]

        @block.sync
        def _(sp):
            def load_chunk(n):
                if n >= RAW:
                    sp.wait_ge(lo_done, n - RAW + 1)
                sp.dma_start(raw[:, n % RAW, 0:CHUNKS[n][3]], source(n)).then_inc(raw_in[n % RAW], 16)

            for n in range(RAW):
                load_chunk(n)
            for l in range(2):
                for i in range(12):
                    k = 12 * l + i
                    if k >= 2:
                        sp.wait_ge(mod_used, k - 1)
                    sp.dma_start(w_mod[:, k % 2], a["w_mod"][l, i]).then_inc(mod_in[k % 2], 16)
            for l in range(2):
                for n in range(0 if l else RAW, len(CHUNKS)):
                    if CHUNKS[n][0] == l and CHUNKS[n][1] not in ("u", "v"):
                        load_chunk(n)
                with sp.Fori(0, BODIES) as i:
                    for u in range(SPLIT):
                        n = UC[l] + SPLIT * i + u
                        sp.wait_ge(lo_done, n - RAW + 1)
                        sp.dma_start(raw[:, (UC[l] + u) % RAW],
                                     a["u"][l, bass.ds(SPLIT * i + u, 1)].rearrange("o p n -> (o p) n"))\
                          .then_inc(raw_in[(UC[l] + u) % RAW], 16)
                for s in range(2):
                    sp.wait_ge(a_st[s], 16 * 64 * (l + 1))
                for s in range(2):
                    sp.wait_ge(gates_out[s], 16 * 5 * (l + 1))

                def load_v(i):
                    for u in range(SPLIT):
                        c = SPLIT * i + u
                        n = VC[l] + c
                        sp.wait_ge(lo_done, n - RAW + 1)
                        sp.dma_start(raw[:, (VC[l] + u) % RAW],
                                     a["v"][l, bass.ds(c, 1)].rearrange("o p n -> (o p) n"))\
                          .then_inc(raw_in[(VC[l] + u) % RAW], 16)
                        if not (isinstance(c, int) and c < 4):
                            sp.wait_ge(p_made, NKEY * l + c - 3)
                        for w, src in enumerate((a["act_s"], a["gate_s"])):
                            sp.dma_start(ag[:, u % 4, w],
                                         src[l, bass.ds(c, 1)].rearrange("o p n -> (o p) n"))\
                              .then_inc(ag_in[u % 4], 16)

                load_v(0)
                with sp.Fori(1, BODIES) as i:
                    load_v(i)
            for k in range(KD):
                sp.wait_ge(y_ready, k + 1)
                sp.dma_start(a["y"][:, k, :], y[:, k, :]).then_inc(y_out, 16)
            sp.wait_ge(y_out, 16 * KD)
            sp.wait_ge(state_out, 16 * 4)

        @block.gpsimd
        def _(pool):
            def low(n, slot, rslot, size):
                pool.wait_ge(hi_done, n + 1)
                pool.tensor_tensor(w_lo[:, slot, 0:size], raw[:, rslot, 0:size],
                                   w_hi[:, slot, 0:size].bitcast(F), ALU.subtract).then_inc(lo_done, 1)

            def last_use(n):
                layer, kind, i, size, first, past = CHUNKS[n]
                if kind == "v":
                    return v_done, 16 * (FIRST_G[layer] + i // GROUP + 1)
                return made, past

            def split_chunk(n):
                slot, rslot, size = n % SPLIT, n % RAW, CHUNKS[n][3]
                pool.wait_ge(raw_in[rslot], 16 * (n // RAW + 1))
                if n >= SPLIT:
                    pool.wait_ge(*last_use(n - SPLIT))
                pool.tensor_copy(w_hi[:, slot, 0:size], raw[:, rslot, 0:size]).then_inc(hi_done, 1)
                low(n, slot, rslot, size)

            def split_loop(first, free_sem, free_base, per_body, free_steps, start):
                with pool.Fori(start, BODIES) as i:
                    for u in range(SPLIT):
                        n0 = first + u
                        pool.wait_ge(raw_in[n0 % RAW], 16 * (n0 // RAW + 1) + 16 * (SPLIT // RAW) * i)
                        pool.wait_ge(free_sem, free_base + free_steps[u] + per_body * i)
                        pool.sem_inc(slot_free, 1)
                        pool.tensor_copy(w_hi[:, n0 % SPLIT, :], raw[:, n0 % RAW, :]).then_inc(hi_done, 1)
                        low(n0 + SPLIT * i, n0 % SPLIT, n0 % RAW, 1024)

            for l in range(2):
                for n in range(len(CHUNKS)):
                    if CHUNKS[n][0] == l and CHUNKS[n][1] not in ("u", "v"):
                        split_chunk(n)
                split_loop(UC[l], made, UM[l] - SPLIT, SPLIT, [u + 1 for u in range(SPLIT)], 0)
                for u in range(SPLIT):
                    split_chunk(VC[l] + u)
                split_loop(VC[l], v_done, 16 * FIRST_G[l], 32,
                           [16 * (u // GROUP) - 16 for u in range(SPLIT)], 1)

        @block.tensor
        def _(pe):
            def begin(m):
                pe.wait_ge(lo_done, PRODUCTS[m][4] + 1)
                if m >= 2:
                    pe.wait_ge(taken[m % 2], m // 2)
                return acc[m % 2], PRODUCTS[m][4] % SPLIT

            def linear(out, w, width, kt, hi, lo, n, off=0):
                for k in range(kt):
                    wh = w_hi[:, w, off + k * width:off + (k + 1) * width]
                    wl = w_lo[:, w, off + k * width:off + (k + 1) * width]
                    pe.matmul(out, wh, hi[:, k, n], start=(k == 0), stop=False)
                    pe.matmul(out, wh, lo[:, k, n], start=False, stop=False)
                    mm = pe.matmul(out, wl, hi[:, k, n], start=False, stop=(k == kt - 1))
                return mm

            def by_feature(m, width=P, kt=KD, hi=a_hi, lo=a_lo, cols=HALF, off=0):
                bank, w = begin(m)
                for h in range(2):
                    mm = linear(bank[0:width, h, 0:cols], w, width, kt, hi, lo,
                                slice(h * cols, (h + 1) * cols), off)
                mm.then_inc(made, 1)

            def by_token(m, tiles, width, kt=KD, hi=a_hi, lo=a_lo):
                bank, w = begin(m)
                flat = bank[:].rearrange("p a n -> p (a n)")
                for j, tile in enumerate(tiles):
                    n = slice(tile * P, tile * P + P)
                    out = flat[:, j * width:(j + 1) * width]
                    for k in range(kt):
                        wc = slice(k * width, (k + 1) * width)
                        pe.matmul(out, hi[:, k, n], w_hi[:, w, wc], start=(k == 0), stop=False)
                        pe.matmul(out, lo[:, k, n], w_hi[:, w, wc], start=False, stop=False)
                        mm = pe.matmul(out, hi[:, k, n], w_lo[:, w, wc], start=False, stop=(k == kt - 1))
                mm.then_inc(made, 1)

            norms = [0]

            def norm_sums(tiles=KD):
                i = norms[0]
                if i:
                    pe.wait_ge(var_ready, i)
                for k in range(tiles):
                    q = SQ[i] + k
                    pe.wait_ge(sq_ready, q + 1)
                    for h in range(2):
                        mm = pe.matmul(aux[0][:, h, 0:HALF], ones[:], tmp[:, q % 2, h * HALF:(h + 1) * HALF],
                                       start=(k == 0), stop=(k == tiles - 1), skip_group_check=True)
                    mm.then_inc(sq_used, 1)
                norms[0] += 1

            pe.wait_ge(silu_ready, 1)
            for k in range(24):
                pe.wait_ge(mod_in[k % 2], 16 * (k // 2 + 1))
                for j in range(4):
                    col = 2 * (4 * k + j)
                    for t in range(KD):
                        mm = pe.matmul(aux[1][:, 1, col:col + 2], w_mod[:, k % 2, t, j * P:(j + 1) * P],
                                       silu_c[:, t, :], start=(t == 0), stop=(t == KD - 1))
                mm.then_inc(mod_used, 1)

            def rope_turn(i, m, src, rows=P):
                has_taken(pe, m)
                if i >= 2:
                    pe.wait_ge(rope_applied, i - 1)
                pe.matmul(aux[1][0:rows, i % 2, :], perm[0:rows, 0:rows], src, start=True, stop=True)\
                  .then_inc(rope_done, 1)

            def scores_of(u):
                j, s, b = UNITS0[u]
                rows = slice(64 * s, 64 * s + 64)
                if u >= 2:
                    pe.wait_ge(s_read, u - 1)
                q = y[rows, 4 + j, b * P:(b + 1) * P]
                bank = aux[0][:, u % 2, :]
                if b == 0:
                    pe.matmul(bank[:, 0:P], q, kT[rows, P:2 * P], start=True, stop=True).then_inc(s_done, 1)
                else:
                    lo, n = local(b)
                    pe.matmul(bank[:, 0:P], q, kT[rows, 0:P], start=True, stop=True)
                    pe.matmul(bank[:, P:P + n * P], q, kT[rows, lo * P:(lo + n) * P], start=True, stop=True)\
                      .then_inc(s_done, 1)

            norm_sums()
            for m in range(IN[0], IN[0] + 6):
                if m == IN[0]:
                    pe.wait_ge(lo_ready, KD)
                if m == IN[0] + 5:
                    by_token(m, range(NT), P)
                else:
                    by_feature(m)
            for i in range(5):
                rope_turn(i, IN[0] + i, y[:, 4 + i, NP_TOK:T] if i < 4 else kT[:, 2 * P:6 * P])
            for m in range(IN[0] + 6, IN[0] + 18):
                by_feature(m)
            pe.wait_ge(rope_applied, 5)
            has_taken(pe, IN[0] + 5)
            pe.wait_ge(cache_in, 32)
            for u in range(NUNIT + 1):
                if u < NUNIT:
                    scores_of(u)
                if u >= 1:
                    j, s, b = UNITS0[u - 1]
                    tiles = [1] if b == 0 else [0] + [local(b)[0] + c for c in range(local(b)[1])]
                    pe.wait_ge(p_ready, u)
                    if u >= 2:
                        pe.wait_ge(pt_ready, u - 1)
                    for c in range(len(tiles)):
                        mm = pe.transpose(aux[1][:, 0, c * P:(c + 1) * P],
                                          s_sb[:, (u - 1) % 2, c * P:(c + 1) * P], ident[:])
                    mm.then_inc(pt_done, 1)
                    pe.wait_ge(pt_ready, u)
                    if u >= 2:
                        pe.wait_ge(pv_read, u - 1)
                    for c, tile in enumerate(tiles):
                        mm = pe.matmul(aux[1][64 * s:64 * s + 64, 1, 0:P], vt[:, tile, 64 * s:64 * s + 64],
                                       pt_sb[:, (u - 1) % 2, c * P:(c + 1) * P],
                                       start=(c == 0), stop=(c == len(tiles) - 1))
                    mm.then_inc(pv_done, 1)

            def out_and_route(l):
                pe.wait_ge(lo_ready, KD * (2 + 3 * l))
                for m in range(OUT[l], OUT[l] + KD):
                    by_feature(m)
                norm_sums()
                pe.wait_ge(lo_ready, KD * (3 + 3 * l))

                def keys(i):
                    has_taken(pe, WQ[l] + i)
                    n = 16 * l + i
                    if i == 0:
                        pe.wait_ge(subk_in, 16 * (l + 1))
                    if n >= 2:
                        pe.wait_ge(sc_read, n - 1)
                    for t in range(NT):
                        mm = pe.matmul(aux[n % 2][:, t // 4, (t % 4) * P:(t % 4 + 1) * P],
                                       tmp[:, i % 2, t * P:(t + 1) * P], subk[:, i, :], start=True, stop=True)
                    mm.then_inc(sc_done, 1)

                for i in range(16):
                    by_feature(WQ[l] + i)
                    if i >= 1:
                        keys(i - 1)
                keys(15)

            def experts(l):
                with pe.Fori(0, BODIES) as i:
                    for u in range(SPLIT):
                        m0, w = UM[l] + u, (UC[l] + u) % SPLIT
                        pe.wait_ge(lo_done, UC[l] + u + 1 + SPLIT * i)
                        pe.wait_ge(taken[m0 % 2], m0 // 2 + (SPLIT // 2) * i)
                        for h in range(2):
                            mm = linear(acc[m0 % 2][:, h, 0:HALF], w, P, KD, a_hi, a_lo,
                                        slice(h * HALF, (h + 1) * HALF))
                        mm.then_inc(made, 1)
                pe.wait_ge(picks_ready, l + 1)
                for n in range(15 * l, 15 * l + 15):
                    t, w = (n - 15 * l) // 3, n % 3
                    if n >= 4:
                        pe.wait_ge(turned_read, n - 3)
                    pe.transpose(aux[(n % 4) // 2][:, n % 2, 0:P], picks[:, w, t, :], ident[:])\
                      .then_inc(turned, 1)
                pe.wait_ge(turned_read, 15 * (l + 1))

                def gate_block(i):
                    for q in range(32):
                        n = 160 * l + q + 32 * i
                        wait(pe, gate_read, n - 3)
                        pe.wait_ge(hot_ready, n + 1)
                        for j in range(4):
                            tok = 4 * q + j
                            mm = pe.matmul(aux[(q % 4) // 2][:, q % 2, j * P:(j + 1) * P],
                                           one_a[:, tok % 8, :], one_b[:, tok % 8, :], start=True, stop=True)
                        mm.then_inc(hot_used, 1)

                gate_block(0)
                with pe.Fori(1, NT) as i:
                    gate_block(i)

                for m in (UM[l] + NKEY - 2, UM[l] + NKEY - 1):
                    has_taken(pe, m)

                def values(i):
                    for gg in range(2):
                        g = FIRST_G[l] + 2 * i + gg
                        pe.wait_ge(p_lo, 4 * g + 4)
                        pe.wait_ge(lo_done, VC[l] + 4 * (2 * i + gg) + 4)
                        for o in range(16):
                            dt, h = o // 2, o % 2
                            wait(pe, v_taken, 16 * g + o - 3)
                            out = acc[(o % 4) // 2][:, o % 2, 0:HALF]
                            n = slice(h * HALF, (h + 1) * HALF)
                            for c in range(GROUP):
                                w = (VC[l] + GROUP * gg + c) % SPLIT
                                ps = GROUP * gg + c
                                wh, wl = w_hi[:, w, dt * P:(dt + 1) * P], w_lo[:, w, dt * P:(dt + 1) * P]
                                pe.matmul(out, wh, a_hi[:, ps, n], start=(c == 0), stop=False)
                                pe.matmul(out, wh, a_lo[:, ps, n], start=False, stop=False)
                                mm = pe.matmul(out, wl, a_hi[:, ps, n], start=False, stop=(c == GROUP - 1))
                            mm.then_inc(v_done, 1)

                values(0)
                with pe.Fori(1, BODIES) as i:
                    values(i)

            out_and_route(0)
            experts(0)

            pe.wait_ge(v_taken, 16 * FIRST_G[1])
            norm_sums()
            pe.wait_ge(lo_ready, 4 * KD)
            for m in range(IN[1], IN[1] + 4):
                by_token(m, range(NT), P)
            for m in range(IN[1] + 4, IN[1] + 14):
                by_feature(m)
            pe.wait_ge(const1_in, 16 * N_CONST1)
            for t in range(NT):
                pe.wait_ge(vv_ready, t + 1)
                if t >= 2:
                    pe.wait_ge(mix_read, t - 1)
                for g in range(4):
                    out = aux[1][:, t % 2, g * P:(g + 1) * P]
                    pe.matmul(out, vv[:, t, g * P:(g + 1) * P], ws_t[:, g, :], start=True, stop=False)
                    mm = pe.matmul(out, ones[0:1, :], b_s[:, g, :], start=False, stop=True)
                mm.then_inc(mix_done, 1)
            pe.wait_ge(mix_read, NT)
            norm_sums(3)
            norm_sums(2)
            has_taken(pe, IN[1] + 13)
            pe.matmul(aux[1][0:32, 1, :], perm[0:32, 96:128], kr[:, NP_TOK:T],
                      start=True, stop=True).then_inc(rope_done, 1)
            pe.wait_ge(lat_lo, 5)
            for i in range(3):
                by_token(UKV + i, [2 * i, 2 * i + 1], 512, 2, ckv_hi, ckv_lo)
            pe.wait_ge(kr_ready, 1)
            pe.wait_ge(cache1_in, 16 * 4)

            flat0 = aux[0][:].rearrange("p a n -> p (a n)")
            flat1 = aux[1][:].rearrange("p a n -> p (a n)")
            for h in range(NH):
                by_feature(HEAD + 2 * h, 96, 3, cq_hi, cq_lo)
                by_feature(HEAD + 2 * h + 1, P, 2, ckv_hi, ckv_lo, 384, 288)
                if h >= 1:
                    pe.wait_ge(pt_ready, NUNIT + NT * h)
                has_taken(pe, HEAD + 2 * h)
                pe.matmul(aux[1][0:96, 0, :], perm[0:96, 0:96], q_head[:, h % 2, NP_TOK:T],
                          start=True, stop=True).then_inc(rope_done, 1)
                has_taken(pe, HEAD + 2 * h + 1)
                pe.wait_ge(rope_applied, 7 + h)
                for b in range(NT + 1):
                    if b < NT:
                        u = NUNIT + NT * h + b
                        if u > NUNIT:
                            pe.wait_ge(s_read, u)
                        q = q_head[:, h % 2, b * P:(b + 1) * P]
                        if b == 0:
                            pe.matmul(flat0[:, 0:P], q, k_head[:, h % 2, 0:P], start=True, stop=True)\
                              .then_inc(s_done, 1)
                        else:
                            pe.matmul(flat0[:, 0:512], q, k_head[:, h % 2, P:P + 512], start=True, stop=True)
                            pe.matmul(flat0[:, 512:640], q, k_head[:, h % 2, P + 512:768], start=True, stop=True)\
                              .then_inc(s_done, 1)
                    if b >= 1:
                        v = NUNIT + NT * h + b - 1
                        tiles = [0] if b == 1 else [1, 2, 3, 4, 5]
                        pe.wait_ge(p_ready, v + 1)
                        if v > NUNIT:
                            pe.wait_ge(pt_ready, v)
                            pe.wait_ge(pv_read, v)
                        for c in range(len(tiles)):
                            mm = pe.transpose(flat1[:, c * P:(c + 1) * P], p_sb[:, v % 2, c * P:(c + 1) * P], ident[:])
                        mm.then_inc(pt_done, 1)
                        pe.wait_ge(pt_ready, v + 1)
                        r = 64 * (h % 2)
                        for c, tile in enumerate(tiles):
                            mm = pe.matmul(flat1[r:r + 64, 768:896], vt1[:, tile, 64 * h:64 * h + 64],
                                           pt1[:, c * P:(c + 1) * P], start=(c == 0), stop=(c == len(tiles) - 1))
                        mm.then_inc(pv_done, 1)
            out_and_route(1)
            experts(1)
            pe.wait_ge(v_taken, 16 * 2 * FIRST_G[1])
            norm_sums()

        @block.scalar
        def _(act):
            for dst, name in ((x, "x"), (cvec, "cvec"), (ident, "ident"), (ones, "ones"), (iota, "iota"),
                              (mask, "mask"), (perm, "perm0"), (rope, "rope0"), (b_mod, "b_mod"),
                              (g_norm, "g_norm"), (sink, "sink"), (conv_w, "conv_w"), (g_small, "g_small")):
                act.dma_start(dst[:], a[name]).then_inc(const_in, 16)
            act.wait_ge(const_in, 16 * N_CONST)
            act.activation(silu_c[:], cvec[:], ACT.Silu).then_inc(silu_ready, 1)

            norm = [0]

            def squares(src, tiles=KD):
                for k in range(tiles):
                    q = SQ[norm[0]] + k
                    if q >= 2:
                        act.wait_ge(sq_used, q - 1)
                    act.activation(tmp[:, q % 2, :], src[:, k, :], ACT.Square).then_inc(sq_ready, 1)

            def root():
                act.wait_ge(var_ready, norm[0] + 1)
                act.activation(rstd[:], rstd[:], ACT.Sqrt).then_inc(rstd_ready, 1)
                norm[0] += 1

            def high(n):
                for k in range(KD):
                    act.wait_ge(h_ready, KD * n + k + 1)
                    act.activation(a_hi[:, k, :], tmp[:, k % 2, :], ACT.Copy).then_inc(hi_ready, 1)

            def take(m, out, in_, func=ACT.Copy):
                act.wait_ge(made, m + 1)
                act.activation(out, in_, func).then_inc(taken[m % 2], 1)

            def feature(m, width=P, cols=HALF):
                return acc[m % 2][0:width, :, 0:cols]

            squares(x)
            root()
            high(0)
            act.wait_ge(mod_used, 24)
            act.dma_start(kT[:, 0:P], a["cache_k"]).then_inc(cache_in, 16)
            act.dma_start(vt[:, 0, :], a["cache_v"]).then_inc(cache_in, 16)
            for i in range(4):
                take(IN[0] + i, halves(y[:, 4 + i, :]), feature(IN[0] + i))
            m = IN[0] + 4
            take(m, halves(kT[:, P:768]), feature(m))
            has_taken(act, m)
            act.dma_start(a["new_k"], kT[:, P:2 * P]).then_inc(state_out, 16)
            m = IN[0] + 5
            act.wait_ge(made, m + 1)
            act.activation(vt[:, 1:5, :].rearrange("p t n -> p (t n)"), acc[m % 2][:, 0, :], ACT.Copy)
            act.activation(vt[:, 5, :], acc[m % 2][:, 1, 0:P], ACT.Copy).then_inc(taken[m % 2], 1)
            has_taken(act, m)
            act.dma_start(a["new_v"], vt[:, 1, :]).then_inc(state_out, 16)
            for j in range(4):
                m = IN[0] + 6 + 3 * j
                take(m, halves(y[:, j, :]), feature(m))
                if j:
                    has_taken(act, m - 1)
                take(m + 1, halves(gate_c[:]), feature(m + 1))
            for u in range(NUNIT + 1):
                if u < NUNIT:
                    j, s, b = UNITS0[u]
                    n, st, hd = keys_of(b), stat[:, u % 2, :], 4 * s + j
                    act.wait_ge(neg_ready, u + 1)
                    act.activation(s_sb[:, u % 2, 0:n], s_sb[:, u % 2, 0:n], ACT.Exp, bias=st[:, 1:2],
                                   accum_out=st[:, 2:3])
                    act.activation(st[:, 3:4], sink[:, hd:hd + 1], ACT.Exp, bias=st[:, 1:2]).then_inc(e_ready, 1)
                if u >= 1:
                    v = u - 1
                    j, s, b = UNITS0[v]
                    n, rows = keys_of(b), slice(64 * s, 64 * s + 64)
                    act.wait_ge(pt_done, v + 1)
                    if v >= 2:
                        act.wait_ge(pv_done, v - 1)
                    act.activation(pt_sb[:, v % 2, 0:n], aux[1][:, 0, 0:n], ACT.Copy).then_inc(pt_ready, 1)
                    act.wait_ge(pv_done, v + 1)
                    act.activation(y[rows, 4 + j, b * P:(b + 1) * P], aux[1][rows, 1, 0:P], ACT.Copy)\
                       .then_inc(pv_read, 1)

            def out_and_route(l):
                act.wait_ge(pv_read, NUNIT * (l + 1))
                act.dma_start(subk[:], a["subk"][l]).then_inc(subk_in, 16)
                if l == 0:
                    act.wait_ge(conv_ready, 4)
                else:
                    act.wait_ge(mix_read, NT)
                act.wait_ge(made, OUT[l])
                for k in range(KD):
                    act.activation(a_hi[:, k, :], y[:, k, :], ACT.Copy).then_inc(hi_ready, 1)
                for m in (OUT[l] + 6, OUT[l] + 7):
                    has_taken(act, m)
                squares(x)
                root()
                high(2 * l + 1)
                act.wait_ge(lo_ready, KD * (3 + 3 * l))
                for i in range(16):
                    m, n = WQ[l] + i, 16 * l + i
                    if i >= 2:
                        act.wait_ge(sc_done, n - 1)
                    take(m, halves(tmp[:, i % 2, :]), feature(m))

            def experts(l):
                def activations(i):
                    for u in range(SPLIT):
                        m0 = UM[l] + u
                        act.wait_ge(made, m0 + 1 + SPLIT * i)
                        wait(act, a_st[u % 2], 16 * 64 * l + 16 * (u // 2) + 64 * i)
                        act.activation(halves(a_out[:, u % 2, :]), feature(m0), ACT.Gelu_apprx_tanh)\
                           .then_inc(taken[m0 % 2], 1)
                        act.wait_ge(taken[m0 % 2], m0 // 2 + 1 + 4 * i)
                        act.dma_start(a["act_s"][l, bass.ds(SPLIT * i + u, 1)].rearrange("o p n -> (o p) n"),
                                      a_out[:, u % 2, :]).then_inc(a_st[u % 2], 16)

                activations(0)
                with act.Fori(1, BODIES) as i:
                    activations(i)
                act.wait_ge(shifted, l + 1)
                gate_in = picks[:, 2, :, :]
                act.activation(gate_in, gate_in, ACT.Exp).then_inc(exp_done, 1)
                for n in range(15 * l, 15 * l + 15):
                    t, w = (n - 15 * l) // 3, n % 3
                    act.wait_ge(turned, n + 1)
                    act.activation(picks_t[:, w, t * P:(t + 1) * P], aux[(n % 4) // 2][:, n % 2, 0:P],
                                   ACT.Copy).then_inc(turned_read, 1)

                def gate_block(i):
                    for k in range(2):
                        wait(act, gates_out[k], 80 * l + 16 * i)
                        for q in range(16):
                            n = 160 * l + 16 * k + q + 32 * i
                            act.wait_ge(hot_used, n + 1)
                            act.activation(gates[k][:, :, 4 * q:4 * q + 4].rearrange("p e t -> p t e"),
                                           aux[(q % 4) // 2][:, q % 2, :].rearrange("p (t e) -> p t e", t=4),
                                           ACT.Copy).then_inc(gate_read, 1)
                        act.wait_ge(gate_read, 160 * l + 16 * k + 16 + 32 * i)
                        act.dma_start(a["gate_s"][l, :, :, bass.ds(128 * i + 64 * k, 64)]
                                      .rearrange("e p t -> p e t"), gates[k][:]).then_inc(gates_out[k], 16)

                gate_block(0)
                with act.Fori(1, NT) as i:
                    gate_block(i)
                act.wait_ge(gates_out[1], 80 * (l + 1))

                def high_p(i):
                    for k in range(SPLIT):
                        n = NKEY * l + k + SPLIT * i
                        act.wait_ge(p_made, n + 1)
                        if not (isinstance(i, int) and i == 0):
                            act.wait_ge(v_done, 16 * (FIRST_G[l] + k // GROUP - 1) + 32 * i)
                        act.activation(a_hi[:, k, :], p_raw[:, k % 2, :], ACT.Copy).then_inc(p_hi, 1)

                high_p(0)
                with act.Fori(1, BODIES) as i:
                    high_p(i)

            out_and_route(0)
            experts(0)

            act.wait_ge(v_taken, 16 * FIRST_G[1])
            for dst, name in ((perm, "perm1"), (rope, "rope1"), (ws_t, "ws_t"), (b_s, "b_s"), (g_sgu, "g_sgu")):
                act.dma_start(dst[:], a[name]).then_inc(const1_in, 16)
            squares(x)
            root()
            high(2)
            for c in range(4):
                m = IN[1] + c
                cols = slice(c * P, (c + 1) * P)
                act.wait_ge(made, m + 1)
                act.activation(vv[:, 0:4, cols], acc[m % 2][:, 0, :].rearrange("p (t n) -> p t n", t=4),
                               ACT.Gelu_apprx_tanh)
                act.activation(vv[:, 4, cols], acc[m % 2][:, 1, 0:P], ACT.Gelu_apprx_tanh)\
                   .then_inc(taken[m % 2], 1)
            for c in range(4):
                m = IN[1] + 4 + c
                take(m, halves(y[:, 4 + c, :]), feature(m), ACT.Gelu_apprx_tanh)
            for m in range(IN[1] + 2, IN[1] + 4):
                has_taken(act, m)
            act.wait_ge(lo_ready, KD * 4)
            for t in range(NT):
                if t:
                    act.wait_ge(ss_ready, t)
                act.activation(rstd[:, 0:512], vv[:, t, :], ACT.Square, accum_out=ss[:, t:t + 1])\
                   .then_inc(ss_ready, 1)
            for c in range(3):
                m = IN[1] + 8 + c
                take(m, halves(cq[:, c, :]), feature(m))
            for c in range(2):
                m = IN[1] + 11 + c
                take(m, halves(ckv[:, c, :]), feature(m))
            m = IN[1] + 13
            take(m, halves(kr[:]), acc[m % 2][0:32, :, 0:HALF])
            has_taken(act, m)
            act.dma_start(a["new_kr"], kr[:, 0:NP_TOK]).then_inc(state_out, 16)
            act.dma_start(kr_rope[:], a["rope_k"]).then_inc(cache1_in, 16)
            act.dma_start(ckv_old[:], a["cache_ckv"]).then_inc(cache1_in, 16)
            for i in range(2):
                act.dma_start(k_head[64:96, i, P:2 * P], a["cache_kr"]).then_inc(cache1_in, 16)
            act.wait_ge(ss_inv, 1)
            act.activation(ss[:, 0:NT], ss[:, 0:NT], ACT.Sqrt).then_inc(ss_root, 1)
            act.wait_ge(mix_read, NT)
            squares(cq, 3)
            root()
            for k in range(3):
                act.wait_ge(lat_norm, k + 1)
                act.activation(cq_hi[:, k, :], cq[:, k, :], ACT.Copy).then_inc(lat_hi, 1)
            act.wait_ge(lat_norm, 3)
            squares(ckv, 2)
            root()
            act.wait_ge(cache1_in, 16 * 4)
            for k in range(2):
                act.wait_ge(lat_norm, 4 + k)
                act.activation(ckv_hi[:, k, 0:P], ckv[:, k, 0:P], ACT.Copy)
                act.activation(ckv_hi[:, k, P:2 * P], ckv_old[:, k, :], ACT.Copy)
                act.activation(ckv_hi[:, k, 2 * P:768], ckv[:, k, P:T], ACT.Copy).then_inc(lat_hi, 1)
            act.dma_start(a["new_ckv"], ckv[:, :, 0:P]).then_inc(state_out, 16)
            for i in range(3):
                m = UKV + i
                take(m, vt1[:, 2 * i:2 * i + 2, :], acc[m % 2][:])
            act.wait_ge(rope_applied, 6)
            act.wait_ge(kr_ready, 1)
            flat0 = aux[0][:].rearrange("p a n -> p (a n)")
            flat1 = aux[1][:].rearrange("p a n -> p (a n)")
            for h in range(NH):
                m = HEAD + 2 * h
                take(m, halves(q_head[:, h % 2, :]), feature(m, 96))
                take(m + 1, halves(k_head[0:64, h % 2, :]), feature(m + 1, 64, 384))
                for b in range(NT + 1):
                    u = NUNIT + NT * h + b
                    if b < NT:
                        n, st = (P if b == 0 else T), stat[:, u % 2, :]
                        act.wait_ge(neg_ready, u + 1)
                        if u >= NUNIT + 2:
                            act.wait_ge(pt_done, u - 1)
                        act.activation(p_sb[:, u % 2, 0:n], flat0[:, 0:n], ACT.Exp, bias=st[:, 1:2],
                                       scale=SCALE_C, accum_out=st[:, 2:3]).then_inc(s_read, 1)
                    if b >= 1:
                        n = P if b == 1 else T
                        rows = slice(64 * (h % 2), 64 * (h % 2) + 64)
                        act.wait_ge(pt_done, u)
                        act.activation(pt1[:, 0:n], flat1[:, 0:n], ACT.Copy).then_inc(pt_ready, 1)
                        act.wait_ge(pv_done, u)
                        act.activation(y[rows, h // 2, (b - 1) * P:b * P], flat1[rows, 768:896], ACT.Copy)\
                           .then_inc(pv_read, 1)
            out_and_route(1)
            experts(1)
            act.wait_ge(v_taken, 16 * 2 * FIRST_G[1])
            squares(x)
            root()

        @block.vector
        def _(dve):
            steps = [0]

            def note(ins):
                ins.then_inc(dve_step, 1)
                steps[0] += 1

            def settle():
                dve.wait_ge(dve_step, steps[0])

            def step(ins):
                note(ins)
                settle()

            norm = [0]

            def variance(tiles=KD):
                dve.wait_ge(sq_used, SQ[norm[0]] + tiles)
                step(dve.tensor_scalar(halves(rstd[:]), aux[0][:, :, 0:HALF], 1.0 / (P * tiles), EPS,
                                       ALU.mult, ALU.add))
                dve.reciprocal(rstd[:], rstd[:]).then_inc(var_ready, 1)
                norm[0] += 1
                dve.wait_ge(rstd_ready, norm[0])

            def normed(n, s):
                l, row = n // 2, (0, 3)[n % 2]
                for k in range(KD + 1):
                    if k < KD:
                        h = tmp[:, k % 2, :]
                        if k >= 2:
                            dve.wait_ge(lo_ready, KD * s + k - 1)
                        step(dve.tensor_tensor(h, x[:, k, :], rstd[:], ALU.mult))
                        for c, cols in ((0, slice(0, P)), (1, slice(P, T))):
                            ins = dve.tensor_scalar(h[:, cols], h[:, cols], gain[:, n, k, c:c + 1],
                                                    mod[:, l, KD * row + k, c:c + 1], ALU.mult, ALU.add)
                            if c == 0:
                                note(ins)
                        ins.then_inc(h_ready, 1)
                    if k >= 1:
                        dve.wait_ge(hi_ready, KD * s + k)
                        dve.tensor_tensor(a_lo[:, k - 1, :], tmp[:, (k - 1) % 2, :],
                                          a_hi[:, k - 1, :].bitcast(F), ALU.subtract).then_inc(lo_ready, 1)

            def add_to_x(k, l, row, banks, free):
                parts = [(slice(0, P), banks[0][:, 0:P], 0), (slice(P, HALF), banks[0][:, P:HALF], 1),
                         (slice(HALF, T), banks[1][:, 0:HALF], 1)]
                for i, (cols, src, c) in enumerate(parts):
                    ins = dve.scalar_tensor_tensor(x[:, k, cols], src, mod[:, l, KD * row + k, c:c + 1],
                                                   x[:, k, cols], ALU.mult, ALU.add)
                    if i < 2:
                        note(ins)
                ins.then_inc(free, 1)

            def rotate(i, src, bank, cos_sin, mult_rows=P):
                t = rstd[0:mult_rows, 0:NL_TOK]
                dve.wait_ge(rope_done, i + 1)
                note(dve.tensor_tensor(t, bank, cos_sin[:, 1, :], ALU.mult))
                step(dve.tensor_tensor(src, src, cos_sin[:, 0, :], ALU.mult))
                dve.tensor_tensor(src, src, t, ALU.add).then_inc(rope_applied, 1)
                dve.wait_ge(rope_applied, i + 1)

            dve.wait_ge(const_in, 16 * N_CONST)
            dve.wait_ge(mod_used, 24)
            step(dve.tensor_tensor(mod[:].rearrange("p l j c -> p (l j) c"),
                                   aux[1][:, 1, 0:192].rearrange("p (j c) -> p j c", c=2),
                                   b_mod[:].rearrange("p l j -> p (l j)").unsqueeze(2).to_broadcast([P, 96, 2]),
                                   ALU.add))
            for n in range(4):
                row = (1, 4)[n % 2]
                note(dve.scalar_tensor_tensor(gain[:, n], mod[:, n // 2, KD * row:KD * row + KD, :], 1.0,
                                              g_norm[:, n, :].unsqueeze(2).to_broadcast([P, KD, 2]),
                                              ALU.add, ALU.mult))
            settle()

            variance()
            normed(0, 0)
            step(dve.memset(u_pad[:], 0.0))
            dve.wait_ge(lo_ready, KD)
            for i in range(5):
                rotate(i, y[:, 4 + i, NP_TOK:T] if i < 4 else kT[:, 2 * P:6 * P], aux[1][:, i % 2, :], rope)
            for j in range(4):
                m = IN[0] + 8 + 3 * j
                dve.wait_ge(made, m + 1)
                has_taken(dve, m - 1)
                bank = acc[m % 2]
                note(dve.tensor_tensor(u_pad[:, 1:129], bank[:, 0, 0:P], gate_c[:, 0:P], ALU.mult))
                note(dve.tensor_tensor(u_pad[:, 131:323], bank[:, 0, P:HALF], gate_c[:, P:HALF], ALU.mult))
                dve.tensor_tensor(u_pad[:, 323:643], bank[:, 1, 0:HALF], gate_c[:, HALF:T], ALU.mult)\
                   .then_inc(taken[m % 2], 1)
                has_taken(dve, m)
                step(dve.tensor_scalar(conv[:], u_pad[:, 0:642], conv_w[:, j, 0:1], None, ALU.mult))
                for w in (1, 2):
                    step(dve.scalar_tensor_tensor(conv[:], u_pad[:, w:w + 642], conv_w[:, j, w:w + 1], conv[:],
                                                  ALU.mult, ALU.add))
                has_taken(dve, m - 2)
                note(dve.tensor_tensor(y[:, j, 0:P], y[:, j, 0:P], conv[:, 0:P], ALU.mult))
                dve.tensor_tensor(y[:, j, P:T], y[:, j, P:T], conv[:, 130:642], ALU.mult).then_inc(conv_ready, 1)
                dve.wait_ge(conv_ready, j + 1)
            for u in range(NUNIT + 1):
                if u < NUNIT:
                    j, s, b = UNITS0[u]
                    n, st, hd = keys_of(b), stat[:, u % 2, :], 4 * s + j
                    dve.wait_ge(s_done, u + 1)
                    if u >= 2:
                        dve.wait_ge(pt_done, u - 1)
                    ins = dve.tensor_scalar(s_sb[:, u % 2, 0:P], aux[0][:, u % 2, 0:P], SCALE_B, None, ALU.mult)
                    if b > 0:
                        note(ins)
                        skip = P * (local(b)[0] - b)
                        ins = dve.scalar_tensor_tensor(s_sb[:, u % 2, P:n], aux[0][:, u % 2, P:n], SCALE_B,
                                                       mask[:, skip:skip + n - P], ALU.mult, ALU.add)
                    ins.then_inc(s_read, 1)
                    dve.wait_ge(s_read, u + 1)
                    step(dve.reduce_max(st[:, 0:1], s_sb[:, u % 2, 0:n], AX.X))
                    dve.tensor_scalar(st[:, 1:2], st[:, 0:1], sink[:, hd:hd + 1], -1.0, ALU.max, ALU.mult)\
                       .then_inc(neg_ready, 1)
                if u >= 1:
                    v = u - 1
                    n, st = keys_of(UNITS0[v][2]), stat[:, v % 2, :]
                    dve.wait_ge(e_ready, v + 1)
                    step(dve.tensor_tensor(st[:, 4:5], st[:, 2:3], st[:, 3:4], ALU.add))
                    step(dve.reciprocal(st[:, 5:6], st[:, 4:5]))
                    dve.tensor_scalar(s_sb[:, v % 2, 0:n], s_sb[:, v % 2, 0:n], st[:, 5:6], None, ALU.mult)\
                       .then_inc(p_ready, 1)

            def out_and_route(l):
                s = 1 + 3 * l
                for k in range(KD):
                    dve.wait_ge(hi_ready, KD * s + k + 1)
                    dve.tensor_tensor(a_lo[:, k, :], y[:, k, :], a_hi[:, k, :].bitcast(F), ALU.subtract)\
                       .then_inc(lo_ready, 1)
                for k in range(KD):
                    m = OUT[l] + k
                    dve.wait_ge(made, m + 1)
                    add_to_x(k, l, 2, (acc[m % 2][:, 0, :], acc[m % 2][:, 1, :]), taken[m % 2])
                variance()
                normed(2 * l + 1, s + 1)
                for i in range(16):
                    n = 16 * l + i
                    dve.wait_ge(sc_done, n + 1)
                    note(dve.tensor_copy(scores[:, 0:4, i, :],
                                         aux[n % 2][:, 0, :].rearrange("p (t k) -> p t k", t=4)))
                    dve.tensor_copy(scores[:, 4, i, :], aux[n % 2][:, 1, 0:P]).then_inc(sc_read, 1)
                dve.wait_ge(sc_read, 16 * (l + 1))

            def top16(heads, values, indices, data):
                for half in range(2):
                    r = slice(8 * half, 8 * half + 8)
                    for h in range(heads):
                        note(dve.max(values[:, h, r], data(h)))
                    settle()
                    for h in range(heads):
                        note(dve.max_index(indices[:, h, r], values[:, h, r], data(h)))
                    settle()
                    if half == 0:
                        for h in range(heads):
                            note(dve.match_replace(data(h), values[:, h, r], data(h), NEG))
                        settle()

            def route(l):
                four = [P, NH, 16, 16]
                for t in range(NT):
                    top16(16, top_v, top_i, lambda h: scores[:, t, h, :])
                    step(dve.tensor_copy(top_f[:], top_i[:]))
                    side = [v[:].rearrange("p (h s) k -> p h s k", s=2) for v in (top_v, top_f)]
                    step(dve.tensor_tensor(cand[:], side[0][:, :, 0, :].unsqueeze(3).to_broadcast(four),
                                           side[0][:, :, 1, :].unsqueeze(2).to_broadcast(four), ALU.add))
                    top16(NH, best, place, lambda h: cand[:, h].rearrange("p i j -> p (i j)"))
                    for s, (amount, op) in enumerate(((4, ALU.logical_shift_right), (15, ALU.bitwise_and))):
                        step(dve.tensor_scalar(part_i[:], place[:], amount, None, op))
                        step(dve.tensor_copy(part_f[:], part_i[:]))
                        step(dve.tensor_tensor(cand[:], part_f[:].unsqueeze(3).to_broadcast(four),
                                               iota[:, 0:16].unsqueeze(1).unsqueeze(1).to_broadcast(four),
                                               ALU.is_equal))
                        step(dve.tensor_tensor(cand[:], cand[:],
                                               side[1][:, :, s, :].unsqueeze(2).to_broadcast(four), ALU.mult))
                        step(dve.tensor_reduce(picks[:, s, t, :].rearrange("p (h k) -> p h k", h=NH), cand[:],
                                               AX.X, ALU.add))
                    gate = picks[:, 2, t, :].rearrange("p (h k) -> p h k", h=NH)
                    ins = dve.tensor_tensor(gate, best[:], best[:, :, 0:1].to_broadcast([P, NH, 16]),
                                            ALU.subtract)
                    if t < NT - 1:
                        step(ins)
                ins.then_inc(shifted, 1)
                dve.wait_ge(exp_done, l + 1)
                every = picks[:, 2, :, :].rearrange("p t (h k) -> p (t h) k", h=NH)
                sums = cand[:].rearrange("p h i j -> p (h i j)")[:, 0:NT * NH]
                step(dve.tensor_reduce(sums, every, AX.X, ALU.add))
                step(dve.reciprocal(sums, sums))
                dve.tensor_tensor(every, every, sums.unsqueeze(2).to_broadcast([P, NT * NH, 16]), ALU.mult)\
                   .then_inc(picks_ready, 1)
                dve.wait_ge(turned_read, 15 * (l + 1))

            def experts(l):
                def one_hots(i):
                    for q in range(32):
                        n = 160 * l + q + 32 * i
                        wait(dve, hot_used, n - 1)
                        for j in range(4):
                            tok = 4 * q + j
                            cell = [picks_t[:, w, bass.ds(P * i + tok, 1)] for w in range(3)]
                            dve.tensor_scalar(one_a[:, tok % 8, :], iota[:], cell[0], cell[2],
                                              ALU.is_equal, ALU.mult)
                            ins = dve.tensor_scalar(one_b[:, tok % 8, :], iota[:], cell[1], None, ALU.is_equal)
                        ins.then_inc(hot_ready, 1)

                one_hots(0)
                with dve.Fori(1, NT) as i:
                    one_hots(i)

                def form(i, k, first=False):
                    n = NKEY * l + k + SPLIT * i
                    dve.wait_ge(ag_in[k % 4], 32 * (32 * l + k // 4 + 1) + 64 * i)
                    wait(dve, p_lo, n - 1)
                    dve.tensor_tensor(p_raw[:, k % 2, :], ag[:, k % 4, 0, :], ag[:, k % 4, 1, :], ALU.mult)\
                       .then_inc(p_made, 1)

                def low_p(i, k):
                    n = NKEY * l + k + SPLIT * i
                    dve.wait_ge(p_hi, n + 1)
                    dve.tensor_tensor(a_lo[:, k, :], p_raw[:, k % 2, :], a_hi[:, k, :].bitcast(F), ALU.subtract)\
                       .then_inc(p_lo, 1)

                def sums(i, last=False):
                    for gg in range(2):
                        g = FIRST_G[l] + gg + 2 * i
                        for o in range(16):
                            if not (last and gg == 1):
                                j, later = o // 4, (i if gg == 0 else i + 1)
                                k = j + (GROUP if gg == 0 else 0)
                                if o % 4 == 0:
                                    form(later, k)
                                if o % 4 == 2:
                                    low_p(later, k)
                            dt, h = o // 2, o % 2
                            bank = acc[(o % 4) // 2][:, o % 2, :]
                            dve.wait_ge(v_done, o + 1 + 16 * g)
                            wait(dve, v_taken, 16 * g - 16 + o + 1)
                            if h == 0:
                                dve.scalar_tensor_tensor(x[:, dt, 0:P], bank[:, 0:P], mod[:, l, 40 + dt, 0:1],
                                                         x[:, dt, 0:P], ALU.mult, ALU.add)
                                cols, src = slice(P, HALF), bank[:, P:HALF]
                            else:
                                cols, src = slice(HALF, T), bank[:, 0:HALF]
                            dve.scalar_tensor_tensor(x[:, dt, cols], src, mod[:, l, 40 + dt, 1:2], x[:, dt, cols],
                                                     ALU.mult, ALU.add).then_inc(v_taken, 1)

                for k in range(GROUP):
                    form(0, k)
                    low_p(0, k)
                sums(0)
                with dve.Fori(1, BODIES - 1) as i:
                    sums(i)
                sums(BODIES - 1, last=True)
                dve.wait_ge(v_taken, 16 * (FIRST_G[l] + 32))

            out_and_route(0)
            route(0)
            experts(0)

            variance()
            normed(2, 3)
            dve.wait_ge(ss_ready, NT)
            step(dve.tensor_scalar(ss[:, 0:NT], ss[:, 0:NT], 1.0 / 512, EPS, ALU.mult, ALU.add))
            dve.reciprocal(ss[:, 0:NT], ss[:, 0:NT]).then_inc(ss_inv, 1)
            dve.wait_ge(ss_root, 1)
            dve.wait_ge(const1_in, 16 * N_CONST1)
            for t in range(NT):
                dve.scalar_tensor_tensor(vv[:, t, :], vv[:, t, :], ss[:, t:t + 1], g_sgu[:], ALU.mult, ALU.mult)\
                   .then_inc(vv_ready, 1)
            for c in range(2):
                has_taken(dve, IN[1] + 6 + c)
            for t in range(NT):
                dve.wait_ge(mix_done, t + 1)
                part = y[:, 4:8, t * P:(t + 1) * P]
                dve.tensor_tensor(part, part, aux[1][:, t % 2, :].rearrange("p (g t) -> p g t", g=4), ALU.mult)\
                   .then_inc(mix_read, 1)
            for first, tiles, t, hi, lo in ((0, 3, cq, cq_hi, cq_lo), (3, 2, ckv, ckv_hi, ckv_lo)):
                variance(tiles)
                for k in range(tiles):
                    dve.scalar_tensor_tensor(t[:, k, :], t[:, k, :], g_small[:, first + k:first + k + 1], rstd[:],
                                             ALU.mult, ALU.mult).then_inc(lat_norm, 1)
                for k in range(tiles):
                    dve.wait_ge(lat_hi, first + k + 1)
                    parts = [(t[:, k, :], slice(0, T))] if first == 0 else \
                        [(t[:, k, 0:P], slice(0, P)), (ckv_old[:, k, :], slice(P, 2 * P)),
                         (t[:, k, P:T], slice(2 * P, 768))]
                    for n, (src, cols) in enumerate(parts):
                        ins = dve.tensor_tensor(lo[:, k, cols], src, hi[:, k, cols].bitcast(F), ALU.subtract)
                        if n < len(parts) - 1:
                            note(ins)
                    ins.then_inc(lat_lo, 1)
            dve.wait_ge(cache1_in, 16 * 4)
            rotate(5, kr[:, NP_TOK:T], aux[1][0:32, 1, :], kr_rope, 32)
            for i in range(2):
                note(dve.tensor_copy(k_head[64:96, i, 0:P], kr[:, 0:P]))
                ins = dve.tensor_copy(k_head[64:96, i, 2 * P:768], kr[:, P:T])
                if i == 0:
                    note(ins)
            ins.then_inc(kr_ready, 1)
            flat0 = aux[0][:].rearrange("p a n -> p (a n)")
            for h in range(NH):
                rotate(6 + h, q_head[:, h % 2, NP_TOK:T], aux[1][0:96, 0, :], rope[0:96], 96)
                for b in range(NT + 1):
                    u = NUNIT + NT * h + b
                    if b < NT:
                        n, st = (P if b == 0 else T), stat[:, u % 2, :]
                        dve.wait_ge(s_done, u + 1)
                        step(dve.reduce_max(st[:, 0:1], flat0[:, 0:n], AX.X))
                        dve.tensor_scalar(st[:, 1:2], st[:, 0:1], -SCALE_C, None, ALU.mult).then_inc(neg_ready, 1)
                    if b >= 1:
                        v = u - 1
                        n, st = (P if b == 1 else T), stat[:, v % 2, :]
                        dve.wait_ge(s_read, v + 1)
                        step(dve.reciprocal(st[:, 5:6], st[:, 2:3]))
                        dve.tensor_scalar(p_sb[:, v % 2, 0:n], p_sb[:, v % 2, 0:n], st[:, 5:6], None, ALU.mult)\
                           .then_inc(p_ready, 1)
            out_and_route(1)
            route(1)
            experts(1)
            variance()
            for k in range(KD):
                dve.scalar_tensor_tensor(y[:, k, :], x[:, k, :], g_norm[:, 4, k:k + 1], rstd[:],
                                         ALU.mult, ALU.mult).then_inc(y_ready, 1)


def constants():
    import numpy as np
    f = np.float32
    out = {"ident": np.eye(P, dtype=f), "ones": np.ones((P, P), f),
           "iota": np.tile(np.arange(NKEY, dtype=f), (P, 1))}
    q, k = np.arange(P)[:, None], np.arange(3 * P)[None, :]
    out["mask"] = np.where(np.abs(k - P - q) <= P, 0.0, NEG).astype(f)

    def tables(dr):
        n = dr // 4
        freqs = np.power(f(10000.0), -np.arange(n, dtype=f) / f(n)).astype(f)
        t = np.arange(NL_TOK)
        row, col = (t // 64).astype(f), (t % 64).astype(f)
        ang = np.concatenate([row[:, None] * freqs, col[:, None] * freqs], axis=1).astype(f)
        cos, sin = np.cos(ang).astype(f).T, np.sin(ang).astype(f).T
        return np.concatenate([cos, cos]), np.concatenate([-sin, sin])

    def swap(dr):
        return np.roll(np.eye(dr, dtype=f), dr // 2, axis=0)

    cos, sin = tables(64)
    out["rope0"] = np.stack([np.tile(cos, (2, 1)), np.tile(sin, (2, 1))], axis=1)
    out["perm0"] = np.kron(np.eye(2, dtype=f), swap(64))
    cos, sin = tables(32)
    rope1, perm1 = np.zeros((P, 2, NL_TOK), f), np.zeros((P, P), f)
    rope1[0:64, 0] = 1.0
    rope1[64:96, 0], rope1[64:96, 1] = cos, sin
    perm1[64:96, 64:96] = swap(32)
    perm1[0:32, 96:128] = swap(32)
    out["rope1"], out["perm1"] = rope1, perm1
    out["rope_k"] = np.stack([cos, sin], axis=1)
    return {n: np.ascontiguousarray(v, dtype=f) for n, v in out.items()}


def layout(i):
    import numpy as np

    def chunks(w, n=None):
        k, m = w.shape[0] // P, w.shape[1] // P
        return w.reshape(k, P, m, P).transpose(2, 1, 0, 3).reshape(m, P, k * P)

    def columns(v):
        return v.reshape(-1, P).T

    def features(t):
        return t.T.reshape(t.shape[1] // P, P, t.shape[0]).transpose(1, 0, 2)

    o = {}
    o["x"] = features(np.concatenate([i["x_prompt"][0], i["x_sample"][0]]))
    o["cvec"] = np.stack([columns(i["c_ctx"]), columns(i["c"][0])], axis=2)
    o["w_mod"] = i["w_mod"].reshape(2, KD, P, 12, 512).transpose(0, 3, 2, 1, 4)
    o["b_mod"] = i["b_mod"].reshape(2, 48, P).transpose(2, 0, 1)
    norms = [i["g_norm1"][0], i["g_norm2"][0], i["g_norm1"][1], i["g_norm2"][1], i["g_final"]]
    o["g_norm"] = np.stack([columns(g) for g in norms], axis=1)
    o["sink"] = np.broadcast_to(i["ev_sink"][0], (P, NH))
    o["conv_w"] = i["ev_conv_w"][0].reshape(3, 4, P).transpose(2, 1, 0)
    o["g_small"] = np.concatenate([columns(i["od_g_qnorm"][0]), columns(i["od_g_kvnorm"][0])], axis=1)
    w = i["ev_w_in"][0]
    heads = [np.concatenate([w[:, 1536 + 64 * h:1600 + 64 * h] for h in (j, 4 + j)], axis=1) for j in range(4)]
    conv = [w[:, 512 * s + P * j:512 * s + P * j + P] for j in range(4) for s in range(3)]
    o["in0"] = chunks(np.concatenate(heads + [w[:, 2048:2304]] + conv, axis=1))
    w = i["ev_w_out"][0]
    rows = [w[512 + 64 * h:576 + 64 * h] for j in range(4) for h in (j, 4 + j)]
    o["out0"] = chunks(np.concatenate([w[0:512]] + rows))
    o["cache_k"] = i["cache_attn_k"][0, 0].reshape(P, P).T
    o["cache_v"] = i["cache_attn_v"][0, 0].reshape(P, P)
    w = i["od_w_in"][0]
    o["in1"] = chunks(np.concatenate([w[:, 1184:1696], w[:, 672:1184], w[:, 0:640], w[:, 640:768]], axis=1))
    uq, ukv = i["od_w_uq"][0], i["od_w_ukv"][0]
    q = uq.reshape(3, P, NH, 96).transpose(2, 1, 0, 3).reshape(NH, P, 288)
    kv = ukv.reshape(2, P, NH, P).transpose(2, 1, 0, 3).reshape(NH, P, 256)
    o["head"] = np.concatenate([q, kv], axis=2)
    o["ukv_v"] = ukv.reshape(2, P, NH, 2, 64)[:, :, :, 1].transpose(1, 0, 2, 3).reshape(P, 1024)
    o["out1"] = chunks(i["od_w_out"][0])
    o["cache_ckv"] = features(i["cache_mla_ckv"][0, 0])
    o["cache_kr"] = i["cache_mla_krope"][0, 0].T
    o["ws_t"] = i["od_w_spatial"][0].transpose(2, 0, 1)
    o["b_s"] = i["od_b_spatial"]
    o["g_sgu"] = np.broadcast_to(i["od_g_sgu"][0], (P, 512))
    o["wq"] = np.stack([chunks(i["peer_wq"][l]) for l in range(2)])
    o["subk"] = i["peer_subkeys"].reshape(2, 16, NKEY, P).transpose(0, 3, 1, 2)
    u = i["peer_u"].reshape(2, NKEY, NKEY, KD, P)
    o["u"] = u.transpose(0, 2, 4, 3, 1).reshape(2, NKEY, P, 1024)
    o["v"] = i["peer_v"].reshape(2, NKEY, NKEY, D).transpose(0, 2, 1, 3)
    return o


_OUTS = {"y": (P, KD, T), "new_k": (P, P), "new_v": (P, P), "new_ckv": (P, 2, P), "new_kr": (32, P)}


def kernel(**inputs):
    import numpy as _np
    import concourse.bacc as _bacc
    from concourse import mybir as _mybir
    from concourse.bass_utils import run_bass_kernel_spmd as _run

    f32 = _mybir.dt.float32
    nc = _bacc.Bacc("TRN2", target_bir_lowering=False, num_devices=1)
    arrays, args = {}, {}
    data = layout({n: _np.asarray(v) for n, v in inputs.items()})
    data.update(constants())
    for name, v in data.items():
        v = _np.ascontiguousarray(v)
        arrays[f"in_{name}"] = v
        args[name] = nc.dram_tensor(f"in_{name}", v.shape, _mybir.dt.from_np(v.dtype), kind="ExternalInput").ap()
    for name, shape in _OUTS.items():
        args[name] = nc.dram_tensor(f"out_{name}", shape, f32, kind="ExternalOutput").ap()
    for name in ("act_s", "gate_s"):
        args[name] = nc.dram_tensor(name, (2, NKEY, P, T), f32, kind="Internal").ap()
    build(nc, args)
    r = _run(nc, [arrays], core_ids=[0]).results[0]
    y = r["out_y"].transpose(2, 1, 0).reshape(T, D)
    new_ckv = r["out_new_ckv"].transpose(2, 1, 0).reshape(1, 1, NP_TOK, 256)
    return (_np.ascontiguousarray(y[None, 0:NP_TOK]), _np.ascontiguousarray(y[None, NP_TOK:T]),
            _np.ascontiguousarray(r["out_new_k"].T).reshape(1, 1, NP_TOK, 2, 64),
            _np.ascontiguousarray(r["out_new_v"]).reshape(1, 1, NP_TOK, 2, 64),
            _np.ascontiguousarray(new_ckv), _np.ascontiguousarray(r["out_new_kr"].T).reshape(1, 1, NP_TOK, 32))
```

```python
import concourse.bass as bass
from concourse import mybir
from contextlib import ExitStack

P = 128
D, KD = 1024, 8
NP_TOK, NL_TOK = 128, 512
T, NT = 640, 5
HALF = 320
NKEY, PICKS = 128, 128
NH = 8
EPS = 1e-6
SCALE_B, SCALE_C = 64.0 ** -0.5, 96.0 ** -0.5
RAW, SPLIT = 2, 8
GROUP = 4
NEG = -1.0e30


def plan():
    chunks, products = [], []

    def add(layer, kind, n, made=1, size=1024, together=False):
        first = len(products)
        for i in range(n):
            if not together:
                first = len(products)
            if not together or i == n - 1:
                products.extend([(layer, kind, i, j, len(chunks)) for j in range(made)])
            chunks.append((layer, kind, i, size, first, first + made))

    add(0, "in", 18)
    add(0, "out", 8)
    add(0, "wq", 16)
    add(0, "u", 128)
    add(0, "v", 128, made=0)
    add(1, "dzv", 4, made=3, together=True)
    add(1, "in", 10)
    add(1, "ukv_v", 1, made=3)
    add(1, "head", 8, made=2, size=3 * 96 + 2 * 128)
    add(1, "out", 8)
    add(1, "wq", 16)
    add(1, "u", 128)
    add(1, "v", 128, made=0)
    return chunks, products


CHUNKS, PRODUCTS = plan()


def chunk_at(layer, kind):
    return next(n for n, c in enumerate(CHUNKS) if c[0] == layer and c[1] == kind)


def product_at(layer, kind):
    return next(n for n, c in enumerate(PRODUCTS) if c[0] == layer and c[1] == kind)


def build(nc, a):
    F, R, U32 = mybir.dt.float32, mybir.dt.float32r, mybir.dt.uint32
    ALU, ACT, AX = mybir.AluOpType, mybir.ActivationFunctionType, mybir.AxisListType
    ctx = ExitStack()
    with ctx:
        slab_bytes = 212 * 1024 - 4480
        slab = ctx.enter_context(nc.sbuf_tensor("slab", [P, slab_bytes // 4], F))
        base = nc.sbuf_base - slab_bytes
        end = [base]

        def at(name, shape, off, dt=F):
            return nc.alloc_sbuf_tensor_at(name, shape, dt, offset=off)

        def sb(name, shape, dt=F):
            size = 4
            for n in shape[1:]:
                size *= n
            off = end[0]
            end[0] += (size + 31) // 32 * 32
            return at(name, shape, off, dt)

        def sem(name):
            return ctx.enter_context(nc.semaphore(name))

        x = sb("x", [P, KD, T])
        act_at = end[0]
        a_hi = sb("a_hi", [P, KD, T], R)
        a_lo = sb("a_lo", [P, KD, T], R)
        raw = sb("raw", [P, RAW, 1024])
        w_hi = sb("w_hi", [P, SPLIT, 1024], R)
        w_lo = sb("w_lo", [P, SPLIT, 1024], R)
        ident = sb("ident", [P, P])
        ones = sb("ones", [P, P])
        iota = sb("iota", [P, P])
        mask = sb("mask", [P, 384])
        perm = sb("perm", [P, P])
        rope = sb("rope", [P, 2, NL_TOK])
        mod = sb("mod", [P, 2, 48, 2])
        b_mod = sb("b_mod", [P, 2, 48])
        g_norm = sb("g_norm", [P, 5, KD])
        gain = sb("gain", [P, 4, KD, 2])
        mod_v = sb("mod_v", [P, 3, 2])
        sink = sb("sink", [P, NH])
        conv_w = sb("conv_w", [P, 4, 3])
        g_small = sb("g_small", [P, 5])
        stat = sb("stat", [P, 4, 8])
        ss = sb("ss", [P, 8])
        tmp_at = end[0]
        tmp = sb("tmp", [P, 2, T])
        rstd = sb("rstd", [P, T])
        picks = at("picks", [P, 3, NT, PICKS], tmp_at)
        a_out_at = end[0]
        a_out = sb("a_out", [P, 2, T])
        work = end[0]
        room = base + slab_bytes - work
        assert room >= 54304, room

        y = at("y", [P, KD, T], work)
        kT = at("kT", [P, 768], work + 20480)
        vt = at("vt", [P, 6, P], work + 23552)
        u_pad = at("u_pad", [P, 648], work + 26624)
        gate_c = at("gate_c", [P, T], work + 29216)
        conv = at("conv", [P, 642], work + 31776)
        s_sb = at("s_sb", [P, 4, 512], work + 36416)
        pt_sb = at("pt_sb", [P, 2, 512], work + 44608)
        vv = at("vv", [P, NT, 512], work + 20480)
        vt1 = at("vt1", [P, 6, 512], work + 20480)
        cq = at("cq", [P, 3, T], work + 32768)
        ckv = at("ckv", [P, 2, T], work + 40448)
        ckv_old = at("ckv_old", [P, 2, P], work + 45568)
        kr = at("kr", [32, T], work + 46592)
        kr_rope = at("kr_rope", [32, 2, NL_TOK], work + 49152)
        p_sb = at("p_sb", [P, 2, T], work + 46592)
        pt1 = at("pt1", [P, T], work + 51712)
        ws_t = at("ws_t", [P, 4, P], work)
        b_s = at("b_s", [1, 4, P], work + 2048)
        g_sgu = at("g_sgu", [P, 512], work + 4096)
        cq_hi = at("cq_hi", [P, 3, T], act_at, R)
        cq_lo = at("cq_lo", [P, 3, T], act_at + 7680, R)
        ckv_hi = at("ckv_hi", [P, 2, 768], act_at + 15360, R)
        ckv_lo = at("ckv_lo", [P, 2, 768], act_at + 21504, R)
        k_head = at("k_head", [96, 2, 768], act_at + 27648)
        q_head = at("q_head", [96, 2, T], act_at + 33792)
        c_all = at("c_all", [P, 2, D], work + 36416)
        w_mod = at("w_mod", [P, 8, D], work)
        w_mod_b = at("w_mod_b", [P, 2, D], work + 44608)
        c_all_v = at("c_all_v", [P, 2, D], work + 37888)
        w_mod_v = at("w_mod_v", [P, 3, D], work + 25600)
        unread = at("unread", [P, D], a_out_at)
        scores = at("scores", [P, NT, 16, NKEY], work)
        subk = at("subk", [P, 16, NKEY], work + 40960)
        cand = at("cand", [P, NH, 16, 16], work + 40960)
        top_v = at("top_v", [P, 16, 16], work + 49152)
        top_i = at("top_i", [P, 16, 16], work + 50176, U32)
        top_f = at("top_f", [P, 16, 16], work + 51200)
        best = at("best", [P, NH, 16], work + 52224)
        place = at("place", [P, NH, 16], work + 52736, U32)
        part_i = at("part_i", [P, NH, 16], work + 53248, U32)
        part_f = at("part_f", [P, NH, 16], work + 53760)
        g_sum = at("g_sum", [P, NH], work + 54272)
        gates = at("gates", [P, NKEY, 64], work)
        one_a = at("one_a", [P, 8, NKEY], work + 32768)
        one_b = at("one_b", [P, 8, NKEY], work + 36864)
        picks_t = at("picks_t", [P, 3, T], work + 40960)
        ag = at("ag", [P, 4, 2, T], work)
        p_raw = at("p_raw", [P, 2, T], work + 20480)

        acc = [ctx.enter_context(nc.psum_tensor(f"acc{i}", [P, 2, 512], F)) for i in range(2)]
        aux = [ctx.enter_context(nc.psum_tensor(f"aux{i}", [P, 2, 512], F)) for i in range(2)]

        const_in = sem("const_in")
        const1_in, cache_in, cache1_in = sem("const1_in"), sem("cache_in"), sem("cache1_in")
        raw_in = [sem(f"raw_in{i}") for i in range(RAW)]
        hi_done, lo_done, slot_free = sem("hi_done"), sem("lo_done"), sem("slot_free")
        made = sem("made")
        taken = [sem(f"taken{i}") for i in range(2)]
        mod_in = [sem(f"mod_in{i}") for i in range(8)]
        mod_b_in = [sem(f"mod_b_in{i}") for i in range(2)]
        mod_used, silu_ready = sem("mod_used"), sem("silu_ready")
        mod_v_in = [sem(f"mod_v_in{i}") for i in range(3)]
        mod_v_used, mod_v_sum, c_in = sem("mod_v_used"), sem("mod_v_sum"), sem("c_in")
        dve_step, act_step = sem("dve_step"), sem("act_step")
        sq_ready, sq_used = sem("sq_ready"), sem("sq_used")
        var_ready, rstd_ready = sem("var_ready"), sem("rstd_ready")
        h_ready, hi_ready, lo_ready = sem("h_ready"), sem("hi_ready"), sem("lo_ready")
        rope_done, rope_applied = sem("rope_done"), sem("rope_applied")
        s_done, s_read = sem("s_done"), sem("s_read")
        neg_ready, e_ready, p_ready = sem("neg_ready"), sem("e_ready"), sem("p_ready")
        pt_done, pt_ready, pv_done, pv_read = sem("pt_done"), sem("pt_ready"), sem("pv_done"), sem("pv_read")
        state_out = sem("state_out")
        mix_done, mix_read, vv_ready = sem("mix_done"), sem("mix_read"), sem("vv_ready")
        conv_ready, ss_ready, ss_inv, ss_root = sem("conv_ready"), sem("ss_ready"), sem("ss_inv"), sem("ss_root")
        lat_norm, lat_hi, lat_lo, kr_ready = sem("lat_norm"), sem("lat_hi"), sem("lat_lo"), sem("kr_ready")
        sc_done, sc_read = sem("sc_done"), sem("sc_read")
        subk_in = sem("subk_in")
        shifted, exp_done, picks_ready = sem("shifted"), sem("exp_done"), sem("picks_ready")
        turned, turned_read = sem("turned"), sem("turned_read")
        hot_ready, hot_used, gate_read = sem("hot_ready"), sem("hot_used"), sem("gate_read")
        gates_out = sem("gates_out")
        a_st = [sem(f"a_stored{i}") for i in range(2)]
        ag_in = [sem(f"ag_in{i}") for i in range(4)]
        p_made, p_hi, p_lo = sem("p_made"), sem("p_hi"), sem("p_lo")
        v_done, v_taken = sem("v_done"), sem("v_taken")
        y_ready, y_out = sem("y_ready"), sem("y_out")
        block = ctx.enter_context(nc.Block())

        N_CONST, N_CONST1 = 12, 5
        FIRST_MOD = 16
        MOD_BESIDE = {1: 2, **{n: 3 for n in range(8, 12)}, **{n: 2 for n in range(12, 21)}}
        MOD_BEFORE_ROPE, MOD_BEFORE_CONV = 14, (6, 4, 4, 4)
        EARLY = 5
        BUILT = (1, 1, 2, 2, 2, 2, 3, 3)
        COPIED = (0, 0, 2, 3, 3, 2, 3, 3)
        OUT = {l: product_at(l, "out") for l in range(2)}
        WQ = {l: product_at(l, "wq") for l in range(2)}
        UM = {l: product_at(l, "u") for l in range(2)}
        IN = {l: product_at(l, "in") for l in range(2)}
        DZV = product_at(1, "dzv")
        UKV, HEAD = product_at(1, "ukv_v"), product_at(1, "head")
        UC = {l: chunk_at(l, "u") for l in range(2)}
        VC = {l: chunk_at(l, "v") for l in range(2)}
        BODIES = NKEY // SPLIT
        NUNIT = NT * NH
        FIRST_G = {0: 0, 1: NKEY // GROUP}

        SQ = [0, 8, 16, 24, 27, 29, 37]
        UNITS0 = [(j, s, b) for j in range(4) for s in range(2) for b in range(NT)]

        def local(b):
            lo, hi = max(1, b - 1), min(4, b + 1)
            return lo + 1, hi - lo + 1

        def key_tiles(b):
            return [1] if b == 0 else [0] + [local(b)[0] + c for c in range(local(b)[1])]

        def s_bank(u):
            return (aux[0][:, 0, :], aux[0][:, 1, :], acc[0][:, 0, :])[u % 3]

        def keys_of(b):
            return P if b == 0 else P + local(b)[1] * P

        def halves(t):
            return t.rearrange("p (h t) -> p h t", h=2)

        def wait(eng, s, value):
            if not isinstance(value, int) or value > 0:
                eng.wait_ge(s, value)

        def has_taken(eng, m):
            eng.wait_ge(taken[m % 2], m // 2 + 1)

        def source(n):
            layer, kind, i, size = CHUNKS[n][:4]
            if kind in ("u", "v"):
                return a[kind][layer, i]
            if kind == "wq":
                return a["wq"][layer, i]
            if kind == "head":
                return a["head"][i]
            if kind == "dzv":
                return a["in1"][i]
            if kind == "in" and layer == 1:
                return a["in1"][4 + i]
            if kind == "ukv_v":
                return a["ukv_v"]
            return a[f"{kind}{layer}"][i]

        @block.sync
        def _(sp):
            def load_chunk(n):
                if n >= RAW:
                    sp.wait_ge(lo_done, n - RAW + 1)
                sp.dma_start(raw[:, n % RAW, 0:CHUNKS[n][3]], source(n)).then_inc(raw_in[n % RAW], 16)

            for n in range(RAW):
                load_chunk(n)
            for k in range(FIRST_MOD):
                if k >= 8:
                    sp.wait_ge(mod_used, k - 7)
                sp.dma_start(w_mod[:, k % 8], a["w_mod"][0, k]).then_inc(mod_in[k % 8], 16)

            for l in range(2):
                tile = FIRST_MOD
                for n in range(0 if l else RAW - 1, len(CHUNKS)):
                    if CHUNKS[n][0] == l and CHUNKS[n][1] not in ("u", "v"):
                        if l or n >= RAW:
                            load_chunk(n)
                        if l == 0:
                            for k in range(tile, tile + MOD_BESIDE.get(n, 0)):
                                if k >= FIRST_MOD + 2:
                                    sp.wait_ge(mod_used, k - 1)
                                sp.dma_start(w_mod_b[:, k % 2], a["w_mod"][0, k]).then_inc(mod_b_in[k % 2], 16)
                            tile += MOD_BESIDE.get(n, 0)
                with sp.Fori(0, BODIES) as i:
                    for u in range(SPLIT):
                        n = UC[l] + SPLIT * i + u
                        sp.wait_ge(lo_done, n - RAW + 1)
                        sp.dma_start(raw[:, (UC[l] + u) % RAW],
                                     a["u"][l, bass.ds(SPLIT * i + u, 1)].rearrange("o p n -> (o p) n"))\
                          .then_inc(raw_in[(UC[l] + u) % RAW], 16)
                def load_raw(c, u):
                    sp.wait_ge(lo_done, VC[l] + c - RAW + 1)
                    sp.dma_start(raw[:, (VC[l] + u) % RAW], a["v"][l, bass.ds(c, 1)].rearrange("o p n -> (o p) n"))\
                      .then_inc(raw_in[(VC[l] + u) % RAW], 16)

                def load_ag(c, u):
                    if not (isinstance(c, int) and c < 4):
                        sp.wait_ge(p_made, NKEY * l + c - 3)
                    for w, src in enumerate((a["act_s"], a["gate_s"])):
                        sp.dma_start(ag[:, u % 4, w], src[l, bass.ds(c, 1)].rearrange("o p n -> (o p) n"))\
                          .then_inc(ag_in[u % 4], 16)

                for u in range(GROUP):
                    load_raw(u, u)
                sp.wait_ge(gates_out, 16 * 10 * (l + 1))
                for s in range(2):
                    sp.wait_ge(a_st[s], 16 * (64 * l + SPLIT // 2))
                for u in range(GROUP):
                    load_ag(u, u)
                for u in range(GROUP, SPLIT):
                    load_raw(u, u)
                for u in range(GROUP, SPLIT):
                    load_ag(u, u)
                for s in range(2):
                    sp.wait_ge(a_st[s], 16 * 64 * (l + 1))
                if l == 0:
                    for u in range(3):
                        sp.dma_start(w_mod_v[:, u], a["w_mod"][1, u]).then_inc(mod_v_in[u], 16)
                with sp.Fori(1, BODIES) as i:
                    for u in range(SPLIT):
                        load_raw(u + SPLIT * i, u)
                        load_ag(u + SPLIT * i, u)
                        if l == 0 and u < 3:
                            sp.wait_ge(mod_v_used, u + 1 - 3 + 3 * i)
                            sp.dma_start(w_mod_v[:, u], a["w_mod"][1, bass.ds(u + 3 * i, 1)]
                                         .rearrange("o p n -> (o p) n")).then_inc(mod_v_in[u], 16)
            for k in range(KD):
                sp.wait_ge(y_ready, k + 1)
                sp.dma_start(a["y"][:, k, :], y[:, k, :]).then_inc(y_out, 16)
            sp.wait_ge(y_out, 16 * KD)
            sp.wait_ge(state_out, 16 * 4)

        @block.gpsimd
        def _(pool):
            def low(n, slot, rslot, size):
                pool.wait_ge(hi_done, n + 1)
                pool.tensor_tensor(w_lo[:, slot, 0:size], raw[:, rslot, 0:size],
                                   w_hi[:, slot, 0:size].bitcast(F), ALU.subtract).then_inc(lo_done, 1)

            def last_use(n):
                layer, kind, i, size, first, past = CHUNKS[n]
                if kind == "v":
                    return v_done, 16 * (FIRST_G[layer] + i // GROUP + 1)
                return made, past

            def split_chunk(n):
                slot, rslot, size = n % SPLIT, n % RAW, CHUNKS[n][3]
                pool.wait_ge(raw_in[rslot], 16 * (n // RAW + 1))
                if n >= SPLIT:
                    pool.wait_ge(*last_use(n - SPLIT))
                pool.tensor_copy(w_hi[:, slot, 0:size], raw[:, rslot, 0:size]).then_inc(hi_done, 1)
                low(n, slot, rslot, size)

            def split_loop(first, free_sem, free_base, per_body, free_steps, start):
                with pool.Fori(start, BODIES) as i:
                    for u in range(SPLIT):
                        n0 = first + u
                        pool.wait_ge(raw_in[n0 % RAW], 16 * (n0 // RAW + 1) + 16 * (SPLIT // RAW) * i)
                        pool.wait_ge(free_sem, free_base + free_steps[u] + per_body * i)
                        pool.sem_inc(slot_free, 1)
                        pool.tensor_copy(w_hi[:, n0 % SPLIT, :], raw[:, n0 % RAW, :]).then_inc(hi_done, 1)
                        low(n0 + SPLIT * i, n0 % SPLIT, n0 % RAW, 1024)

            for l in range(2):
                for n in range(len(CHUNKS)):
                    if CHUNKS[n][0] == l and CHUNKS[n][1] not in ("u", "v"):
                        split_chunk(n)
                split_loop(UC[l], made, UM[l] - SPLIT, SPLIT, [u + 1 for u in range(SPLIT)], 0)
                for u in range(SPLIT):
                    split_chunk(VC[l] + u)
                split_loop(VC[l], v_done, 16 * FIRST_G[l], 32,
                           [16 * (u // GROUP) - 16 for u in range(SPLIT)], 1)

        @block.tensor
        def _(pe):
            def begin(m):
                pe.wait_ge(lo_done, PRODUCTS[m][4] + 1)
                if m >= 2:
                    pe.wait_ge(taken[m % 2], m // 2)
                return acc[m % 2], PRODUCTS[m][4] % SPLIT

            def linear_step(out, w, width, k, kt, hi, lo, n, off=0):
                wh = w_hi[:, w, off + k * width:off + (k + 1) * width]
                wl = w_lo[:, w, off + k * width:off + (k + 1) * width]
                pe.matmul(out, wh, hi[:, k, n], start=(k == 0), stop=False)
                pe.matmul(out, wh, lo[:, k, n], start=False, stop=False)
                return pe.matmul(out, wl, hi[:, k, n], start=False, stop=(k == kt - 1))

            def linear(out, w, width, kt, hi, lo, n, off=0):
                for k in range(kt):
                    mm = linear_step(out, w, width, k, kt, hi, lo, n, off)
                return mm

            def by_feature(m, width=P, kt=KD, hi=a_hi, lo=a_lo, cols=HALF, off=0):
                bank, w = begin(m)
                for h in range(2):
                    mm = linear(bank[0:width, h, 0:cols], w, width, kt, hi, lo,
                                slice(h * cols, (h + 1) * cols), off)
                mm.then_inc(made, 1)

            def by_token(m, tiles, width, kt=KD, hi=a_hi, lo=a_lo, weights=None):
                bank, w = begin(m)
                flat = bank[:].rearrange("p a n -> p (a n)")
                weights = weights or (lambda t, k: t[:, w, k * width:(k + 1) * width])
                for j, tile in enumerate(tiles):
                    n = slice(tile * P, tile * P + P)
                    out = flat[:, j * width:(j + 1) * width]
                    for k in range(kt):
                        pe.matmul(out, hi[:, k, n], weights(w_hi, k), start=(k == 0), stop=False)
                        pe.matmul(out, lo[:, k, n], weights(w_hi, k), start=False, stop=False)
                        mm = pe.matmul(out, hi[:, k, n], weights(w_lo, k), start=False, stop=(k == kt - 1))
                mm.then_inc(made, 1)

            norms = [0]

            def norm_sums(tiles=KD):
                i = norms[0]
                if i:
                    pe.wait_ge(var_ready, i)
                for k in range(tiles):
                    q = SQ[i] + k
                    pe.wait_ge(sq_ready, q + 1)
                    for h in range(2):
                        mm = pe.matmul(aux[0][:, h, 0:HALF], ones[:], tmp[:, q % 2, h * HALF:(h + 1) * HALF],
                                       start=(k == 0), stop=(k == tiles - 1), skip_group_check=True)
                    mm.then_inc(sq_used, 1)
                norms[0] += 1

            def rope_turn(i, m, src, rows=P):
                has_taken(pe, m)
                if i >= 2:
                    pe.wait_ge(rope_applied, i - 1)
                pe.matmul(aux[1][0:rows, i % 2, :], perm[0:rows, 0:rows], src, start=True, stop=True)\
                  .then_inc(rope_done, 1)

            def scores_of(u):
                j, s, b = UNITS0[u]
                rows = slice(64 * s, 64 * s + 64)
                if u >= 3:
                    pe.wait_ge(s_read, u - 2)
                q = y[rows, 4 + j, b * P:(b + 1) * P]
                bank = s_bank(u)
                if b == 0:
                    pe.matmul(bank[:, 0:P], q, kT[rows, P:2 * P], start=True, stop=True).then_inc(s_done, 1)
                else:
                    lo, n = local(b)
                    pe.matmul(bank[:, 0:P], q, kT[rows, 0:P], start=True, stop=True)
                    pe.matmul(bank[:, P:P + n * P], q, kT[rows, lo * P:(lo + n) * P], start=True, stop=True)\
                      .then_inc(s_done, 1)

            norm_sums()
            for m in range(IN[0], IN[0] + 6):
                if m == IN[0]:
                    pe.wait_ge(lo_ready, KD)
                if m == IN[0] + 5:
                    by_token(m, range(NT), P)
                else:
                    by_feature(m)
            for i in range(5):
                rope_turn(i, IN[0] + i, y[:, 4 + i, NP_TOK:T] if i < 4 else kT[:, 2 * P:6 * P])
            for m in range(IN[0] + 6, IN[0] + 18):
                by_feature(m)
            pe.wait_ge(rope_applied, 5)
            has_taken(pe, IN[0] + 5)
            pe.wait_ge(cache_in, 32)
            for m in (IN[0] + 16, IN[0] + 17):
                has_taken(pe, m)
            for u in range(3):
                scores_of(u)

            def weigh(v):
                j, s, b = UNITS0[v]
                tiles = key_tiles(b)
                pe.wait_ge(pt_ready, v + 1)
                if v >= 1:
                    pe.wait_ge(pv_read, v)
                for c, tile in enumerate(tiles):
                    mm = pe.matmul(aux[1][64 * s:64 * s + 64, 1, 0:P], vt[:, tile, 64 * s:64 * s + 64],
                                   pt_sb[:, v % 2, c * P:(c + 1) * P],
                                   start=(c == 0), stop=(c == len(tiles) - 1))
                mm.then_inc(pv_done, 1)

            for v in range(NUNIT):
                if v + 3 < NUNIT:
                    scores_of(v + 3)
                pe.wait_ge(p_ready, v + 1)
                if v >= 1:
                    pe.wait_ge(pt_ready, v)
                for c in range(len(key_tiles(UNITS0[v][2]))):
                    mm = pe.transpose(aux[1][:, 0, c * P:(c + 1) * P],
                                      s_sb[:, v % 4, c * P:(c + 1) * P], ident[:])
                mm.then_inc(pt_done, 1)
                if v >= 1:
                    weigh(v - 1)
            weigh(NUNIT - 1)

            def out_and_route(l):
                pe.wait_ge(lo_ready, KD * (2 + 3 * l))
                for m in range(OUT[l], OUT[l] + KD):
                    by_feature(m)
                norm_sums()
                pe.wait_ge(lo_ready, KD * (3 + 3 * l))

                def keys(i):
                    has_taken(pe, WQ[l] + i)
                    n = 16 * l + i
                    if i == 0:
                        pe.wait_ge(subk_in, 16 * (l + 1))
                    if n >= 2:
                        pe.wait_ge(sc_read, n - 1)
                    for t in range(NT):
                        mm = pe.matmul(aux[n % 2][:, t // 4, (t % 4) * P:(t % 4 + 1) * P],
                                       tmp[:, i % 2, t * P:(t + 1) * P], subk[:, i, :], start=True, stop=True)
                    mm.then_inc(sc_done, 1)

                for i in range(16):
                    by_feature(WQ[l] + i)
                    if i >= 1:
                        keys(i - 1)
                keys(15)

            def experts(l):
                def expert(m0, w, split_value, taken_value, beside=0, between=None):
                    pe.wait_ge(lo_done, split_value)
                    pe.wait_ge(taken[m0 % 2], taken_value)
                    spots = [2 * KD * (j + 1) // beside - 1 for j in range(beside)]
                    for h in range(2):
                        n = slice(h * HALF, (h + 1) * HALF)
                        for k in range(KD):
                            mm = linear_step(acc[m0 % 2][:, h, 0:HALF], w, P, k, KD, a_hi, a_lo, n)
                            if h == 1 and k == KD - 1:
                                mm.then_inc(made, 1)
                            if KD * h + k in spots:
                                between()

                with pe.Fori(0, EARLY) as i:
                    for u in range(SPLIT):
                        expert(UM[l] + u, (UC[l] + u) % SPLIT, UC[l] + u + 1 + SPLIT * i,
                               (UM[l] + u) // 2 + (SPLIT // 2) * i)
                pe.wait_ge(picks_ready, l + 1)
                for n in range(15 * l, 15 * l + 15):
                    t, w = (n - 15 * l) // 3, n % 3
                    if n >= 4:
                        pe.wait_ge(turned_read, n - 3)
                    pe.transpose(aux[(n % 4) // 2][:, n % 2, 0:P], picks[:, w, t, :], ident[:])\
                      .then_inc(turned, 1)
                pe.wait_ge(turned_read, 15 * (l + 1))

                def gates_of_four(n, q):
                    wait(pe, gate_read, n - 3)
                    pe.wait_ge(hot_ready, n + 1)
                    for j in range(4):
                        tok = (4 * q + j) % 8
                        mm = pe.matmul(aux[(q % 4) // 2][:, q % 2, j * P:(j + 1) * P],
                                       one_a[:, tok, :], one_b[:, tok, :], start=True, stop=True)
                    mm.then_inc(hot_used, 1)

                def late(i):
                    for k in range(2):
                        built = iter(range(16))

                        def next_four():
                            q = next(built)
                            gates_of_four(160 * l + 16 * k + q + 32 * i, q)

                        for u in range(SPLIT):
                            c = SPLIT * (EARLY + k) + u
                            expert(UM[l] + c, (UC[l] + c) % SPLIT, UC[l] + c + 1 + 2 * SPLIT * i,
                                   (UM[l] + c) // 2 + SPLIT * i, BUILT[u], next_four)

                late(0)
                with pe.Fori(1, NT) as i:
                    late(i)
                for c in range(NKEY - SPLIT, NKEY):
                    expert(UM[l] + c, (UC[l] + c) % SPLIT, UC[l] + c + 1, (UM[l] + c) // 2)

                for m in (UM[l] + NKEY - 2, UM[l] + NKEY - 1):
                    has_taken(pe, m)

                def values(i):
                    for gg in range(2):
                        g = FIRST_G[l] + 2 * i + gg
                        pe.wait_ge(p_lo, 4 * g + 4)
                        pe.wait_ge(lo_done, VC[l] + 4 * (2 * i + gg) + 4)
                        for o in range(16):
                            dt, h = o // 2, o % 2
                            wait(pe, v_taken, 16 * g + o - 3)
                            out = acc[(o % 4) // 2][:, o % 2, 0:HALF]
                            n = slice(h * HALF, (h + 1) * HALF)
                            for c in range(GROUP):
                                w = (VC[l] + GROUP * gg + c) % SPLIT
                                ps = GROUP * gg + c
                                wh, wl = w_hi[:, w, dt * P:(dt + 1) * P], w_lo[:, w, dt * P:(dt + 1) * P]
                                pe.matmul(out, wh, a_hi[:, ps, n], start=(c == 0), stop=False)
                                pe.matmul(out, wh, a_lo[:, ps, n], start=False, stop=False)
                                mm = pe.matmul(out, wl, a_hi[:, ps, n], start=False, stop=(c == GROUP - 1))
                            mm.then_inc(v_done, 1)

                values(0)
                with pe.Fori(1, BODIES) as i:
                    values(i)

            out_and_route(0)
            experts(0)

            pe.wait_ge(v_taken, 16 * FIRST_G[1])
            norm_sums()
            pe.wait_ge(lo_ready, 4 * KD)
            first = chunk_at(1, "dzv") % SPLIT
            for i, tiles in enumerate(((0, 1), (2, 3), (4,))):
                by_token(DZV + i, tiles, 512,
                         weights=lambda t, k: t[:, first:first + 4, k * P:(k + 1) * P])
            for m in range(IN[1], IN[1] + 10):
                by_feature(m)
            pe.wait_ge(const1_in, 16 * N_CONST1)
            for t in range(NT):
                pe.wait_ge(vv_ready, t + 1)
                if t >= 2:
                    pe.wait_ge(mix_read, t - 1)
                for g in range(4):
                    out = aux[1][:, t % 2, g * P:(g + 1) * P]
                    pe.matmul(out, vv[:, t, g * P:(g + 1) * P], ws_t[:, g, :], start=True, stop=False)
                    mm = pe.matmul(out, ones[0:1, :], b_s[:, g, :], start=False, stop=True)
                mm.then_inc(mix_done, 1)
            pe.wait_ge(mix_read, NT)
            norm_sums(3)
            norm_sums(2)
            has_taken(pe, IN[1] + 9)
            pe.matmul(aux[1][0:32, 1, :], perm[0:32, 96:128], kr[:, NP_TOK:T],
                      start=True, stop=True).then_inc(rope_done, 1)
            pe.wait_ge(lat_lo, 5)
            for i in range(3):
                by_token(UKV + i, [2 * i, 2 * i + 1], 512, 2, ckv_hi, ckv_lo)
            pe.wait_ge(kr_ready, 1)
            pe.wait_ge(cache1_in, 16 * 4)

            flat0 = [b[:].rearrange("p a n -> p (a n)") for b in (aux[0], acc[0])]
            flat1 = aux[1][:].rearrange("p a n -> p (a n)")

            def head_product(h, which):
                m = HEAD + 2 * h + which
                pe.wait_ge(lo_done, PRODUCTS[m][4] + 1)
                has_taken(pe, m - 1)
                w = PRODUCTS[m][4] % SPLIT
                width, kt, hi, lo, cols, off = ((96, 3, cq_hi, cq_lo, HALF, 0),
                                                (P, 2, ckv_hi, ckv_lo, 384, 288))[which]
                if which == 1:
                    pe.wait_ge(rope_applied, 7 + h)
                for half in range(2):
                    mm = linear(acc[1][0:width, half, 0:cols], w, width, kt, hi, lo,
                                slice(half * cols, (half + 1) * cols), off)
                mm.then_inc(made, 1)

            def head_turn(h):
                has_taken(pe, HEAD + 2 * h)
                pe.matmul(acc[1][0:96, 0, :], perm[0:96, 0:96], q_head[:, h % 2, NP_TOK:T],
                          start=True, stop=True).then_inc(rope_done, 1)

            def scores_c(v):
                h, b = divmod(v, NT)
                if b == 0:
                    has_taken(pe, HEAD + 2 * h + 1)
                if v >= 2:
                    pe.wait_ge(s_read, NUNIT + v - 1)
                q, s = q_head[:, h % 2, b * P:(b + 1) * P], flat0[v % 2]
                if b == 0:
                    mm = pe.matmul(s[:, 0:P], q, k_head[:, h % 2, 0:P], start=True, stop=True)
                else:
                    pe.matmul(s[:, 0:512], q, k_head[:, h % 2, P:P + 512], start=True, stop=True)
                    mm = pe.matmul(s[:, 512:640], q, k_head[:, h % 2, P + 512:768], start=True, stop=True)
                mm.then_inc(s_done, 1)

            has_taken(pe, HEAD - 1)
            has_taken(pe, HEAD - 2)
            head_product(0, 0)
            head_turn(0)
            head_product(0, 1)
            scores_c(0)
            scores_c(1)
            for v in range(NUNIT):
                h, b = divmod(v, NT)
                if h + 1 < NH:
                    if b == 0:
                        head_product(h + 1, 0)
                    elif b == 1:
                        head_turn(h + 1)
                    elif b == 2:
                        head_product(h + 1, 1)
                tiles = [0] if b == 0 else [1, 2, 3, 4, 5]
                pe.wait_ge(p_ready, NUNIT + v + 1)
                if v >= 1:
                    pe.wait_ge(pt_ready, NUNIT + v)
                    pe.wait_ge(pv_read, NUNIT + v)
                for c in range(len(tiles)):
                    mm = pe.transpose(flat1[:, c * P:(c + 1) * P], p_sb[:, v % 2, c * P:(c + 1) * P], ident[:])
                mm.then_inc(pt_done, 1)
                if v + 2 < NUNIT:
                    scores_c(v + 2)
                pe.wait_ge(pt_ready, NUNIT + v + 1)
                r = 64 * (h % 2)
                for c, tile in enumerate(tiles):
                    mm = pe.matmul(flat1[r:r + 64, 768:896], vt1[:, tile, 64 * h:64 * h + 64],
                                   pt1[:, c * P:(c + 1) * P], start=(c == 0), stop=(c == len(tiles) - 1))
                mm.then_inc(pv_done, 1)
            out_and_route(1)
            experts(1)
            pe.wait_ge(v_taken, 16 * 2 * FIRST_G[1])
            norm_sums()

        @block.scalar
        def _(act):
            act.dma_start(c_all[:], a["c_all"]).then_inc(c_in, 16)
            for dst, name in ((x, "x"), (ident, "ident"), (ones, "ones"), (iota, "iota"),
                              (mask, "mask"), (perm, "perm0"), (rope, "rope0"), (b_mod, "b_mod"),
                              (g_norm, "g_norm"), (sink, "sink"), (conv_w, "conv_w"), (g_small, "g_small")):
                act.dma_start(dst[:], a[name]).then_inc(const_in, 16)
            act.wait_ge(c_in, 16)
            act.activation(c_all[:], c_all[:], ACT.Silu).then_inc(silu_ready, 1)
            act.wait_ge(const_in, 16 * N_CONST)

            norm = [0]

            def squares(src, tiles=KD):
                for k in range(tiles):
                    q = SQ[norm[0]] + k
                    if q >= 2:
                        act.wait_ge(sq_used, q - 1)
                    act.activation(tmp[:, q % 2, :], src[:, k, :], ACT.Square).then_inc(sq_ready, 1)

            def root():
                act.wait_ge(var_ready, norm[0] + 1)
                act.activation(rstd[:], rstd[:], ACT.Sqrt).then_inc(rstd_ready, 1)
                norm[0] += 1

            def high(n):
                for k in range(KD):
                    act.wait_ge(h_ready, KD * n + k + 1)
                    act.activation(a_hi[:, k, :], tmp[:, k % 2, :], ACT.Copy).then_inc(hi_ready, 1)

            def take(m, out, in_, func=ACT.Copy):
                act.wait_ge(made, m + 1)
                act.activation(out, in_, func).then_inc(taken[m % 2], 1)

            def feature(m, width=P, cols=HALF):
                return acc[m % 2][0:width, :, 0:cols]

            squares(x)
            root()
            high(0)
            act.wait_ge(mod_used, FIRST_MOD)
            act.dma_start(kT[:, 0:P], a["cache_k"]).then_inc(cache_in, 16)
            act.dma_start(vt[:, 0, :], a["cache_v"]).then_inc(cache_in, 16)
            for i in range(4):
                take(IN[0] + i, halves(y[:, 4 + i, :]), feature(IN[0] + i))
            m = IN[0] + 4
            take(m, halves(kT[:, P:768]), feature(m))
            has_taken(act, m)
            act.dma_start(a["new_k"], kT[:, P:2 * P]).then_inc(state_out, 16)
            m = IN[0] + 5
            act.wait_ge(made, m + 1)
            act.activation(vt[:, 1:5, :].rearrange("p t n -> p (t n)"), acc[m % 2][:, 0, :], ACT.Copy)
            act.activation(vt[:, 5, :], acc[m % 2][:, 1, 0:P], ACT.Copy).then_inc(taken[m % 2], 1)
            has_taken(act, m)
            act.dma_start(a["new_v"], vt[:, 1, :]).then_inc(state_out, 16)
            for j in range(4):
                m = IN[0] + 6 + 3 * j
                take(m, halves(y[:, j, :]), feature(m))
                if j:
                    has_taken(act, m - 1)
                take(m + 1, halves(gate_c[:]), feature(m + 1))
            act.wait_ge(mod_used, 48)
            for u in range(NUNIT + 4):
                if 3 <= u < NUNIT + 3:
                    v = u - 3
                    n = keys_of(UNITS0[v][2])
                    act.wait_ge(pt_done, v + 1)
                    if v >= 2:
                        act.wait_ge(pv_done, v - 1)
                    act.activation(pt_sb[:, v % 2, 0:n], aux[1][:, 0, 0:n], ACT.Copy).then_inc(pt_ready, 1)
                if u >= 4:
                    v = u - 4
                    j, s, b = UNITS0[v]
                    rows = slice(64 * s, 64 * s + 64)
                    act.wait_ge(pv_done, v + 1)
                    act.activation(y[rows, 4 + j, b * P:(b + 1) * P], aux[1][rows, 1, 0:P], ACT.Copy)\
                       .then_inc(pv_read, 1)
                if u < NUNIT:
                    j, s, b = UNITS0[u]
                    n, st, hd = keys_of(b), stat[:, u % 4, :], 4 * s + j
                    act.wait_ge(neg_ready, u + 1)
                    act.activation(s_sb[:, u % 4, 0:n], s_sb[:, u % 4, 0:n], ACT.Exp, bias=st[:, 1:2],
                                   accum_out=st[:, 2:3])
                    act.activation(st[:, 3:4], sink[:, hd:hd + 1], ACT.Exp, bias=st[:, 1:2]).then_inc(e_ready, 1)

            def out_and_route(l):
                act.wait_ge(pv_read, NUNIT * (l + 1))
                act.dma_start(subk[:], a["subk"][l]).then_inc(subk_in, 16)
                if l == 0:
                    act.wait_ge(conv_ready, 4)
                else:
                    act.wait_ge(mix_read, NT)
                act.wait_ge(made, OUT[l])
                for k in range(KD):
                    act.activation(a_hi[:, k, :], y[:, k, :], ACT.Copy).then_inc(hi_ready, 1)
                for m in (OUT[l] + 6, OUT[l] + 7):
                    has_taken(act, m)
                squares(x)
                root()
                high(2 * l + 1)
                act.wait_ge(lo_ready, KD * (3 + 3 * l))
                for i in range(16):
                    m, n = WQ[l] + i, 16 * l + i
                    if i >= 2:
                        act.wait_ge(sc_done, n - 1)
                    take(m, halves(tmp[:, i % 2, :]), feature(m))

            def experts(l):
                def activation(u, made_value, stored_value, taken_value, c):
                    m0 = UM[l] + u
                    act.wait_ge(made, made_value)
                    wait(act, a_st[u % 2], stored_value)
                    act.activation(halves(a_out[:, u % 2, :]), feature(m0), ACT.Gelu_apprx_tanh)\
                       .then_inc(taken[m0 % 2], 1)
                    act.wait_ge(taken[m0 % 2], taken_value)
                    act.dma_start(a["act_s"][l, bass.ds(c, 1)].rearrange("o p n -> (o p) n"),
                                  a_out[:, u % 2, :]).then_inc(a_st[u % 2], 16)

                def early(i):
                    for u in range(SPLIT):
                        m0 = UM[l] + u
                        activation(u, m0 + 1 + SPLIT * i, 1024 * l + 16 * (u // 2) + 64 * i,
                                   m0 // 2 + 1 + 4 * i, SPLIT * i + u)

                early(0)
                with act.Fori(1, EARLY) as i:
                    early(i)
                act.wait_ge(shifted, l + 1)
                gate_in = picks[:, 2, :, :]
                act.activation(gate_in, gate_in, ACT.Exp).then_inc(exp_done, 1)
                for n in range(15 * l, 15 * l + 15):
                    t, w = (n - 15 * l) // 3, n % 3
                    act.wait_ge(turned, n + 1)
                    act.activation(picks_t[:, w, t * P:(t + 1) * P], aux[(n % 4) // 2][:, n % 2, 0:P],
                                   ACT.Copy).then_inc(turned_read, 1)

                def late(i):
                    for k in range(2):
                        q = 0
                        for u in range(SPLIT):
                            c = SPLIT * (EARLY + k) + u
                            m0 = UM[l] + c
                            activation(c, m0 + 1 + 16 * i, 1024 * l + 16 * (c // 2) + 128 * i,
                                       m0 // 2 + 1 + 8 * i, c + 16 * i)
                            for _ in range(COPIED[u]):
                                n = 160 * l + 16 * k + q + 32 * i
                                act.wait_ge(hot_used, n + 1)
                                if q == 0:
                                    wait(act, gates_out, 160 * l + 16 * k + 32 * i)
                                act.activation(gates[:, :, 4 * q:4 * q + 4].rearrange("p e t -> p t e"),
                                               aux[(q % 4) // 2][:, q % 2, :].rearrange("p (t e) -> p t e", t=4),
                                               ACT.Copy).then_inc(gate_read, 1)
                                q += 1
                        act.wait_ge(gate_read, 160 * l + 16 * k + 16 + 32 * i)
                        act.dma_start(a["gate_s"][l, :, :, bass.ds(128 * i + 64 * k, 64)]
                                      .rearrange("e p t -> p e t"), gates[:]).then_inc(gates_out, 16)

                late(0)
                with act.Fori(1, NT) as i:
                    late(i)
                for c in range(NKEY - SPLIT, NKEY):
                    m0 = UM[l] + c
                    activation(c, m0 + 1, 1024 * l + 16 * (c // 2), m0 // 2 + 1, c)
                def high_p(i, chunks=range(SPLIT)):
                    for k in chunks:
                        n = NKEY * l + k + SPLIT * i
                        act.wait_ge(p_made, n + 1)
                        if not (isinstance(i, int) and i == 0):
                            act.wait_ge(v_done, 16 * (FIRST_G[l] + k // GROUP - 1) + 32 * i)
                        act.activation(a_hi[:, k, :], p_raw[:, k % 2, :], ACT.Copy).then_inc(p_hi, 1)

                high_p(0, range(GROUP))
                if l == 0:
                    act.dma_start(c_all_v[:], a["c_all"]).then_inc(c_in, 16)
                    act.wait_ge(c_in, 32)
                    act.activation(c_all_v[:], c_all_v[:], ACT.Silu).then_inc(silu_ready, 1)
                high_p(0, range(GROUP, SPLIT))
                with act.Fori(1, BODIES) as i:
                    high_p(i)

            out_and_route(0)
            experts(0)

            act.wait_ge(v_taken, 16 * FIRST_G[1])
            for dst, name in ((perm, "perm1"), (rope, "rope1"), (ws_t, "ws_t"), (b_s, "b_s"), (g_sgu, "g_sgu")):
                act.dma_start(dst[:], a[name]).then_inc(const1_in, 16)
            squares(x)
            root()
            high(2)
            for i in range(3):
                m, n = DZV + i, min(2, NT - 2 * i)
                take(m, vv[:, 2 * i:2 * i + n, :], acc[m % 2][:, 0:n, :], ACT.Gelu_apprx_tanh)
            for c in range(4):
                m = IN[1] + c
                take(m, halves(y[:, 4 + c, :]), feature(m), ACT.Gelu_apprx_tanh)
            for i in (1, 2):
                has_taken(act, DZV + i)
            act.wait_ge(lo_ready, KD * 4)
            for t in range(NT):
                if t:
                    act.wait_ge(ss_ready, t)
                act.activation(rstd[:, 0:512], vv[:, t, :], ACT.Square, accum_out=ss[:, t:t + 1])\
                   .then_inc(ss_ready, 1)
            for c in range(3):
                m = IN[1] + 4 + c
                take(m, halves(cq[:, c, :]), feature(m))
            for c in range(2):
                m = IN[1] + 7 + c
                take(m, halves(ckv[:, c, :]), feature(m))
            m = IN[1] + 9
            take(m, halves(kr[:]), acc[m % 2][0:32, :, 0:HALF])
            has_taken(act, m)
            act.dma_start(a["new_kr"], kr[:, 0:NP_TOK]).then_inc(state_out, 16)
            act.dma_start(kr_rope[:], a["rope_k"]).then_inc(cache1_in, 16)
            act.dma_start(ckv_old[:], a["cache_ckv"]).then_inc(cache1_in, 16)
            for i in range(2):
                act.dma_start(k_head[64:96, i, P:2 * P], a["cache_kr"]).then_inc(cache1_in, 16)
            act.wait_ge(ss_inv, 1)
            act.activation(ss[:, 0:NT], ss[:, 0:NT], ACT.Sqrt).then_inc(ss_root, 1)
            act.wait_ge(mix_read, NT)
            squares(cq, 3)
            root()
            for k in range(3):
                act.wait_ge(lat_norm, k + 1)
                act.activation(cq_hi[:, k, :], cq[:, k, :], ACT.Copy).then_inc(lat_hi, 1)
            act.wait_ge(lat_norm, 3)
            squares(ckv, 2)
            root()
            act.wait_ge(cache1_in, 16 * 4)
            for k in range(2):
                act.wait_ge(lat_norm, 4 + k)
                act.activation(ckv_hi[:, k, 0:P], ckv[:, k, 0:P], ACT.Copy)
                act.activation(ckv_hi[:, k, P:2 * P], ckv_old[:, k, :], ACT.Copy)
                act.activation(ckv_hi[:, k, 2 * P:768], ckv[:, k, P:T], ACT.Copy).then_inc(lat_hi, 1)
            act.dma_start(a["new_ckv"], ckv[:, :, 0:P]).then_inc(state_out, 16)
            for i in range(3):
                m = UKV + i
                take(m, vt1[:, 2 * i:2 * i + 2, :], acc[m % 2][:])
            act.wait_ge(rope_applied, 6)
            act.wait_ge(kr_ready, 1)
            flat0 = [b[:].rearrange("p a n -> p (a n)") for b in (aux[0], acc[0])]
            flat1 = aux[1][:].rearrange("p a n -> p (a n)")

            def take_head(h, which):
                m = HEAD + 2 * h + which
                act.wait_ge(made, m + 1)
                out, rows, cols = ((q_head[:, h % 2, :], 96, HALF), (k_head[0:64, h % 2, :], 64, 384))[which]
                act.activation(halves(out), acc[1][0:rows, :, 0:cols], ACT.Copy).then_inc(taken[m % 2], 1)

            take_head(0, 0)
            take_head(0, 1)
            for u in range(NUNIT + 2):
                if u >= 2:
                    v = u - 2
                    h, b = divmod(v, NT)
                    n = P if b == 0 else T
                    rows = slice(64 * (h % 2), 64 * (h % 2) + 64)
                    if h + 1 < NH and b in (0, 2):
                        take_head(h + 1, b // 2)
                    act.wait_ge(pt_done, NUNIT + v + 1)
                    act.activation(pt1[:, 0:n], flat1[:, 0:n], ACT.Copy).then_inc(pt_ready, 1)
                    act.wait_ge(pv_done, NUNIT + v + 1)
                    act.activation(y[rows, h // 2, b * P:(b + 1) * P], flat1[rows, 768:896], ACT.Copy)\
                       .then_inc(pv_read, 1)
                if u < NUNIT:
                    h, b = divmod(u, NT)
                    n, st = (P if b == 0 else T), stat[:, u % 2, :]
                    act.wait_ge(neg_ready, NUNIT + u + 1)
                    if u >= 2:
                        act.wait_ge(pt_done, NUNIT + u - 1)
                    act.activation(p_sb[:, u % 2, 0:n], flat0[u % 2][:, 0:n], ACT.Exp, bias=st[:, 1:2],
                                   scale=SCALE_C, accum_out=st[:, 2:3]).then_inc(s_read, 1)
            out_and_route(1)
            experts(1)
            act.wait_ge(v_taken, 16 * 2 * FIRST_G[1])
            squares(x)
            root()

        @block.vector
        def _(dve):
            steps = [0]

            def note(ins):
                ins.then_inc(dve_step, 1)
                steps[0] += 1

            def settle():
                dve.wait_ge(dve_step, steps[0])

            def step(ins):
                note(ins)
                settle()

            norm = [0]

            def variance(tiles=KD):
                dve.wait_ge(sq_used, SQ[norm[0]] + tiles)
                step(dve.tensor_scalar(halves(rstd[:]), aux[0][:, :, 0:HALF], 1.0 / (P * tiles), EPS,
                                       ALU.mult, ALU.add))
                dve.reciprocal(rstd[:], rstd[:]).then_inc(var_ready, 1)
                norm[0] += 1
                dve.wait_ge(rstd_ready, norm[0])

            def normed(n, s):
                l, row = n // 2, (0, 3)[n % 2]
                for k in range(KD + 1):
                    if k < KD:
                        h = tmp[:, k % 2, :]
                        if k >= 2:
                            dve.wait_ge(lo_ready, KD * s + k - 1)
                        step(dve.tensor_tensor(h, x[:, k, :], rstd[:], ALU.mult))
                        for c, cols in ((0, slice(0, P)), (1, slice(P, T))):
                            ins = dve.tensor_scalar(h[:, cols], h[:, cols], gain[:, n, k, c:c + 1],
                                                    mod[:, l, KD * row + k, c:c + 1], ALU.mult, ALU.add)
                            if c == 0:
                                note(ins)
                        ins.then_inc(h_ready, 1)
                    if k >= 1:
                        dve.wait_ge(hi_ready, KD * s + k)
                        dve.tensor_tensor(a_lo[:, k - 1, :], tmp[:, (k - 1) % 2, :],
                                          a_hi[:, k - 1, :].bitcast(F), ALU.subtract).then_inc(lo_ready, 1)

            def add_to_x(k, l, row, banks, free):
                parts = [(slice(0, P), banks[0][:, 0:P], 0), (slice(P, HALF), banks[0][:, P:HALF], 1),
                         (slice(HALF, T), banks[1][:, 0:HALF], 1)]
                for i, (cols, src, c) in enumerate(parts):
                    ins = dve.scalar_tensor_tensor(x[:, k, cols], src, mod[:, l, KD * row + k, c:c + 1],
                                                   x[:, k, cols], ALU.mult, ALU.add)
                    if i < 2:
                        note(ins)
                ins.then_inc(free, 1)

            def rotate(i, src, bank, cos_sin, mult_rows=P):
                t = rstd[0:mult_rows, 0:NL_TOK]
                dve.wait_ge(rope_done, i + 1)
                note(dve.tensor_tensor(t, bank, cos_sin[:, 1, :], ALU.mult))
                step(dve.tensor_tensor(src, src, cos_sin[:, 0, :], ALU.mult))
                dve.tensor_tensor(src, src, t, ALU.add).then_inc(rope_applied, 1)
                dve.wait_ge(rope_applied, i + 1)

            def modulate(w, out):
                for c in range(2):
                    ins = dve.tensor_tensor_reduce(out=unread[:], in0=w, in1=c_all[:, c, :],
                                                   scale=1.0, scalar=0.0, op0=ALU.mult, op1=ALU.add,
                                                   accum_out=out[:, c:c + 1])
                    if c == 0:
                        step(ins)
                ins.then_inc(mod_used, 1)

            def add_bias(l, first=0, past=48):
                step(dve.tensor_tensor(mod[:, l, first:past], mod[:, l, first:past],
                                       b_mod[:, l, first:past].unsqueeze(2).to_broadcast([P, past - first, 2]),
                                       ALU.add))

            dve.wait_ge(silu_ready, 1)
            for k in range(FIRST_MOD):
                dve.wait_ge(mod_in[k % 8], 16 * (k // 8 + 1))
                modulate(w_mod[:, k % 8, :], mod[:, 0, k, :])
                dve.wait_ge(mod_used, k + 1)
            dve.wait_ge(const_in, 16 * N_CONST)
            add_bias(0, 0, FIRST_MOD)

            def gains(n):
                row = (1, 4)[n % 2]
                step(dve.scalar_tensor_tensor(gain[:, n], mod[:, n // 2, KD * row:KD * row + KD, :], 1.0,
                                              g_norm[:, n, :].unsqueeze(2).to_broadcast([P, KD, 2]),
                                              ALU.add, ALU.mult))

            gains(0)

            variance()
            normed(0, 0)
            step(dve.memset(u_pad[:], 0.0))
            dve.wait_ge(lo_ready, KD)

            tile = FIRST_MOD

            def modulate_b(tiles):
                for k in tiles:
                    dve.wait_ge(mod_b_in[k % 2], 16 * ((k - FIRST_MOD) // 2 + 1))
                    modulate(w_mod_b[:, k % 2, :], mod[:, 0, k, :])
                    dve.wait_ge(mod_used, k + 1)

            modulate_b(range(tile, tile + MOD_BEFORE_ROPE))
            tile += MOD_BEFORE_ROPE
            for i in range(5):
                rotate(i, y[:, 4 + i, NP_TOK:T] if i < 4 else kT[:, 2 * P:6 * P], aux[1][:, i % 2, :], rope)
            for j in range(4):
                modulate_b(range(tile, tile + MOD_BEFORE_CONV[j]))
                tile += MOD_BEFORE_CONV[j]
                m = IN[0] + 8 + 3 * j
                dve.wait_ge(made, m + 1)
                has_taken(dve, m - 1)
                bank = acc[m % 2]
                note(dve.tensor_tensor(u_pad[:, 1:129], bank[:, 0, 0:P], gate_c[:, 0:P], ALU.mult))
                note(dve.tensor_tensor(u_pad[:, 131:323], bank[:, 0, P:HALF], gate_c[:, P:HALF], ALU.mult))
                dve.tensor_tensor(u_pad[:, 323:643], bank[:, 1, 0:HALF], gate_c[:, HALF:T], ALU.mult)\
                   .then_inc(taken[m % 2], 1)
                has_taken(dve, m)
                step(dve.tensor_scalar(conv[:], u_pad[:, 0:642], conv_w[:, j, 0:1], None, ALU.mult))
                for w in (1, 2):
                    step(dve.scalar_tensor_tensor(conv[:], u_pad[:, w:w + 642], conv_w[:, j, w:w + 1], conv[:],
                                                  ALU.mult, ALU.add))
                has_taken(dve, m - 2)
                note(dve.tensor_tensor(y[:, j, 0:P], y[:, j, 0:P], conv[:, 0:P], ALU.mult))
                dve.tensor_tensor(y[:, j, P:T], y[:, j, P:T], conv[:, 130:642], ALU.mult).then_inc(conv_ready, 1)
                dve.wait_ge(conv_ready, j + 1)
            add_bias(0, FIRST_MOD, 48)
            for u in range(NUNIT + 3):
                if u >= 3:
                    v = u - 3
                    n, st = keys_of(UNITS0[v][2]), stat[:, v % 4, :]
                    dve.wait_ge(e_ready, v + 1)
                    step(dve.tensor_tensor(st[:, 4:5], st[:, 2:3], st[:, 3:4], ALU.add))
                    step(dve.reciprocal(st[:, 5:6], st[:, 4:5]))
                    dve.tensor_scalar(s_sb[:, v % 4, 0:n], s_sb[:, v % 4, 0:n], st[:, 5:6], None, ALU.mult)\
                       .then_inc(p_ready, 1)
                if u < NUNIT:
                    j, s, b = UNITS0[u]
                    n, st, hd = keys_of(b), stat[:, u % 4, :], 4 * s + j
                    dve.wait_ge(s_done, u + 1)
                    if u >= 4:
                        dve.wait_ge(pt_done, u - 3)
                    ins = dve.tensor_scalar(s_sb[:, u % 4, 0:P], s_bank(u)[:, 0:P], SCALE_B, None, ALU.mult)
                    if b > 0:
                        note(ins)
                        skip = P * (local(b)[0] - b)
                        ins = dve.scalar_tensor_tensor(s_sb[:, u % 4, P:n], s_bank(u)[:, P:n], SCALE_B,
                                                       mask[:, skip:skip + n - P], ALU.mult, ALU.add)
                    ins.then_inc(s_read, 1)
                    dve.wait_ge(s_read, u + 1)
                    step(dve.reduce_max(st[:, 0:1], s_sb[:, u % 4, 0:n], AX.X))
                    dve.tensor_scalar(st[:, 1:2], st[:, 0:1], sink[:, hd:hd + 1], -1.0, ALU.max, ALU.mult)\
                       .then_inc(neg_ready, 1)

            def out_and_route(l):
                s = 1 + 3 * l
                gains(2 * l + 1)
                for k in range(KD):
                    dve.wait_ge(hi_ready, KD * s + k + 1)
                    dve.tensor_tensor(a_lo[:, k, :], y[:, k, :], a_hi[:, k, :].bitcast(F), ALU.subtract)\
                       .then_inc(lo_ready, 1)
                for k in range(KD):
                    m = OUT[l] + k
                    dve.wait_ge(made, m + 1)
                    add_to_x(k, l, 2, (acc[m % 2][:, 0, :], acc[m % 2][:, 1, :]), taken[m % 2])
                variance()
                normed(2 * l + 1, s + 1)
                for i in range(16):
                    n = 16 * l + i
                    dve.wait_ge(sc_done, n + 1)
                    note(dve.tensor_copy(scores[:, 0:4, i, :],
                                         aux[n % 2][:, 0, :].rearrange("p (t k) -> p t k", t=4)))
                    dve.tensor_copy(scores[:, 4, i, :], aux[n % 2][:, 1, 0:P]).then_inc(sc_read, 1)
                dve.wait_ge(sc_read, 16 * (l + 1))

            def top16(heads, values, indices, data):
                for half in range(2):
                    r = slice(8 * half, 8 * half + 8)
                    for h in range(heads):
                        note(dve.max(values[:, h, r], data(h)))
                    settle()
                    for h in range(heads):
                        note(dve.max_index(indices[:, h, r], values[:, h, r], data(h)))
                    settle()
                    if half == 0:
                        for h in range(heads):
                            note(dve.match_replace(data(h), values[:, h, r], data(h), NEG))
                        settle()

            def route(l):
                four = [P, NH, 16, 16]
                for t in range(NT):
                    top16(16, top_v, top_i, lambda h: scores[:, t, h, :])
                    step(dve.tensor_copy(top_f[:], top_i[:]))
                    side = [v[:].rearrange("p (h s) k -> p h s k", s=2) for v in (top_v, top_f)]
                    step(dve.tensor_tensor(cand[:], side[0][:, :, 0, :].unsqueeze(3).to_broadcast(four),
                                           side[0][:, :, 1, :].unsqueeze(2).to_broadcast(four), ALU.add))
                    top16(NH, best, place, lambda h: cand[:, h].rearrange("p i j -> p (i j)"))
                    for s, (amount, op) in enumerate(((4, ALU.logical_shift_right), (15, ALU.bitwise_and))):
                        step(dve.tensor_scalar(part_i[:], place[:], amount, None, op))
                        step(dve.tensor_copy(part_f[:], part_i[:]))
                        step(dve.tensor_tensor(cand[:], part_f[:].unsqueeze(3).to_broadcast(four),
                                               iota[:, 0:16].unsqueeze(1).unsqueeze(1).to_broadcast(four),
                                               ALU.is_equal))
                        step(dve.tensor_tensor(cand[:], cand[:],
                                               side[1][:, :, s, :].unsqueeze(2).to_broadcast(four), ALU.mult))
                        step(dve.tensor_reduce(picks[:, s, t, :].rearrange("p (h k) -> p h k", h=NH), cand[:],
                                               AX.X, ALU.add))
                    gate = picks[:, 2, t, :].rearrange("p (h k) -> p h k", h=NH)
                    ins = dve.tensor_tensor(gate, best[:], best[:, :, 0:1].to_broadcast([P, NH, 16]),
                                            ALU.subtract)
                    if t < NT - 1:
                        step(ins)
                ins.then_inc(shifted, 1)
                dve.wait_ge(exp_done, l + 1)
                every = picks[:, 2, :, :].rearrange("p t (h k) -> p (t h) k", h=NH)
                sums = cand[:].rearrange("p h i j -> p (h i j)")[:, 0:NT * NH]
                step(dve.tensor_reduce(sums, every, AX.X, ALU.add))
                step(dve.reciprocal(sums, sums))
                dve.tensor_tensor(every, every, sums.unsqueeze(2).to_broadcast([P, NT * NH, 16]), ALU.mult)\
                   .then_inc(picks_ready, 1)
                dve.wait_ge(turned_read, 15 * (l + 1))

            def experts(l):
                def one_hots(i):
                    for q in range(32):
                        n = 160 * l + q + 32 * i
                        wait(dve, hot_used, n - 1)
                        for j in range(4):
                            tok = 4 * q + j
                            cell = [picks_t[:, w, bass.ds(P * i + tok, 1)] for w in range(3)]
                            dve.tensor_scalar(one_a[:, tok % 8, :], iota[:], cell[0], cell[2],
                                              ALU.is_equal, ALU.mult)
                            ins = dve.tensor_scalar(one_b[:, tok % 8, :], iota[:], cell[1], None, ALU.is_equal)
                        ins.then_inc(hot_ready, 1)

                one_hots(0)
                with dve.Fori(1, NT) as i:
                    one_hots(i)

                def form(i, k, first=False):
                    n = NKEY * l + k + SPLIT * i
                    dve.wait_ge(ag_in[k % 4], 32 * (32 * l + k // 4 + 1) + 64 * i)
                    wait(dve, p_lo, n - 1)
                    dve.tensor_tensor(p_raw[:, k % 2, :], ag[:, k % 4, 0, :], ag[:, k % 4, 1, :], ALU.mult)\
                       .then_inc(p_made, 1)

                def low_p(i, k):
                    n = NKEY * l + k + SPLIT * i
                    dve.wait_ge(p_hi, n + 1)
                    dve.tensor_tensor(a_lo[:, k, :], p_raw[:, k % 2, :], a_hi[:, k, :].bitcast(F), ALU.subtract)\
                       .then_inc(p_lo, 1)

                def modulate_v(i, s):
                    dve.wait_ge(mod_v_in[s], 16 + 16 * i)
                    w, c_v = w_mod_v[:, s, :], c_all_v
                    dve.wait_ge(silu_ready, 2)
                    for c in range(2):
                        wait(dve, mod_v_sum, 2 * s + c + 6 * i)
                        dve.tensor_tensor_reduce(out=unread[:], in0=w, in1=c_v[:, c, :], scale=1.0, scalar=0.0,
                                                 op0=ALU.mult, op1=ALU.add, accum_out=mod_v[:, s, c:c + 1])\
                           .then_inc(mod_v_sum, 1)
                    dve.wait_ge(mod_v_sum, 2 * s + 2 + 6 * i)
                    dve.tensor_copy(mod[:, 1, bass.ds(3 * i + s, 1), :], mod_v[:, s:s + 1, :])\
                       .then_inc(mod_v_used, 1)

                def sums(i, last=False):
                    for gg in range(2):
                        g = FIRST_G[l] + gg + 2 * i
                        for o in range(16):
                            if l == 0 and (gg, o) in ((0, 7), (0, 15), (1, 7)):
                                modulate_v(i, {(0, 7): 0, (0, 15): 1, (1, 7): 2}[gg, o])
                            if not (last and gg == 1):
                                j, later = o // 4, (i if gg == 0 else i + 1)
                                k = j + (GROUP if gg == 0 else 0)
                                if o % 4 == 0:
                                    form(later, k)
                                if o % 4 == 2:
                                    low_p(later, k)
                            dt, h = o // 2, o % 2
                            bank = acc[(o % 4) // 2][:, o % 2, :]
                            dve.wait_ge(v_done, o + 1 + 16 * g)
                            wait(dve, v_taken, 16 * g - 16 + o + 1)
                            if h == 0:
                                dve.scalar_tensor_tensor(x[:, dt, 0:P], bank[:, 0:P], mod[:, l, 40 + dt, 0:1],
                                                         x[:, dt, 0:P], ALU.mult, ALU.add)
                                cols, src = slice(P, HALF), bank[:, P:HALF]
                            else:
                                cols, src = slice(HALF, T), bank[:, 0:HALF]
                            dve.scalar_tensor_tensor(x[:, dt, cols], src, mod[:, l, 40 + dt, 1:2], x[:, dt, cols],
                                                     ALU.mult, ALU.add).then_inc(v_taken, 1)

                for k in range(GROUP):
                    form(0, k)
                    low_p(0, k)
                sums(0)
                with dve.Fori(1, BODIES - 1) as i:
                    sums(i)
                sums(BODIES - 1, last=True)
                dve.wait_ge(v_taken, 16 * (FIRST_G[l] + 32))
                if l == 0:
                    dve.wait_ge(mod_v_used, 48)

            out_and_route(0)
            route(0)
            experts(0)

            add_bias(1)
            gains(2)
            variance()
            normed(2, 3)
            dve.wait_ge(ss_ready, NT)
            step(dve.tensor_scalar(ss[:, 0:NT], ss[:, 0:NT], 1.0 / 512, EPS, ALU.mult, ALU.add))
            dve.reciprocal(ss[:, 0:NT], ss[:, 0:NT]).then_inc(ss_inv, 1)
            dve.wait_ge(ss_root, 1)
            dve.wait_ge(const1_in, 16 * N_CONST1)
            for t in range(NT):
                dve.scalar_tensor_tensor(vv[:, t, :], vv[:, t, :], ss[:, t:t + 1], g_sgu[:], ALU.mult, ALU.mult)\
                   .then_inc(vv_ready, 1)
            for c in range(2):
                has_taken(dve, IN[1] + 2 + c)
            for t in range(NT):
                dve.wait_ge(mix_done, t + 1)
                part = y[:, 4:8, t * P:(t + 1) * P]
                dve.tensor_tensor(part, part, aux[1][:, t % 2, :].rearrange("p (g t) -> p g t", g=4), ALU.mult)\
                   .then_inc(mix_read, 1)
            for first, tiles, t, hi, lo in ((0, 3, cq, cq_hi, cq_lo), (3, 2, ckv, ckv_hi, ckv_lo)):
                variance(tiles)
                for k in range(tiles):
                    dve.scalar_tensor_tensor(t[:, k, :], t[:, k, :], g_small[:, first + k:first + k + 1], rstd[:],
                                             ALU.mult, ALU.mult).then_inc(lat_norm, 1)
                for k in range(tiles):
                    dve.wait_ge(lat_hi, first + k + 1)
                    parts = [(t[:, k, :], slice(0, T))] if first == 0 else \
                        [(t[:, k, 0:P], slice(0, P)), (ckv_old[:, k, :], slice(P, 2 * P)),
                         (t[:, k, P:T], slice(2 * P, 768))]
                    for n, (src, cols) in enumerate(parts):
                        ins = dve.tensor_tensor(lo[:, k, cols], src, hi[:, k, cols].bitcast(F), ALU.subtract)
                        if n < len(parts) - 1:
                            note(ins)
                    ins.then_inc(lat_lo, 1)
            dve.wait_ge(cache1_in, 16 * 4)
            rotate(5, kr[:, NP_TOK:T], aux[1][0:32, 1, :], kr_rope, 32)
            for i in range(2):
                note(dve.tensor_copy(k_head[64:96, i, 0:P], kr[:, 0:P]))
                ins = dve.tensor_copy(k_head[64:96, i, 2 * P:768], kr[:, P:T])
                if i == 0:
                    note(ins)
            ins.then_inc(kr_ready, 1)
            flat0 = [b[:].rearrange("p a n -> p (a n)") for b in (aux[0], acc[0])]

            def turn_head(h):
                rotate(6 + h, q_head[:, h % 2, NP_TOK:T], acc[1][0:96, 0, :], rope[0:96], 96)

            turn_head(0)
            for u in range(NUNIT + 2):
                if u >= 2:
                    v = u - 2
                    h, b = divmod(v, NT)
                    n, st = (P if b == 0 else T), stat[:, v % 2, :]
                    dve.wait_ge(s_read, NUNIT + v + 1)
                    step(dve.reciprocal(st[:, 5:6], st[:, 2:3]))
                    dve.tensor_scalar(p_sb[:, v % 2, 0:n], p_sb[:, v % 2, 0:n], st[:, 5:6], None, ALU.mult)\
                       .then_inc(p_ready, 1)
                    if h + 1 < NH and b == 1:
                        turn_head(h + 1)
                if u < NUNIT:
                    n, st = (P if u % NT == 0 else T), stat[:, u % 2, :]
                    dve.wait_ge(s_done, NUNIT + u + 1)
                    step(dve.reduce_max(st[:, 0:1], flat0[u % 2][:, 0:n], AX.X))
                    dve.tensor_scalar(st[:, 1:2], st[:, 0:1], -SCALE_C, None, ALU.mult).then_inc(neg_ready, 1)
            out_and_route(1)
            route(1)
            experts(1)
            variance()
            for k in range(KD):
                dve.scalar_tensor_tensor(y[:, k, :], x[:, k, :], g_norm[:, 4, k:k + 1], rstd[:],
                                         ALU.mult, ALU.mult).then_inc(y_ready, 1)


def constants():
    import numpy as np
    f = np.float32
    out = {"ident": np.eye(P, dtype=f), "ones": np.ones((P, P), f),
           "iota": np.tile(np.arange(NKEY, dtype=f), (P, 1))}
    q, k = np.arange(P)[:, None], np.arange(3 * P)[None, :]
    out["mask"] = np.where(np.abs(k - P - q) <= P, 0.0, NEG).astype(f)

    def tables(dr):
        n = dr // 4
        freqs = np.power(f(10000.0), -np.arange(n, dtype=f) / f(n)).astype(f)
        t = np.arange(NL_TOK)
        row, col = (t // 64).astype(f), (t % 64).astype(f)
        ang = np.concatenate([row[:, None] * freqs, col[:, None] * freqs], axis=1).astype(f)
        cos, sin = np.cos(ang).astype(f).T, np.sin(ang).astype(f).T
        return np.concatenate([cos, cos]), np.concatenate([-sin, sin])

    def swap(dr):
        return np.roll(np.eye(dr, dtype=f), dr // 2, axis=0)

    cos, sin = tables(64)
    out["rope0"] = np.stack([np.tile(cos, (2, 1)), np.tile(sin, (2, 1))], axis=1)
    out["perm0"] = np.kron(np.eye(2, dtype=f), swap(64))
    cos, sin = tables(32)
    rope1, perm1 = np.zeros((P, 2, NL_TOK), f), np.zeros((P, P), f)
    rope1[0:64, 0] = 1.0
    rope1[64:96, 0], rope1[64:96, 1] = cos, sin
    perm1[64:96, 64:96] = swap(32)
    perm1[0:32, 96:128] = swap(32)
    out["rope1"], out["perm1"] = rope1, perm1
    out["rope_k"] = np.stack([cos, sin], axis=1)
    return {n: np.ascontiguousarray(v, dtype=f) for n, v in out.items()}


def layout(i):
    import numpy as np

    def chunks(w, n=None):
        k, m = w.shape[0] // P, w.shape[1] // P
        return w.reshape(k, P, m, P).transpose(2, 1, 0, 3).reshape(m, P, k * P)

    def columns(v):
        return v.reshape(-1, P).T

    def features(t):
        return t.T.reshape(t.shape[1] // P, P, t.shape[0]).transpose(1, 0, 2)

    o = {}
    o["x"] = features(np.concatenate([i["x_prompt"][0], i["x_sample"][0]]))
    o["c_all"] = np.broadcast_to(np.stack([i["c_ctx"], i["c"][0]]), (P, 2, D))
    o["w_mod"] = i["w_mod"].transpose(0, 2, 1).reshape(2, 48, P, D)
    o["b_mod"] = i["b_mod"].reshape(2, 48, P).transpose(2, 0, 1)
    norms = [i["g_norm1"][0], i["g_norm2"][0], i["g_norm1"][1], i["g_norm2"][1], i["g_final"]]
    o["g_norm"] = np.stack([columns(g) for g in norms], axis=1)
    o["sink"] = np.broadcast_to(i["ev_sink"][0], (P, NH))
    o["conv_w"] = i["ev_conv_w"][0].reshape(3, 4, P).transpose(2, 1, 0)
    o["g_small"] = np.concatenate([columns(i["od_g_qnorm"][0]), columns(i["od_g_kvnorm"][0])], axis=1)
    w = i["ev_w_in"][0]
    heads = [np.concatenate([w[:, 1536 + 64 * h:1600 + 64 * h] for h in (j, 4 + j)], axis=1) for j in range(4)]
    conv = [w[:, 512 * s + P * j:512 * s + P * j + P] for j in range(4) for s in range(3)]
    o["in0"] = chunks(np.concatenate(heads + [w[:, 2048:2304]] + conv, axis=1))
    w = i["ev_w_out"][0]
    rows = [w[512 + 64 * h:576 + 64 * h] for j in range(4) for h in (j, 4 + j)]
    o["out0"] = chunks(np.concatenate([w[0:512]] + rows))
    o["cache_k"] = i["cache_attn_k"][0, 0].reshape(P, P).T
    o["cache_v"] = i["cache_attn_v"][0, 0].reshape(P, P)
    w = i["od_w_in"][0]
    o["in1"] = chunks(np.concatenate([w[:, 1184:1696], w[:, 672:1184], w[:, 0:640], w[:, 640:768]], axis=1))
    uq, ukv = i["od_w_uq"][0], i["od_w_ukv"][0]
    q = uq.reshape(3, P, NH, 96).transpose(2, 1, 0, 3).reshape(NH, P, 288)
    kv = ukv.reshape(2, P, NH, P).transpose(2, 1, 0, 3).reshape(NH, P, 256)
    o["head"] = np.concatenate([q, kv], axis=2)
    o["ukv_v"] = ukv.reshape(2, P, NH, 2, 64)[:, :, :, 1].transpose(1, 0, 2, 3).reshape(P, 1024)
    o["out1"] = chunks(i["od_w_out"][0])
    o["cache_ckv"] = features(i["cache_mla_ckv"][0, 0])
    o["cache_kr"] = i["cache_mla_krope"][0, 0].T
    o["ws_t"] = i["od_w_spatial"][0].transpose(2, 0, 1)
    o["b_s"] = i["od_b_spatial"]
    o["g_sgu"] = np.broadcast_to(i["od_g_sgu"][0], (P, 512))
    o["wq"] = np.stack([chunks(i["peer_wq"][l]) for l in range(2)])
    o["subk"] = i["peer_subkeys"].reshape(2, 16, NKEY, P).transpose(0, 3, 1, 2)
    u = i["peer_u"].reshape(2, NKEY, NKEY, KD, P)
    o["u"] = u.transpose(0, 2, 4, 3, 1).reshape(2, NKEY, P, 1024)
    o["v"] = i["peer_v"].reshape(2, NKEY, NKEY, D).transpose(0, 2, 1, 3)
    return o


_OUTS = {"y": (P, KD, T), "new_k": (P, P), "new_v": (P, P), "new_ckv": (P, 2, P), "new_kr": (32, P)}


def kernel(**inputs):
    import numpy as _np
    import concourse.bacc as _bacc
    from concourse import mybir as _mybir
    from concourse.bass_utils import run_bass_kernel_spmd as _run

    f32 = _mybir.dt.float32
    nc = _bacc.Bacc("TRN2", target_bir_lowering=False, num_devices=1)
    arrays, args = {}, {}
    data = layout({n: _np.asarray(v) for n, v in inputs.items()})
    data.update(constants())
    for name, v in data.items():
        v = _np.ascontiguousarray(v)
        arrays[f"in_{name}"] = v
        args[name] = nc.dram_tensor(f"in_{name}", v.shape, _mybir.dt.from_np(v.dtype), kind="ExternalInput").ap()
    for name, shape in _OUTS.items():
        args[name] = nc.dram_tensor(f"out_{name}", shape, f32, kind="ExternalOutput").ap()
    for name in ("act_s", "gate_s"):
        args[name] = nc.dram_tensor(name, (2, NKEY, P, T), f32, kind="Internal").ap()
    build(nc, args)
    r = _run(nc, [arrays], core_ids=[0]).results[0]
    y = r["out_y"].transpose(2, 1, 0).reshape(T, D)
    new_ckv = r["out_new_ckv"].transpose(2, 1, 0).reshape(1, 1, NP_TOK, 256)
    return (_np.ascontiguousarray(y[None, 0:NP_TOK]), _np.ascontiguousarray(y[None, NP_TOK:T]),
            _np.ascontiguousarray(r["out_new_k"].T).reshape(1, 1, NP_TOK, 2, 64),
            _np.ascontiguousarray(r["out_new_v"]).reshape(1, 1, NP_TOK, 2, 64),
            _np.ascontiguousarray(new_ckv), _np.ascontiguousarray(r["out_new_kr"].T).reshape(1, 1, NP_TOK, 32))
```

```python
import concourse.bass as bass
from concourse import mybir
from contextlib import ExitStack

P = 128
D, KD = 1024, 8
NP_TOK, NL_TOK = 128, 512
T, NT = 640, 5
HALF = 320
NKEY, PICKS = 128, 128
NH = 8
EPS = 1e-6
SCALE_B, SCALE_C = 64.0 ** -0.5, 96.0 ** -0.5
RAW, SPLIT = 2, 8
GROUP = 4
NEG = -1.0e30


def plan():
    chunks, products = [], []

    def add(layer, kind, n, made=1, size=1024, together=False):
        first = len(products)
        for i in range(n):
            if not together:
                first = len(products)
            if not together or i == n - 1:
                products.extend([(layer, kind, i, j, len(chunks)) for j in range(made)])
            chunks.append((layer, kind, i, size, first, first + made))

    add(0, "in", 18)
    add(0, "out", 8)
    add(0, "wq", 16)
    add(0, "u", 128)
    add(0, "v", 128, made=0)
    add(1, "dzv", 4, made=3, together=True)
    add(1, "in", 10)
    add(1, "ukv_v", 1, made=3)
    add(1, "head", 8, made=2, size=3 * 96 + 2 * 128)
    add(1, "out", 8)
    add(1, "wq", 16)
    add(1, "u", 128)
    add(1, "v", 128, made=0)
    return chunks, products


CHUNKS, PRODUCTS = plan()


def chunk_at(layer, kind):
    return next(n for n, c in enumerate(CHUNKS) if c[0] == layer and c[1] == kind)


def product_at(layer, kind):
    return next(n for n, c in enumerate(PRODUCTS) if c[0] == layer and c[1] == kind)


def build(nc, a):
    F, R, U32, BF = mybir.dt.float32, mybir.dt.float32r, mybir.dt.uint32, mybir.dt.bfloat16
    ALU, ACT, AX = mybir.AluOpType, mybir.ActivationFunctionType, mybir.AxisListType
    ctx = ExitStack()
    with ctx:
        slab_bytes = 212 * 1024 - 4480
        slab = ctx.enter_context(nc.sbuf_tensor("slab", [P, slab_bytes // 4], F))
        base = nc.sbuf_base - slab_bytes
        end = [base]

        def at(name, shape, off, dt=F):
            return nc.alloc_sbuf_tensor_at(name, shape, dt, offset=off)

        def sb(name, shape, dt=F):
            size = 4
            for n in shape[1:]:
                size *= n
            if dt == BF:
                size //= 2
            off = end[0]
            end[0] += (size + 31) // 32 * 32
            return at(name, shape, off, dt)

        def sem(name):
            return ctx.enter_context(nc.semaphore(name))

        x = sb("x", [P, KD, T])
        act_at = end[0]
        a_hi = sb("a_hi", [P, KD, T], R)
        a_lo = sb("a_lo", [P, KD, T], R)
        raw = sb("raw", [P, RAW, 1024])
        w_hi = sb("w_hi", [P, SPLIT, 1024], R)
        w_lo = sb("w_lo", [P, SPLIT, 1024], R)
        ident = sb("ident", [P, P])
        ones = sb("ones", [P, P])
        iota = sb("iota", [P, P])
        iota_b = sb("iota_b", [P, P], BF)
        mask = sb("mask", [P, 384])
        perm = sb("perm", [P, P])
        rope = sb("rope", [P, 2, NL_TOK])
        mod = sb("mod", [P, 2, 48, 2])
        b_mod = sb("b_mod", [P, 2, 48])
        g_norm = sb("g_norm", [P, 5, KD])
        gain = sb("gain", [P, 4, KD, 2])
        mod_v = sb("mod_v", [P, 3, 2])
        sink = sb("sink", [P, NH])
        conv_w = sb("conv_w", [P, 4, 3])
        g_small = sb("g_small", [P, 5])
        stat = sb("stat", [P, 4, 8])
        ss = sb("ss", [P, 8])
        c_cols = sb("c_cols", [P, KD, 2])
        tmp_at = end[0]
        tmp = sb("tmp", [P, 2, T])
        rstd = sb("rstd", [P, T])
        picks = at("picks", [P, 3, NT, PICKS], tmp_at)
        a_out_at = end[0]
        a_out = sb("a_out", [P, 2, T])
        work = end[0]
        room = base + slab_bytes - work
        assert room >= 54304, room

        y = at("y", [P, KD, T], work)
        kT = at("kT", [P, 768], work + 20480)
        vt = at("vt", [P, 6, P], work + 23552)
        u_pad = at("u_pad", [P, 648], work + 26624)
        gate_c = at("gate_c", [P, T], work + 29216)
        conv = at("conv", [P, 642], work + 31776)
        s_sb = at("s_sb", [P, 4, 512], work + 36416)
        pt_sb = at("pt_sb", [P, 2, 512], work + 44608)
        vv = at("vv", [P, NT, 512], work + 20480)
        vt1 = at("vt1", [P, 6, 512], work + 20480)
        cq = at("cq", [P, 3, T], work + 32768)
        ckv = at("ckv", [P, 2, T], work + 40448)
        ckv_old = at("ckv_old", [P, 2, P], work + 45568)
        kr = at("kr", [32, T], work + 46592)
        kr_rope = at("kr_rope", [32, 2, NL_TOK], work + 49152)
        p_sb = at("p_sb", [P, 2, T], work + 46592)
        pt1 = at("pt1", [P, T], work + 51712)
        ws_t = at("ws_t", [P, 4, P], work)
        b_s = at("b_s", [1, 4, P], work + 2048)
        g_sgu = at("g_sgu", [P, 512], work + 4096)
        cq_hi = at("cq_hi", [P, 3, T], act_at, R)
        cq_lo = at("cq_lo", [P, 3, T], act_at + 7680, R)
        ckv_hi = at("ckv_hi", [P, 2, 768], act_at + 15360, R)
        ckv_lo = at("ckv_lo", [P, 2, 768], act_at + 21504, R)
        k_head = at("k_head", [96, 2, 768], act_at + 27648)
        q_head = at("q_head", [96, 2, T], act_at + 33792)
        c_all = at("c_all", [P, 2, D], work + 36416)
        w_mod = at("w_mod", [P, 8, D], work)
        w_mod_b = at("w_mod_b", [P, 2, D], work + 44608)
        c_all_v = at("c_all_v", [P, 2, D], work + 37888)
        w_mod_v = at("w_mod_v", [P, 3, D], work + 25600)
        unread = at("unread", [P, D], a_out_at)
        scores = at("scores", [P, NT, 16, NKEY], work)
        subk = at("subk", [P, 16, NKEY], work + 40960)
        cand = at("cand", [P, NH, 16, 16], work + 40960)
        top_v = at("top_v", [P, 16, 16], work + 49152)
        top_i = at("top_i", [P, 16, 16], work + 50176, U32)
        top_f = at("top_f", [P, 16, 16], work + 51200)
        best = at("best", [P, NH, 16], work + 52224)
        place = at("place", [P, NH, 16], work + 52736, U32)
        part_i = at("part_i", [P, NH, 16], work + 53248, U32)
        part_f = at("part_f", [P, NH, 16], work + 53760)
        g_sum = at("g_sum", [P, NH], work + 54272)
        gates = at("gates", [P, NKEY, 64], work)
        one_a = at("one_a", [P, 8, NKEY], work + 32768, BF)
        one_b = at("one_b", [P, 8, 3, NKEY], work + 34816, BF)
        picks_t = at("picks_t", [P, 5, T], work + 40960)
        part_b = at("part_b", [P, T], work + 32768, BF)
        ag = at("ag", [P, 4, 2, T], work)
        p_raw = at("p_raw", [P, 2, T], work + 20480)

        acc = [ctx.enter_context(nc.psum_tensor(f"acc{i}", [P, 2, 512], F)) for i in range(2)]
        aux = [ctx.enter_context(nc.psum_tensor(f"aux{i}", [P, 2, 512], F)) for i in range(2)]

        const_in = sem("const_in")
        const1_in, cache_in, cache1_in = sem("const1_in"), sem("cache_in"), sem("cache1_in")
        raw_in = [sem(f"raw_in{i}") for i in range(RAW)]
        hi_done, lo_done, slot_free = sem("hi_done"), sem("lo_done"), sem("slot_free")
        made = sem("made")
        taken = [sem(f"taken{i}") for i in range(2)]
        mod_in = [sem(f"mod_in{i}") for i in range(8)]
        mod_b_in = [sem(f"mod_b_in{i}") for i in range(2)]
        x_in, ones_in, c_cols_in, c_ready = sem("x_in"), sem("ones_in"), sem("c_cols_in"), sem("c_ready")
        mod_pe_used = sem("mod_pe_used")
        mod_used, silu_ready = sem("mod_used"), sem("silu_ready")
        mod_v_in = [sem(f"mod_v_in{i}") for i in range(3)]
        mod_v_used, mod_v_sum, c_in = sem("mod_v_used"), sem("mod_v_sum"), sem("c_in")
        dve_step, modulated = sem("dve_step"), sem("modulated")
        sq_ready, sq_used = sem("sq_ready"), sem("sq_used")
        var_ready, rstd_ready = sem("var_ready"), sem("rstd_ready")
        h_ready, hi_ready, lo_ready = sem("h_ready"), sem("hi_ready"), sem("lo_ready")
        rope_done, rope_applied = sem("rope_done"), sem("rope_applied")
        s_done, s_read = sem("s_done"), sem("s_read")
        neg_ready, e_ready, p_ready = sem("neg_ready"), sem("e_ready"), sem("p_ready")
        pt_done, pt_ready, pv_done, pv_read = sem("pt_done"), sem("pt_ready"), sem("pv_done"), sem("pv_read")
        state_out = sem("state_out")
        mix_done, mix_read, vv_ready = sem("mix_done"), sem("mix_read"), sem("vv_ready")
        conv_ready, ss_ready, ss_inv, ss_root = sem("conv_ready"), sem("ss_ready"), sem("ss_inv"), sem("ss_root")
        lat_norm, lat_hi, lat_lo, kr_ready = sem("lat_norm"), sem("lat_hi"), sem("lat_lo"), sem("kr_ready")
        sc_done, sc_read = sem("sc_done"), sem("sc_read")
        subk_in = sem("subk_in")
        shifted, exp_done, picks_ready = sem("shifted"), sem("exp_done"), sem("picks_ready")
        turned, turned_read = sem("turned"), sem("turned_read")
        hot_ready, hot_used, gate_read = sem("hot_ready"), sem("hot_used"), sem("gate_read")
        gates_out = sem("gates_out")
        a_st = [sem(f"a_stored{i}") for i in range(4)]
        ag_in = [sem(f"ag_in{i}") for i in range(4)]
        p_made, p_hi, p_lo = sem("p_made"), sem("p_hi"), sem("p_lo")
        v_done, v_taken = sem("v_done"), sem("v_taken")
        y_ready, y_out = sem("y_ready"), sem("y_out")
        block = ctx.enter_context(nc.Block())

        N_CONST, N_CONST1 = 10, 5
        BY_DVE = 10
        FIRST_MOD = 16
        MOD_BESIDE = {1: 2, **{n: 3 for n in range(8, 12)}, **{n: 2 for n in range(12, 21)}}
        MOD_BEFORE_ROPE, MOD_BEFORE_CONV = 14, (6, 4, 4, 4)
        EARLY = 5
        BRIDGE = 1
        BUILT = (1, 1, 1, 1, 3, 3, 3, 3)
        COPIED = (0, 0, 0, 4, 3, 3, 3, 3)
        OUT = {l: product_at(l, "out") for l in range(2)}
        WQ = {l: product_at(l, "wq") for l in range(2)}
        UM = {l: product_at(l, "u") for l in range(2)}
        IN = {l: product_at(l, "in") for l in range(2)}
        DZV = product_at(1, "dzv")
        UKV, HEAD = product_at(1, "ukv_v"), product_at(1, "head")
        UC = {l: chunk_at(l, "u") for l in range(2)}
        VC = {l: chunk_at(l, "v") for l in range(2)}
        PIECES = 4
        A_EARLY = EARLY * SPLIT // 2
        A_LATE = (NKEY - EARLY * SPLIT) // 4
        A_ALL = (A_EARLY + A_LATE, A_EARLY + A_LATE, A_LATE, A_LATE)
        BODIES = NKEY // SPLIT
        NUNIT = NT * NH
        FIRST_G = {0: 0, 1: NKEY // GROUP}

        SQ = [0, 8, 16, 24, 27, 29, 37]
        MIXED_AT = [3, 5, 7, 9] + [2 * NT * (j + 1) + 4 for j in range(3)]
        UNITS0 = [(j, s, b) for j in range(4) for s in range(2) for b in range(NT)]

        def local(b):
            lo, hi = max(1, b - 1), min(4, b + 1)
            return lo + 1, hi - lo + 1

        def key_tiles(b):
            return [1] if b == 0 else [0] + [local(b)[0] + c for c in range(local(b)[1])]

        def s_bank(u):
            return (aux[0][:, 0, :], aux[0][:, 1, :], acc[0][:, 0, :])[u % 3]

        def keys_of(b):
            return P if b == 0 else P + local(b)[1] * P

        def halves(t):
            return t.rearrange("p (h t) -> p h t", h=2)

        def wait(eng, s, value):
            if not isinstance(value, int) or value > 0:
                eng.wait_ge(s, value)

        def has_taken(eng, m):
            eng.wait_ge(taken[m % 2], m // 2 + 1)

        def source(n):
            layer, kind, i, size = CHUNKS[n][:4]
            if kind in ("u", "v"):
                return a[kind][layer, i]
            if kind == "wq":
                return a["wq"][layer, i]
            if kind == "head":
                return a["head"][i]
            if kind == "dzv":
                return a["in1"][i]
            if kind == "in" and layer == 1:
                return a["in1"][4 + i]
            if kind == "ukv_v":
                return a["ukv_v"]
            return a[f"{kind}{layer}"][i]

        @block.sync
        def _(sp):
            def load_chunk(n):
                if n >= RAW:
                    sp.wait_ge(lo_done, n - RAW + 1)
                sp.dma_start(raw[:, n % RAW, 0:CHUNKS[n][3]], source(n)).then_inc(raw_in[n % RAW], 16)

            for n in range(RAW):
                load_chunk(n)
            for n in range(BY_DVE):
                if n >= 5:
                    sp.wait_ge(mod_used, n - 4)
                sp.dma_start(w_mod[:, n % 5], a["w_mod"][0, n]).then_inc(mod_in[n % 5], 16)
                if n < FIRST_MOD - BY_DVE:
                    if n >= 3:
                        sp.wait_ge(mod_pe_used, n - 2)
                    sp.dma_start(w_mod[:, 5 + n % 3], a["w_mod0"][n]).then_inc(mod_in[5 + n % 3], 16)

            for l in range(2):
                tile = FIRST_MOD
                for n in range(0 if l else RAW - 1, len(CHUNKS)):
                    if CHUNKS[n][0] == l and CHUNKS[n][1] not in ("u", "v"):
                        if l or n >= RAW:
                            load_chunk(n)
                        if l == 0:
                            for k in range(tile, tile + MOD_BESIDE.get(n, 0)):
                                if k >= FIRST_MOD + 2:
                                    sp.wait_ge(mod_used, k - 1 - (FIRST_MOD - BY_DVE))
                                sp.dma_start(w_mod_b[:, k % 2], a["w_mod"][0, k]).then_inc(mod_b_in[k % 2], 16)
                            tile += MOD_BESIDE.get(n, 0)
                with sp.Fori(0, BODIES) as i:
                    for u in range(SPLIT):
                        n = UC[l] + SPLIT * i + u
                        sp.wait_ge(lo_done, n - RAW + 1)
                        sp.dma_start(raw[:, (UC[l] + u) % RAW],
                                     a["u"][l, bass.ds(SPLIT * i + u, 1)].rearrange("o p n -> (o p) n"))\
                          .then_inc(raw_in[(UC[l] + u) % RAW], 16)
                def load_raw(c, u):
                    sp.wait_ge(lo_done, VC[l] + c - RAW + 1)
                    sp.dma_start(raw[:, (VC[l] + u) % RAW], a["v"][l, bass.ds(c, 1)].rearrange("o p n -> (o p) n"))\
                      .then_inc(raw_in[(VC[l] + u) % RAW], 16)

                def load_ag(c, u):
                    if not (isinstance(c, int) and c < 4):
                        sp.wait_ge(p_made, NKEY * l + c - 3)
                    for w, src in enumerate((a["act_s"], a["gate_s"])):
                        sp.dma_start(ag[:, u % 4, w], src[l, bass.ds(c, 1)].rearrange("o p n -> (o p) n"))\
                          .then_inc(ag_in[u % 4], 16)

                for u in range(GROUP):
                    load_raw(u, u)
                sp.wait_ge(gates_out, 16 * PIECES * 10 * (l + 1))
                for s in range(2):
                    sp.wait_ge(a_st[s], 16 * (A_ALL[s] * l + SPLIT // 2))
                for u in range(GROUP):
                    load_ag(u, u)
                for u in range(GROUP, SPLIT):
                    load_raw(u, u)
                for u in range(GROUP, SPLIT):
                    load_ag(u, u)
                for s in range(4):
                    sp.wait_ge(a_st[s], 16 * A_ALL[s] * (l + 1))
                if l == 0:
                    for u in range(3):
                        sp.dma_start(w_mod_v[:, u], a["w_mod"][1, u]).then_inc(mod_v_in[u], 16)
                with sp.Fori(1, BODIES) as i:
                    for u in range(SPLIT):
                        load_raw(u + SPLIT * i, u)
                        load_ag(u + SPLIT * i, u)
                        if l == 0 and u < 3:
                            sp.wait_ge(mod_v_used, u + 1 - 3 + 3 * i)
                            sp.dma_start(w_mod_v[:, u], a["w_mod"][1, bass.ds(u + 3 * i, 1)]
                                         .rearrange("o p n -> (o p) n")).then_inc(mod_v_in[u], 16)
            for k in range(KD):
                sp.wait_ge(y_ready, k + 1)
                sp.dma_start(a["y"][:, k, :], y[:, k, :]).then_inc(y_out, 16)
            sp.wait_ge(y_out, 16 * KD)
            sp.wait_ge(state_out, 16 * 4)

        @block.gpsimd
        def _(pool):
            def low(n, slot, rslot, size):
                pool.wait_ge(hi_done, n + 1)
                pool.tensor_tensor(w_lo[:, slot, 0:size], raw[:, rslot, 0:size],
                                   w_hi[:, slot, 0:size].bitcast(F), ALU.subtract).then_inc(lo_done, 1)

            def last_use(n):
                layer, kind, i, size, first, past = CHUNKS[n]
                if kind == "v":
                    return v_done, 16 * (FIRST_G[layer] + i // GROUP + 1)
                return made, past

            def split_chunk(n):
                slot, rslot, size = n % SPLIT, n % RAW, CHUNKS[n][3]
                pool.wait_ge(raw_in[rslot], 16 * (n // RAW + 1))
                if n >= SPLIT:
                    pool.wait_ge(*last_use(n - SPLIT))
                pool.tensor_copy(w_hi[:, slot, 0:size], raw[:, rslot, 0:size]).then_inc(hi_done, 1)
                low(n, slot, rslot, size)

            def split_loop(first, free_sem, free_base, per_body, free_steps, start):
                with pool.Fori(start, BODIES) as i:
                    for u in range(SPLIT):
                        n0 = first + u
                        pool.wait_ge(raw_in[n0 % RAW], 16 * (n0 // RAW + 1) + 16 * (SPLIT // RAW) * i)
                        pool.wait_ge(free_sem, free_base + free_steps[u] + per_body * i)
                        pool.sem_inc(slot_free, 1)
                        pool.tensor_copy(w_hi[:, n0 % SPLIT, :], raw[:, n0 % RAW, :]).then_inc(hi_done, 1)
                        low(n0 + SPLIT * i, n0 % SPLIT, n0 % RAW, 1024)

            for l in range(2):
                for n in range(len(CHUNKS)):
                    if CHUNKS[n][0] == l and CHUNKS[n][1] not in ("u", "v"):
                        split_chunk(n)
                split_loop(UC[l], made, UM[l] - SPLIT, SPLIT, [u + 1 for u in range(SPLIT)], 0)
                for u in range(SPLIT):
                    split_chunk(VC[l] + u)
                split_loop(VC[l], v_done, 16 * FIRST_G[l], 32,
                           [16 * (u // GROUP) - 16 for u in range(SPLIT)], 1)

        @block.tensor
        def _(pe):
            def begin(m):
                pe.wait_ge(lo_done, PRODUCTS[m][4] + 1)
                if m >= 2:
                    pe.wait_ge(taken[m % 2], m // 2)
                return acc[m % 2], PRODUCTS[m][4] % SPLIT

            def linear_step(out, w, width, k, kt, hi, lo, n, off=0):
                wh = w_hi[:, w, off + k * width:off + (k + 1) * width]
                wl = w_lo[:, w, off + k * width:off + (k + 1) * width]
                pe.matmul(out, wh, hi[:, k, n], start=(k == 0), stop=False)
                pe.matmul(out, wh, lo[:, k, n], start=False, stop=False)
                return pe.matmul(out, wl, hi[:, k, n], start=False, stop=(k == kt - 1))

            def linear(out, w, width, kt, hi, lo, n, off=0):
                for k in range(kt):
                    mm = linear_step(out, w, width, k, kt, hi, lo, n, off)
                return mm

            def by_feature(m, width=P, kt=KD, hi=a_hi, lo=a_lo, cols=HALF, off=0):
                bank, w = begin(m)
                for h in range(2):
                    mm = linear(bank[0:width, h, 0:cols], w, width, kt, hi, lo,
                                slice(h * cols, (h + 1) * cols), off)
                mm.then_inc(made, 1)

            def by_feature_pair(m, ready):
                pair = [begin(m), begin(m + 1)]
                for k in range(KD):
                    pe.wait_ge(lo_ready, ready + k + 1)
                    for bank, w in pair:
                        for h in range(2):
                            mm = linear_step(bank[:, h, 0:HALF], w, P, k, KD, a_hi, a_lo,
                                             slice(h * HALF, (h + 1) * HALF))
                        if k == KD - 1:
                            mm.then_inc(made, 1)

            def by_token(m, tiles, width, kt=KD, hi=a_hi, lo=a_lo, weights=None, ready=None):
                bank, w = begin(m)
                flat = bank[:].rearrange("p a n -> p (a n)")
                weights = weights or (lambda t, k: t[:, w, k * width:(k + 1) * width])
                order = [(j, k) for j in range(len(tiles)) for k in range(kt)]
                if ready is not None:
                    order.sort(key=lambda jk: jk[1])
                for j, k in order:
                    if ready is not None and j == 0:
                        pe.wait_ge(lo_ready, ready + k + 1)
                    n = slice(tiles[j] * P, tiles[j] * P + P)
                    out = flat[:, j * width:(j + 1) * width]
                    pe.matmul(out, hi[:, k, n], weights(w_hi, k), start=(k == 0), stop=False)
                    pe.matmul(out, lo[:, k, n], weights(w_hi, k), start=False, stop=False)
                    mm = pe.matmul(out, hi[:, k, n], weights(w_lo, k), start=False, stop=(k == kt - 1))
                mm.then_inc(made, 1)

            norms = [0]

            def norm_sum(k, tiles=KD):
                i = norms[0]
                if k == 0 and i:
                    pe.wait_ge(var_ready, i)
                q = SQ[i] + k
                pe.wait_ge(sq_ready, q + 1)
                for h in range(2):
                    mm = pe.matmul(aux[0][:, h, 0:HALF], ones[:], tmp[:, q % 2, h * HALF:(h + 1) * HALF],
                                   start=(k == 0), stop=(k == tiles - 1), skip_group_check=True)
                mm.then_inc(sq_used, 1)
                if k == tiles - 1:
                    norms[0] += 1

            def norm_sums(tiles=KD):
                for k in range(tiles):
                    norm_sum(k, tiles)

            def rope_turn(i, m, src, rows=P):
                has_taken(pe, m)
                if i >= 2:
                    pe.wait_ge(rope_applied, i - 1)
                pe.matmul(aux[1][0:rows, i % 2, :], perm[0:rows, 0:rows], src, start=True, stop=True)\
                  .then_inc(rope_done, 1)

            def scores_of(u):
                j, s, b = UNITS0[u]
                rows = slice(64 * s, 64 * s + 64)
                if u >= 3:
                    pe.wait_ge(s_read, u - 2)
                q = y[rows, 4 + j, b * P:(b + 1) * P]
                bank = s_bank(u)
                if b == 0:
                    pe.matmul(bank[:, 0:P], q, kT[rows, P:2 * P], start=True, stop=True).then_inc(s_done, 1)
                else:
                    lo, n = local(b)
                    pe.matmul(bank[:, 0:P], q, kT[rows, 0:P], start=True, stop=True)
                    pe.matmul(bank[:, P:P + n * P], q, kT[rows, lo * P:(lo + n) * P], start=True, stop=True)\
                      .then_inc(s_done, 1)

            pe.wait_ge(ones_in, 16)
            pe.wait_ge(c_ready, 1)
            for k in range(KD):
                norm_sum(k)
                if k < FIRST_MOD - BY_DVE:
                    pe.wait_ge(mod_in[5 + k % 3], 16 * (k // 3 + 1))
                    for kt in range(KD):
                        mm = pe.matmul(aux[1][:, 0, 2 * k:2 * k + 2], w_mod[:, 5 + k % 3, kt * P:(kt + 1) * P],
                                       c_cols[:, kt, :], start=(kt == 0), stop=(kt == KD - 1))
                    mm.then_inc(mod_pe_used, 1)
            by_feature_pair(IN[0], 0)
            for m in range(IN[0] + 2, IN[0] + 6):
                if m == IN[0] + 5:
                    by_token(m, range(NT), P)
                else:
                    by_feature(m)
            for i in range(5):
                rope_turn(i, IN[0] + i, y[:, 4 + i, NP_TOK:T] if i < 4 else kT[:, 2 * P:6 * P])
            for m in range(IN[0] + 6, IN[0] + 18):
                by_feature(m)
            pe.wait_ge(rope_applied, 5)
            has_taken(pe, IN[0] + 5)
            pe.wait_ge(cache_in, 32)
            for m in (IN[0] + 16, IN[0] + 17):
                has_taken(pe, m)
            for u in range(3):
                scores_of(u)

            def weigh(v):
                j, s, b = UNITS0[v]
                tiles = key_tiles(b)
                pe.wait_ge(pt_ready, v + 1)
                if v >= 1:
                    pe.wait_ge(pv_read, v)
                for c, tile in enumerate(tiles):
                    mm = pe.matmul(aux[1][64 * s:64 * s + 64, 1, 0:P], vt[:, tile, 64 * s:64 * s + 64],
                                   pt_sb[:, v % 2, c * P:(c + 1) * P],
                                   start=(c == 0), stop=(c == len(tiles) - 1))
                mm.then_inc(pv_done, 1)

            for v in range(NUNIT):
                if v + 3 < NUNIT:
                    scores_of(v + 3)
                pe.wait_ge(p_ready, v + 1)
                if v >= 1:
                    pe.wait_ge(pt_ready, v)
                for c in range(len(key_tiles(UNITS0[v][2]))):
                    mm = pe.transpose(aux[1][:, 0, c * P:(c + 1) * P],
                                      s_sb[:, v % 4, c * P:(c + 1) * P], ident[:])
                mm.then_inc(pt_done, 1)
                if v >= 1:
                    weigh(v - 1)
            weigh(NUNIT - 1)

            def out_and_route(l):
                by_feature_pair(OUT[l], KD * (1 + 3 * l))
                norm_sum(0)
                for k in range(2, KD):
                    by_feature(OUT[l] + k)
                    norm_sum(k - 1)
                norm_sum(KD - 1)

                def keys(i):
                    has_taken(pe, WQ[l] + i)
                    n = 16 * l + i
                    if i == 0:
                        pe.wait_ge(subk_in, 16 * (l + 1))
                    if n >= 2:
                        pe.wait_ge(sc_read, n - 1)
                    for t in range(NT):
                        mm = pe.matmul(aux[n % 2][:, t // 4, (t % 4) * P:(t % 4 + 1) * P],
                                       tmp[:, i % 2, t * P:(t + 1) * P], subk[:, i, :], start=True, stop=True)
                    mm.then_inc(sc_done, 1)

                by_feature_pair(WQ[l], KD * (2 + 3 * l))
                keys(0)
                for i in range(2, 16):
                    by_feature(WQ[l] + i)
                    keys(i - 1)
                keys(15)

            def experts(l):
                def expert(m0, w, split_value, taken_value, beside=0, between=None):
                    pe.wait_ge(lo_done, split_value)
                    pe.wait_ge(taken[m0 % 2], taken_value)
                    spots = [2 * KD * (j + 1) // beside - 1 for j in range(beside)]
                    for h in range(2):
                        n = slice(h * HALF, (h + 1) * HALF)
                        for k in range(KD):
                            mm = linear_step(acc[m0 % 2][:, h, 0:HALF], w, P, k, KD, a_hi, a_lo, n)
                            if h == 1 and k == KD - 1:
                                mm.then_inc(made, 1)
                            if KD * h + k in spots:
                                between()

                with pe.Fori(0, EARLY) as i:
                    for u in range(SPLIT):
                        expert(UM[l] + u, (UC[l] + u) % SPLIT, UC[l] + u + 1 + SPLIT * i,
                               (UM[l] + u) // 2 + (SPLIT // 2) * i)
                for c in range(SPLIT * EARLY, SPLIT * EARLY + BRIDGE):
                    expert(UM[l] + c, (UC[l] + c) % SPLIT, UC[l] + c + 1, (UM[l] + c) // 2)
                pe.wait_ge(picks_ready, l + 1)
                for n in range(15 * l, 15 * l + 15):
                    t, w = (n - 15 * l) // 3, n % 3
                    if n >= 4:
                        pe.wait_ge(turned_read, n - 3)
                    pe.transpose(aux[(n % 4) // 2][:, n % 2, 0:P], picks[:, w, t, :], ident[:])\
                      .then_inc(turned, 1)
                pe.wait_ge(turned_read, 15 * (l + 1))

                def gates_of_four(n, q):
                    wait(pe, gate_read, n - 3)
                    pe.wait_ge(hot_ready, n + 1)
                    for j in range(4):
                        tok = (4 * q + j) % 8
                        for part in range(3):
                            mm = pe.matmul(aux[(q % 4) // 2][:, q % 2, j * P:(j + 1) * P], one_a[:, tok, :],
                                           one_b[:, tok, part, :], start=(part == 0), stop=(part == 2))
                    mm.then_inc(hot_used, 1)

                def late(i):
                    for k in range(2):
                        built = iter(range(16))

                        def next_four():
                            q = next(built)
                            gates_of_four(160 * l + 16 * k + q + 32 * i, q)

                        for u in range(SPLIT):
                            c = SPLIT * (EARLY + k) + BRIDGE + u
                            expert(UM[l] + c, (UC[l] + c) % SPLIT, UC[l] + c + 1 + 2 * SPLIT * i,
                                   (UM[l] + c) // 2 + SPLIT * i, BUILT[u], next_four)

                late(0)
                with pe.Fori(1, NT) as i:
                    late(i)
                for c in range(NKEY - SPLIT + BRIDGE, NKEY):
                    expert(UM[l] + c, (UC[l] + c) % SPLIT, UC[l] + c + 1, (UM[l] + c) // 2)

                for m in (UM[l] + NKEY - 2, UM[l] + NKEY - 1):
                    has_taken(pe, m)

                def values(i, first=False, last=False):
                    for gg in range(2):
                        g = FIRST_G[l] + 2 * i + gg
                        if not (first and gg == 0):
                            pe.wait_ge(p_lo, 4 * g + 4)
                        pe.wait_ge(lo_done, VC[l] + 4 * (2 * i + gg) + 4)
                        for o in range(16):
                            dt, h = o // 2, o % 2
                            wait(pe, v_taken, 16 * g + o - 3)
                            out = acc[(o % 4) // 2][:, o % 2, 0:HALF]
                            n = slice(h * HALF, (h + 1) * HALF)
                            for c in range(GROUP):
                                if first and gg == 0 and o == 0:
                                    pe.wait_ge(p_lo, 4 * g + c + 1)
                                w = (VC[l] + GROUP * gg + c) % SPLIT
                                ps = GROUP * gg + c
                                wh, wl = w_hi[:, w, dt * P:(dt + 1) * P], w_lo[:, w, dt * P:(dt + 1) * P]
                                pe.matmul(out, wh, a_hi[:, ps, n], start=(c == 0), stop=False)
                                pe.matmul(out, wh, a_lo[:, ps, n], start=False, stop=False)
                                mm = pe.matmul(out, wl, a_hi[:, ps, n], start=False, stop=(c == GROUP - 1))
                            mm.then_inc(v_done, 1)
                            if last and gg == 1 and o >= 3 and o % 2 == 1:
                                norm_sum((o - 3) // 2)

                values(0, first=True)
                with pe.Fori(1, BODIES - 1) as i:
                    values(i)
                values(BODIES - 1, last=True)
                norm_sum(KD - 1)

            out_and_route(0)
            experts(0)

            pe.wait_ge(v_taken, 16 * FIRST_G[1])
            first = chunk_at(1, "dzv") % SPLIT
            for i, tiles in enumerate(((0, 1), (2, 3), (4,))):
                by_token(DZV + i, tiles, 512, ready=3 * KD if i == 0 else None,
                         weights=lambda t, k: t[:, first:first + 4, k * P:(k + 1) * P])
            for m in range(IN[1], IN[1] + 10):
                by_feature(m)
                if m == IN[1] + 6:
                    norm_sums(3)
                if m == IN[1] + 7:
                    norm_sums(2)
            pe.wait_ge(const1_in, 16 * N_CONST1)
            for t in range(NT):
                pe.wait_ge(vv_ready, t + 1)
                if t >= 2:
                    pe.wait_ge(mix_read, t - 1)
                for g in range(4):
                    out = aux[1][:, t % 2, g * P:(g + 1) * P]
                    pe.matmul(out, vv[:, t, g * P:(g + 1) * P], ws_t[:, g, :], start=True, stop=False)
                    mm = pe.matmul(out, ones[0:1, :], b_s[:, g, :], start=False, stop=True)
                mm.then_inc(mix_done, 1)
            pe.wait_ge(mix_read, NT)
            has_taken(pe, IN[1] + 5)
            pe.matmul(aux[1][0:32, 1, :], perm[0:32, 96:128], kr[:, NP_TOK:T],
                      start=True, stop=True).then_inc(rope_done, 1)
            pe.wait_ge(lat_lo, 5)
            for i in range(3):
                by_token(UKV + i, [2 * i, 2 * i + 1], 512, 2, ckv_hi, ckv_lo)
            pe.wait_ge(kr_ready, 1)
            pe.wait_ge(cache1_in, 16 * 4)

            flat0 = [b[:].rearrange("p a n -> p (a n)") for b in (aux[0], acc[0])]
            flat1 = aux[1][:].rearrange("p a n -> p (a n)")

            def head_product(h, which):
                m = HEAD + 2 * h + which
                pe.wait_ge(lo_done, PRODUCTS[m][4] + 1)
                has_taken(pe, m - 1)
                w = PRODUCTS[m][4] % SPLIT
                width, kt, hi, lo, cols, off = ((96, 3, cq_hi, cq_lo, HALF, 0),
                                                (P, 2, ckv_hi, ckv_lo, 384, 288))[which]
                if which == 1:
                    pe.wait_ge(rope_applied, 7 + h)
                for half in range(2):
                    mm = linear(acc[1][0:width, half, 0:cols], w, width, kt, hi, lo,
                                slice(half * cols, (half + 1) * cols), off)
                mm.then_inc(made, 1)

            def head_turn(h):
                has_taken(pe, HEAD + 2 * h)
                pe.matmul(acc[1][0:96, 0, :], perm[0:96, 0:96], q_head[:, h % 2, NP_TOK:T],
                          start=True, stop=True).then_inc(rope_done, 1)

            def scores_c(v):
                h, b = divmod(v, NT)
                if b == 0:
                    has_taken(pe, HEAD + 2 * h + 1)
                if v >= 2:
                    pe.wait_ge(s_read, NUNIT + v - 1)
                q, s = q_head[:, h % 2, b * P:(b + 1) * P], flat0[v % 2]
                if b == 0:
                    mm = pe.matmul(s[:, 0:P], q, k_head[:, h % 2, 0:P], start=True, stop=True)
                else:
                    pe.matmul(s[:, 0:512], q, k_head[:, h % 2, P:P + 512], start=True, stop=True)
                    mm = pe.matmul(s[:, 512:640], q, k_head[:, h % 2, P + 512:768], start=True, stop=True)
                mm.then_inc(s_done, 1)

            has_taken(pe, HEAD - 1)
            has_taken(pe, HEAD - 2)
            head_product(0, 0)
            head_turn(0)
            head_product(0, 1)
            scores_c(0)
            scores_c(1)
            for v in range(NUNIT):
                h, b = divmod(v, NT)
                if h + 1 < NH:
                    if b == 0:
                        head_product(h + 1, 0)
                    elif b == 1:
                        head_turn(h + 1)
                    elif b == 2:
                        head_product(h + 1, 1)
                tiles = [0] if b == 0 else [1, 2, 3, 4, 5]
                pe.wait_ge(p_ready, NUNIT + v + 1)
                if v >= 1:
                    pe.wait_ge(pt_ready, NUNIT + v)
                    pe.wait_ge(pv_read, NUNIT + v)
                for c in range(len(tiles)):
                    mm = pe.transpose(flat1[:, c * P:(c + 1) * P], p_sb[:, v % 2, c * P:(c + 1) * P], ident[:])
                mm.then_inc(pt_done, 1)
                if v + 2 < NUNIT:
                    scores_c(v + 2)
                pe.wait_ge(pt_ready, NUNIT + v + 1)
                r = 64 * (h % 2)
                for c, tile in enumerate(tiles):
                    mm = pe.matmul(flat1[r:r + 64, 768:896], vt1[:, tile, 64 * h:64 * h + 64],
                                   pt1[:, c * P:(c + 1) * P], start=(c == 0), stop=(c == len(tiles) - 1))
                mm.then_inc(pv_done, 1)
            out_and_route(1)
            experts(1)

        @block.scalar
        def _(act):
            act.dma_start(c_all[:], a["c_all"]).then_inc(c_in, 16)
            act.dma_start(c_cols[:], a["c_cols"]).then_inc(c_cols_in, 16)
            act.dma_start(ones[:], a["ones"]).then_inc(ones_in, 16)
            act.dma_start(x[:], a["x"]).then_inc(x_in, 16)
            for dst, name in ((ident, "ident"), (iota, "iota"),
                              (mask, "mask"), (perm, "perm0"), (rope, "rope0"), (b_mod, "b_mod"),
                              (g_norm, "g_norm"), (sink, "sink"), (conv_w, "conv_w"), (g_small, "g_small")):
                act.dma_start(dst[:], a[name]).then_inc(const_in, 16)
            act.wait_ge(c_in, 16)
            act.activation(c_all[:], c_all[:], ACT.Silu).then_inc(silu_ready, 1)
            act.wait_ge(c_cols_in, 16)
            act.activation(c_cols[:], c_cols[:], ACT.Silu).then_inc(c_ready, 1)
            act.wait_ge(x_in, 16)

            norm = [0]

            def squares(src, tiles=KD, complete=None):
                for k in range(tiles):
                    q = SQ[norm[0]] + k
                    if complete:
                        complete(k)
                    if q >= 2:
                        act.wait_ge(sq_used, q - 1)
                    act.activation(tmp[:, q % 2, :], src[:, k, :], ACT.Square).then_inc(sq_ready, 1)

            def root():
                act.wait_ge(var_ready, norm[0] + 1)
                act.activation(rstd[:], rstd[:], ACT.Sqrt).then_inc(rstd_ready, 1)
                norm[0] += 1

            def high(n):
                l, row = n // 2, (0, 3)[n % 2]
                for k in range(KD):
                    act.wait_ge(h_ready, KD * n + k + 1)
                    for c, cols in ((0, slice(0, P)), (1, slice(P, T))):
                        h = tmp[:, k % 2, cols]
                        act.activation(h, h, ACT.Identity, bias=mod[:, l, KD * row + k, c:c + 1],
                                       scale=gain[:, n, k, c:c + 1]).then_inc(modulated, 1)
                    act.wait_ge(modulated, 2 * (KD * n + k + 1))
                    act.activation(a_hi[:, k, :], tmp[:, k % 2, :], ACT.Copy).then_inc(hi_ready, 1)

            def take(m, out, in_, func=ACT.Copy):
                act.wait_ge(made, m + 1)
                act.activation(out, in_, func).then_inc(taken[m % 2], 1)

            def feature(m, width=P, cols=HALF):
                return acc[m % 2][0:width, :, 0:cols]

            squares(x)
            root()
            high(0)
            act.wait_ge(mod_used, BY_DVE)
            act.dma_start(kT[:, 0:P], a["cache_k"]).then_inc(cache_in, 16)
            act.dma_start(vt[:, 0, :], a["cache_v"]).then_inc(cache_in, 16)
            for i in range(4):
                take(IN[0] + i, halves(y[:, 4 + i, :]), feature(IN[0] + i))
            m = IN[0] + 4
            take(m, halves(kT[:, P:768]), feature(m))
            has_taken(act, m)
            act.dma_start(a["new_k"], kT[:, P:2 * P]).then_inc(state_out, 16)
            m = IN[0] + 5
            act.wait_ge(made, m + 1)
            act.activation(vt[:, 1:5, :].rearrange("p t n -> p (t n)"), acc[m % 2][:, 0, :], ACT.Copy)
            act.activation(vt[:, 5, :], acc[m % 2][:, 1, 0:P], ACT.Copy).then_inc(taken[m % 2], 1)
            has_taken(act, m)
            act.dma_start(a["new_v"], vt[:, 1, :]).then_inc(state_out, 16)
            for j in range(4):
                m = IN[0] + 6 + 3 * j
                take(m, halves(y[:, j, :]), feature(m))
                if j:
                    has_taken(act, m - 1)
                take(m + 1, halves(gate_c[:]), feature(m + 1))
            act.wait_ge(mod_used, 48 - (FIRST_MOD - BY_DVE))
            for u in range(NUNIT + 4):
                if 3 <= u < NUNIT + 3:
                    v = u - 3
                    n = keys_of(UNITS0[v][2])
                    act.wait_ge(pt_done, v + 1)
                    if v >= 2:
                        act.wait_ge(pv_done, v - 1)
                    act.activation(pt_sb[:, v % 2, 0:n], aux[1][:, 0, 0:n], ACT.Copy).then_inc(pt_ready, 1)
                if u >= 4:
                    v = u - 4
                    j, s, b = UNITS0[v]
                    rows = slice(64 * s, 64 * s + 64)
                    act.wait_ge(pv_done, v + 1)
                    act.activation(y[rows, 4 + j, b * P:(b + 1) * P], aux[1][rows, 1, 0:P], ACT.Copy)\
                       .then_inc(pv_read, 1)
                if u < NUNIT:
                    j, s, b = UNITS0[u]
                    n, st, hd = keys_of(b), stat[:, u % 4, :], 4 * s + j
                    act.wait_ge(neg_ready, u + 1)
                    act.activation(s_sb[:, u % 4, 0:n], s_sb[:, u % 4, 0:n], ACT.Exp, bias=st[:, 1:2],
                                   accum_out=st[:, 2:3])
                    act.activation(st[:, 3:4], sink[:, hd:hd + 1], ACT.Exp, bias=st[:, 1:2]).then_inc(e_ready, 1)
                if u in MIXED_AT:
                    k = MIXED_AT.index(u)
                    if k == 0:
                        act.wait_ge(made, OUT[0])
                        act.wait_ge(conv_ready, 4)
                    act.activation(a_hi[:, k, :], y[:, k, :], ACT.Copy).then_inc(hi_ready, 1)

            def out_and_route(l):
                act.wait_ge(pv_read, NUNIT * (l + 1))
                act.dma_start(subk[:], a["subk"][l]).then_inc(subk_in, 16)
                if l == 0:
                    act.wait_ge(conv_ready, 4)
                else:
                    act.wait_ge(mix_read, NT)
                act.wait_ge(made, OUT[l])
                for k in range(0 if l else KD - 1, KD):
                    act.activation(a_hi[:, k, :], y[:, k, :], ACT.Copy).then_inc(hi_ready, 1)
                squares(x, complete=lambda k: has_taken(act, OUT[l] + k))
                root()
                high(2 * l + 1)
                act.wait_ge(lo_ready, KD * (3 + 3 * l))
                for i in range(16):
                    m, n = WQ[l] + i, 16 * l + i
                    if i >= 2:
                        act.wait_ge(sc_done, n - 1)
                    take(m, halves(tmp[:, i % 2, :]), feature(m))

            def experts(l):
                def activation(slot, m0, made_value, stores, taken_value, c):
                    out = a_out[:, slot, :] if slot < 2 else tmp[:, slot - 2, :]
                    act.wait_ge(made, made_value)
                    wait(act, a_st[slot], 16 * stores)
                    act.activation(halves(out), feature(m0), ACT.Gelu_apprx_tanh).then_inc(taken[m0 % 2], 1)
                    act.wait_ge(taken[m0 % 2], taken_value)
                    act.dma_start(a["act_s"][l, bass.ds(c, 1)].rearrange("o p n -> (o p) n"), out)\
                       .then_inc(a_st[slot], 16)

                def late_stores(c):
                    return A_ALL[c % 4] * l + (A_EARLY if c % 4 < 2 else 0) + (c - EARLY * SPLIT) // 4

                def early(i):
                    for u in range(SPLIT):
                        m0 = UM[l] + u
                        activation(u % 2, m0, m0 + 1 + SPLIT * i, A_ALL[u % 2] * l + u // 2 + 4 * i,
                                   m0 // 2 + 1 + 4 * i, SPLIT * i + u)

                early(0)
                with act.Fori(1, EARLY) as i:
                    early(i)
                act.wait_ge(shifted, l + 1)
                gate_in = picks[:, 2, :, :]
                act.activation(gate_in, gate_in, ACT.Exp).then_inc(exp_done, 1)
                for c in range(SPLIT * EARLY, SPLIT * EARLY + BRIDGE):
                    m0 = UM[l] + c
                    activation(c % 4, m0, m0 + 1, late_stores(c), m0 // 2 + 1, c)
                for n in range(15 * l, 15 * l + 15):
                    t, w = (n - 15 * l) // 3, n % 3
                    act.wait_ge(turned, n + 1)
                    act.activation(picks_t[:, w, t * P:(t + 1) * P], aux[(n % 4) // 2][:, n % 2, 0:P],
                                   ACT.Copy).then_inc(turned_read, 1)

                def store_gates(piece, first_token):
                    keys = slice(NKEY // PIECES * piece, NKEY // PIECES * (piece + 1))
                    act.dma_start(a["gate_s"][l, keys, :, bass.ds(first_token, 64)].rearrange("e p t -> p e t"),
                                  gates[:, keys, :]).then_inc(gates_out, 16)

                def late(i, first=False):
                    for k in range(2):
                        q = 0
                        for u in range(SPLIT):
                            c = SPLIT * (EARLY + k) + BRIDGE + u
                            m0 = UM[l] + c
                            activation(c % 4, m0, m0 + 1 + 16 * i, late_stores(c) + 4 * i,
                                       m0 // 2 + 1 + 8 * i, c + 16 * i)
                            if u == 0 and not (first and k == 0):
                                store_gates(PIECES - 1, 128 * i + 64 * k - 64)
                            for _ in range(COPIED[u]):
                                n = 160 * l + 16 * k + q + 32 * i
                                act.wait_ge(hot_used, n + 1)
                                if q == 0:
                                    wait(act, gates_out, PIECES * (160 * l + 16 * k + 32 * i))
                                act.activation(gates[:, :, 4 * q:4 * q + 4].rearrange("p e t -> p t e"),
                                               aux[(q % 4) // 2][:, q % 2, :].rearrange("p (t e) -> p t e", t=4),
                                               ACT.Copy).then_inc(gate_read, 1)
                                q += 1
                        act.wait_ge(gate_read, 160 * l + 16 * k + 16 + 32 * i)
                        for piece in range(PIECES - 1):
                            store_gates(piece, 128 * i + 64 * k)

                late(0, first=True)
                with act.Fori(1, NT) as i:
                    late(i)
                for c in range(NKEY - SPLIT + BRIDGE, NKEY):
                    m0 = UM[l] + c
                    activation(c % 4, m0, m0 + 1, late_stores(c), m0 // 2 + 1, c)
                    if c == NKEY - SPLIT + BRIDGE:
                        store_gates(PIECES - 1, T - 64)

                def high_p(i, chunks=range(SPLIT)):
                    for k in chunks:
                        n = NKEY * l + k + SPLIT * i
                        act.wait_ge(p_made, n + 1)
                        if not (isinstance(i, int) and i == 0):
                            act.wait_ge(v_done, 16 * (FIRST_G[l] + k // GROUP - 1) + 32 * i)
                        act.activation(a_hi[:, k, :], p_raw[:, k % 2, :], ACT.Copy).then_inc(p_hi, 1)

                high_p(0, range(GROUP))
                if l == 0:
                    act.dma_start(c_all_v[:], a["c_all"]).then_inc(c_in, 16)
                    act.wait_ge(c_in, 32)
                    act.activation(c_all_v[:], c_all_v[:], ACT.Silu).then_inc(silu_ready, 1)
                high_p(0, range(GROUP, SPLIT))
                with act.Fori(1, BODIES) as i:
                    high_p(i)

            out_and_route(0)
            experts(0)

            def x_complete(l):
                return lambda k: act.wait_ge(v_taken, 16 * (FIRST_G[l] + NKEY // GROUP) - 14 + 2 * k)

            squares(x, complete=x_complete(0))
            for dst, name in ((perm, "perm1"), (rope, "rope1"), (ws_t, "ws_t"), (b_s, "b_s"), (g_sgu, "g_sgu")):
                act.dma_start(dst[:], a[name]).then_inc(const1_in, 16)
            root()
            high(2)
            for i in range(3):
                m, n = DZV + i, min(2, NT - 2 * i)
                take(m, vv[:, 2 * i:2 * i + n, :], acc[m % 2][:, 0:n, :], ACT.Gelu_apprx_tanh)
            for i in (1, 2):
                has_taken(act, DZV + i)
            act.wait_ge(lo_ready, KD * 4)
            for t in range(NT):
                if t:
                    act.wait_ge(ss_ready, t)
                act.activation(rstd[:, 0:512], vv[:, t, :], ACT.Square, accum_out=ss[:, t:t + 1])\
                   .then_inc(ss_ready, 1)
            for c in range(3):
                m = IN[1] + c
                take(m, halves(cq[:, c, :]), feature(m))
            act.wait_ge(ss_inv, 1)
            act.activation(ss[:, 0:NT], ss[:, 0:NT], ACT.Sqrt).then_inc(ss_root, 1)
            for c in range(2):
                m = IN[1] + 3 + c
                take(m, halves(ckv[:, c, :]), feature(m))
            m = IN[1] + 5
            take(m, halves(kr[:]), acc[m % 2][0:32, :, 0:HALF])
            has_taken(act, m)
            act.dma_start(a["new_kr"], kr[:, 0:NP_TOK]).then_inc(state_out, 16)
            act.dma_start(kr_rope[:], a["rope_k"]).then_inc(cache1_in, 16)
            act.dma_start(ckv_old[:], a["cache_ckv"]).then_inc(cache1_in, 16)

            def take_gating(c):
                m = IN[1] + 6 + c
                take(m, halves(y[:, 4 + c, :]), feature(m), ACT.Gelu_apprx_tanh)

            has_taken(act, IN[1] + 2)
            squares(cq, 3)
            take_gating(0)
            root()
            has_taken(act, IN[1] + 4)
            squares(ckv, 2)
            take_gating(1)
            root()
            take_gating(2)
            take_gating(3)
            for i in range(2):
                act.dma_start(k_head[64:96, i, P:2 * P], a["cache_kr"]).then_inc(cache1_in, 16)
            for k in range(3):
                act.wait_ge(lat_norm, k + 1)
                act.activation(cq_hi[:, k, :], cq[:, k, :], ACT.Copy).then_inc(lat_hi, 1)
            act.wait_ge(cache1_in, 16 * 4)
            for k in range(2):
                act.wait_ge(lat_norm, 4 + k)
                act.activation(ckv_hi[:, k, 0:P], ckv[:, k, 0:P], ACT.Copy)
                act.activation(ckv_hi[:, k, P:2 * P], ckv_old[:, k, :], ACT.Copy)
                act.activation(ckv_hi[:, k, 2 * P:768], ckv[:, k, P:T], ACT.Copy).then_inc(lat_hi, 1)
            act.dma_start(a["new_ckv"], ckv[:, :, 0:P]).then_inc(state_out, 16)
            for i in range(3):
                m = UKV + i
                take(m, vt1[:, 2 * i:2 * i + 2, :], acc[m % 2][:])
            act.wait_ge(rope_applied, 6)
            act.wait_ge(kr_ready, 1)
            flat0 = [b[:].rearrange("p a n -> p (a n)") for b in (aux[0], acc[0])]
            flat1 = aux[1][:].rearrange("p a n -> p (a n)")

            def take_head(h, which):
                m = HEAD + 2 * h + which
                act.wait_ge(made, m + 1)
                out, rows, cols = ((q_head[:, h % 2, :], 96, HALF), (k_head[0:64, h % 2, :], 64, 384))[which]
                act.activation(halves(out), acc[1][0:rows, :, 0:cols], ACT.Copy).then_inc(taken[m % 2], 1)

            take_head(0, 0)
            take_head(0, 1)
            for u in range(NUNIT + 2):
                if u >= 2:
                    v = u - 2
                    h, b = divmod(v, NT)
                    n = P if b == 0 else T
                    rows = slice(64 * (h % 2), 64 * (h % 2) + 64)
                    if h + 1 < NH and b in (0, 2):
                        take_head(h + 1, b // 2)
                    act.wait_ge(pt_done, NUNIT + v + 1)
                    act.activation(pt1[:, 0:n], flat1[:, 0:n], ACT.Copy).then_inc(pt_ready, 1)
                    act.wait_ge(pv_done, NUNIT + v + 1)
                    act.activation(y[rows, h // 2, b * P:(b + 1) * P], flat1[rows, 768:896], ACT.Copy)\
                       .then_inc(pv_read, 1)
                if u < NUNIT:
                    h, b = divmod(u, NT)
                    n, st = (P if b == 0 else T), stat[:, u % 2, :]
                    act.wait_ge(neg_ready, NUNIT + u + 1)
                    if u >= 2:
                        act.wait_ge(pt_done, NUNIT + u - 1)
                    act.activation(p_sb[:, u % 2, 0:n], flat0[u % 2][:, 0:n], ACT.Exp, bias=st[:, 1:2],
                                   scale=SCALE_C, accum_out=st[:, 2:3]).then_inc(s_read, 1)
            out_and_route(1)
            experts(1)
            squares(x, complete=x_complete(1))
            root()

        @block.vector
        def _(dve):
            steps = [0]

            def note(ins):
                ins.then_inc(dve_step, 1)
                steps[0] += 1

            def settle():
                dve.wait_ge(dve_step, steps[0])

            def step(ins):
                note(ins)
                settle()

            norm = [0]

            def variance(tiles=KD):
                dve.wait_ge(sq_used, SQ[norm[0]] + tiles)
                step(dve.tensor_scalar(halves(rstd[:]), aux[0][:, :, 0:HALF], 1.0 / (P * tiles), EPS,
                                       ALU.mult, ALU.add))
                dve.reciprocal(rstd[:], rstd[:]).then_inc(var_ready, 1)
                norm[0] += 1
                dve.wait_ge(rstd_ready, norm[0])

            def normed(s):
                for k in range(KD + 1):
                    if k < KD:
                        h = tmp[:, k % 2, :]
                        if k >= 2:
                            dve.wait_ge(lo_ready, KD * s + k - 1)
                        dve.tensor_tensor(h, x[:, k, :], rstd[:], ALU.mult).then_inc(h_ready, 1)
                    if k >= 1:
                        dve.wait_ge(hi_ready, KD * s + k)
                        dve.tensor_tensor(a_lo[:, k - 1, :], tmp[:, (k - 1) % 2, :],
                                          a_hi[:, k - 1, :].bitcast(F), ALU.subtract).then_inc(lo_ready, 1)

            def add_to_x(k, l, row, banks, free):
                parts = [(slice(0, P), banks[0][:, 0:P], 0), (slice(P, HALF), banks[0][:, P:HALF], 1),
                         (slice(HALF, T), banks[1][:, 0:HALF], 1)]
                for i, (cols, src, c) in enumerate(parts):
                    ins = dve.scalar_tensor_tensor(x[:, k, cols], src, mod[:, l, KD * row + k, c:c + 1],
                                                   x[:, k, cols], ALU.mult, ALU.add)
                    if i < 2:
                        note(ins)
                ins.then_inc(free, 1)

            def rotate(i, src, bank, cos_sin, mult_rows=P):
                t = rstd[0:mult_rows, 0:NL_TOK]
                dve.wait_ge(rope_done, i + 1)
                note(dve.tensor_tensor(t, bank, cos_sin[:, 1, :], ALU.mult))
                step(dve.tensor_tensor(src, src, cos_sin[:, 0, :], ALU.mult))
                dve.tensor_tensor(src, src, t, ALU.add).then_inc(rope_applied, 1)
                dve.wait_ge(rope_applied, i + 1)

            def modulate(w, out):
                for c in range(2):
                    ins = dve.tensor_tensor_reduce(out=unread[:], in0=w, in1=c_all[:, c, :],
                                                   scale=1.0, scalar=0.0, op0=ALU.mult, op1=ALU.add,
                                                   accum_out=out[:, c:c + 1])
                    if c == 0:
                        step(ins)
                ins.then_inc(mod_used, 1)

            def add_bias(l, first=0, past=48):
                step(dve.tensor_tensor(mod[:, l, first:past], mod[:, l, first:past],
                                       b_mod[:, l, first:past].unsqueeze(2).to_broadcast([P, past - first, 2]),
                                       ALU.add))

            dve.wait_ge(silu_ready, 1)
            for k in range(BY_DVE):
                dve.wait_ge(mod_in[k % 5], 16 * (k // 5 + 1))
                modulate(w_mod[:, k % 5, :], mod[:, 0, k, :])
                dve.wait_ge(mod_used, k + 1)
            dve.wait_ge(const_in, 16 * N_CONST)
            dve.wait_ge(mod_pe_used, FIRST_MOD - BY_DVE)
            step(dve.tensor_copy(mod[:, 0, BY_DVE:FIRST_MOD],
                                 aux[1][:, 0, 0:2 * (FIRST_MOD - BY_DVE)].rearrange("p (k c) -> p k c", c=2)))
            add_bias(0, 0, FIRST_MOD)

            def gains(n):
                row = (1, 4)[n % 2]
                step(dve.scalar_tensor_tensor(gain[:, n], mod[:, n // 2, KD * row:KD * row + KD, :], 1.0,
                                              g_norm[:, n, :].unsqueeze(2).to_broadcast([P, KD, 2]),
                                              ALU.add, ALU.mult))

            gains(0)

            step(dve.tensor_copy(iota_b[:], iota[:]))
            variance()
            normed(0)
            step(dve.memset(u_pad[:], 0.0))
            dve.wait_ge(lo_ready, KD)

            tile = FIRST_MOD

            def modulate_b(tiles):
                for k in tiles:
                    dve.wait_ge(mod_b_in[k % 2], 16 * ((k - FIRST_MOD) // 2 + 1))
                    modulate(w_mod_b[:, k % 2, :], mod[:, 0, k, :])
                    dve.wait_ge(mod_used, k + 1 - (FIRST_MOD - BY_DVE))

            modulate_b(range(tile, tile + MOD_BEFORE_ROPE))
            tile += MOD_BEFORE_ROPE
            for i in range(5):
                rotate(i, y[:, 4 + i, NP_TOK:T] if i < 4 else kT[:, 2 * P:6 * P], aux[1][:, i % 2, :], rope)
            for j in range(4):
                modulate_b(range(tile, tile + MOD_BEFORE_CONV[j]))
                tile += MOD_BEFORE_CONV[j]
                m = IN[0] + 8 + 3 * j
                dve.wait_ge(made, m + 1)
                has_taken(dve, m - 1)
                bank = acc[m % 2]
                note(dve.tensor_tensor(u_pad[:, 1:129], bank[:, 0, 0:P], gate_c[:, 0:P], ALU.mult))
                note(dve.tensor_tensor(u_pad[:, 131:323], bank[:, 0, P:HALF], gate_c[:, P:HALF], ALU.mult))
                dve.tensor_tensor(u_pad[:, 323:643], bank[:, 1, 0:HALF], gate_c[:, HALF:T], ALU.mult)\
                   .then_inc(taken[m % 2], 1)
                has_taken(dve, m)
                step(dve.tensor_scalar(conv[:], u_pad[:, 0:642], conv_w[:, j, 0:1], None, ALU.mult))
                for w in (1, 2):
                    step(dve.scalar_tensor_tensor(conv[:], u_pad[:, w:w + 642], conv_w[:, j, w:w + 1], conv[:],
                                                  ALU.mult, ALU.add))
                has_taken(dve, m - 2)
                note(dve.tensor_tensor(y[:, j, 0:P], y[:, j, 0:P], conv[:, 0:P], ALU.mult))
                dve.tensor_tensor(y[:, j, P:T], y[:, j, P:T], conv[:, 130:642], ALU.mult).then_inc(conv_ready, 1)
                dve.wait_ge(conv_ready, j + 1)
            add_bias(0, FIRST_MOD, 48)
            def low_part(k, s):
                dve.wait_ge(hi_ready, KD * s + k + 1)
                dve.tensor_tensor(a_lo[:, k, :], y[:, k, :], a_hi[:, k, :].bitcast(F), ALU.subtract)\
                   .then_inc(lo_ready, 1)

            for u in range(NUNIT + 3):
                if u - 2 in MIXED_AT:
                    low_part(MIXED_AT.index(u - 2), 1)
                if u >= 3:
                    v = u - 3
                    n, st = keys_of(UNITS0[v][2]), stat[:, v % 4, :]
                    dve.wait_ge(e_ready, v + 1)
                    step(dve.tensor_tensor(st[:, 4:5], st[:, 2:3], st[:, 3:4], ALU.add))
                    step(dve.reciprocal(st[:, 5:6], st[:, 4:5]))
                    dve.tensor_scalar(s_sb[:, v % 4, 0:n], s_sb[:, v % 4, 0:n], st[:, 5:6], None, ALU.mult)\
                       .then_inc(p_ready, 1)
                if u < NUNIT:
                    j, s, b = UNITS0[u]
                    n, st, hd = keys_of(b), stat[:, u % 4, :], 4 * s + j
                    dve.wait_ge(s_done, u + 1)
                    if u >= 4:
                        dve.wait_ge(pt_done, u - 3)
                    ins = dve.tensor_scalar(s_sb[:, u % 4, 0:P], s_bank(u)[:, 0:P], SCALE_B, None, ALU.mult)
                    if b > 0:
                        note(ins)
                        skip = P * (local(b)[0] - b)
                        ins = dve.scalar_tensor_tensor(s_sb[:, u % 4, P:n], s_bank(u)[:, P:n], SCALE_B,
                                                       mask[:, skip:skip + n - P], ALU.mult, ALU.add)
                    ins.then_inc(s_read, 1)
                    dve.wait_ge(s_read, u + 1)
                    step(dve.reduce_max(st[:, 0:1], s_sb[:, u % 4, 0:n], AX.X))
                    dve.tensor_scalar(st[:, 1:2], st[:, 0:1], sink[:, hd:hd + 1], -1.0, ALU.max, ALU.mult)\
                       .then_inc(neg_ready, 1)

            def out_and_route(l):
                s = 1 + 3 * l
                gains(2 * l + 1)
                for k in range(0 if l else KD - 1, KD):
                    low_part(k, s)
                for k in range(KD):
                    m = OUT[l] + k
                    dve.wait_ge(made, m + 1)
                    add_to_x(k, l, 2, (acc[m % 2][:, 0, :], acc[m % 2][:, 1, :]), taken[m % 2])
                variance()
                normed(s + 1)
                for i in range(16):
                    n = 16 * l + i
                    dve.wait_ge(sc_done, n + 1)
                    note(dve.tensor_copy(scores[:, 0:4, i, :],
                                         aux[n % 2][:, 0, :].rearrange("p (t k) -> p t k", t=4)))
                    dve.tensor_copy(scores[:, 4, i, :], aux[n % 2][:, 1, 0:P]).then_inc(sc_read, 1)
                dve.wait_ge(sc_read, 16 * (l + 1))

            def top16(heads, values, indices, data):
                for half in range(2):
                    r = slice(8 * half, 8 * half + 8)
                    for h in range(heads):
                        note(dve.max(values[:, h, r], data(h)))
                    settle()
                    for h in range(heads):
                        note(dve.max_index(indices[:, h, r], values[:, h, r], data(h)))
                    settle()
                    if half == 0:
                        for h in range(heads):
                            note(dve.match_replace(data(h), values[:, h, r], data(h), NEG))
                        settle()

            def route(l):
                four = [P, NH, 16, 16]
                for t in range(NT):
                    top16(16, top_v, top_i, lambda h: scores[:, t, h, :])
                    step(dve.tensor_copy(top_f[:], top_i[:]))
                    side = [v[:].rearrange("p (h s) k -> p h s k", s=2) for v in (top_v, top_f)]
                    step(dve.tensor_tensor(cand[:], side[0][:, :, 0, :].unsqueeze(3).to_broadcast(four),
                                           side[0][:, :, 1, :].unsqueeze(2).to_broadcast(four), ALU.add))
                    top16(NH, best, place, lambda h: cand[:, h].rearrange("p i j -> p (i j)"))
                    for s, (amount, op) in enumerate(((4, ALU.logical_shift_right), (15, ALU.bitwise_and))):
                        step(dve.tensor_scalar(part_i[:], place[:], amount, None, op))
                        step(dve.tensor_copy(part_f[:], part_i[:]))
                        step(dve.tensor_tensor(cand[:], part_f[:].unsqueeze(3).to_broadcast(four),
                                               iota[:, 0:16].unsqueeze(1).unsqueeze(1).to_broadcast(four),
                                               ALU.is_equal))
                        step(dve.tensor_tensor(cand[:], cand[:],
                                               side[1][:, :, s, :].unsqueeze(2).to_broadcast(four), ALU.mult))
                        step(dve.tensor_reduce(picks[:, s, t, :].rearrange("p (h k) -> p h k", h=NH), cand[:],
                                               AX.X, ALU.add))
                    gate = picks[:, 2, t, :].rearrange("p (h k) -> p h k", h=NH)
                    ins = dve.tensor_tensor(gate, best[:], best[:, :, 0:1].to_broadcast([P, NH, 16]),
                                            ALU.subtract)
                    if t < NT - 1:
                        step(ins)
                ins.then_inc(shifted, 1)
                dve.wait_ge(exp_done, l + 1)
                every = picks[:, 2, :, :].rearrange("p t (h k) -> p (t h) k", h=NH)
                sums = cand[:].rearrange("p h i j -> p (h i j)")[:, 0:NT * NH]
                step(dve.tensor_reduce(sums, every, AX.X, ALU.add))
                step(dve.reciprocal(sums, sums))
                dve.tensor_tensor(every, every, sums.unsqueeze(2).to_broadcast([P, NT * NH, 16]), ALU.mult)\
                   .then_inc(picks_ready, 1)
                dve.wait_ge(turned_read, 15 * (l + 1))
                for part in range(2):
                    step(dve.tensor_copy(part_b[:], picks_t[:, 2 + part, :]))
                    step(dve.tensor_tensor(picks_t[:, 3 + part, :], picks_t[:, 2 + part, :], part_b[:],
                                           ALU.subtract))
                    step(dve.tensor_copy(picks_t[:, 2 + part, :], part_b[:]))

            def experts(l):
                def one_hots(i):
                    for q in range(32):
                        n = 160 * l + q + 32 * i
                        wait(dve, hot_used, n - 1)
                        for j in range(4):
                            tok = 4 * q + j
                            column = bass.ds(P * i + tok, 1)
                            dve.tensor_scalar(one_a[:, tok % 8, :], iota_b[:], picks_t[:, 0, column], None,
                                              ALU.is_equal)
                            ins = dve.scalar_tensor_tensor(
                                one_b[:, tok % 8], iota_b[:].unsqueeze(1).to_broadcast([P, 3, NKEY]),
                                picks_t[:, 1, column], picks_t[:, 2:5, column].to_broadcast([P, 3, NKEY]),
                                ALU.is_equal, ALU.mult)
                        ins.then_inc(hot_ready, 1)

                one_hots(0)
                with dve.Fori(1, NT) as i:
                    one_hots(i)

                def form(i, k, first=False):
                    n = NKEY * l + k + SPLIT * i
                    dve.wait_ge(ag_in[k % 4], 32 * (32 * l + k // 4 + 1) + 64 * i)
                    wait(dve, p_lo, n - 1)
                    dve.tensor_tensor(p_raw[:, k % 2, :], ag[:, k % 4, 0, :], ag[:, k % 4, 1, :], ALU.mult)\
                       .then_inc(p_made, 1)

                def low_p(i, k):
                    n = NKEY * l + k + SPLIT * i
                    dve.wait_ge(p_hi, n + 1)
                    dve.tensor_tensor(a_lo[:, k, :], p_raw[:, k % 2, :], a_hi[:, k, :].bitcast(F), ALU.subtract)\
                       .then_inc(p_lo, 1)

                def modulate_v(i, s):
                    dve.wait_ge(mod_v_in[s], 16 + 16 * i)
                    w, c_v = w_mod_v[:, s, :], c_all_v
                    dve.wait_ge(silu_ready, 2)
                    for c in range(2):
                        wait(dve, mod_v_sum, 2 * s + c + 6 * i)
                        dve.tensor_tensor_reduce(out=unread[:], in0=w, in1=c_v[:, c, :], scale=1.0, scalar=0.0,
                                                 op0=ALU.mult, op1=ALU.add, accum_out=mod_v[:, s, c:c + 1])\
                           .then_inc(mod_v_sum, 1)
                    dve.wait_ge(mod_v_sum, 2 * s + 2 + 6 * i)
                    dve.tensor_copy(mod[:, 1, bass.ds(3 * i + s, 1), :], mod_v[:, s:s + 1, :])\
                       .then_inc(mod_v_used, 1)

                def sums(i, last=False):
                    for gg in range(2):
                        g = FIRST_G[l] + gg + 2 * i
                        for o in range(16):
                            if l == 0 and (gg, o) in ((0, 7), (0, 15), (1, 7)):
                                modulate_v(i, {(0, 7): 0, (0, 15): 1, (1, 7): 2}[gg, o])
                            if not (last and gg == 1):
                                j, later = o // 4, (i if gg == 0 else i + 1)
                                k = j + (GROUP if gg == 0 else 0)
                                if o % 4 == 0:
                                    form(later, k)
                                if o % 4 == 2:
                                    low_p(later, k)
                            dt, h = o // 2, o % 2
                            bank = acc[(o % 4) // 2][:, o % 2, :]
                            dve.wait_ge(v_done, o + 1 + 16 * g)
                            wait(dve, v_taken, 16 * g - 16 + o + 1)
                            if h == 0:
                                dve.scalar_tensor_tensor(x[:, dt, 0:P], bank[:, 0:P], mod[:, l, 40 + dt, 0:1],
                                                         x[:, dt, 0:P], ALU.mult, ALU.add)
                                cols, src = slice(P, HALF), bank[:, P:HALF]
                            else:
                                cols, src = slice(HALF, T), bank[:, 0:HALF]
                            dve.scalar_tensor_tensor(x[:, dt, cols], src, mod[:, l, 40 + dt, 1:2], x[:, dt, cols],
                                                     ALU.mult, ALU.add).then_inc(v_taken, 1)

                for k in range(GROUP):
                    form(0, k)
                    low_p(0, k)
                sums(0)
                with dve.Fori(1, BODIES - 1) as i:
                    sums(i)
                sums(BODIES - 1, last=True)
                dve.wait_ge(v_taken, 16 * (FIRST_G[l] + 32))
                if l == 0:
                    dve.wait_ge(mod_v_used, 48)

            out_and_route(0)
            route(0)
            experts(0)

            add_bias(1)
            gains(2)
            variance()
            normed(3)
            dve.wait_ge(ss_ready, NT)
            step(dve.tensor_scalar(ss[:, 0:NT], ss[:, 0:NT], 1.0 / 512, EPS, ALU.mult, ALU.add))
            dve.reciprocal(ss[:, 0:NT], ss[:, 0:NT]).then_inc(ss_inv, 1)
            dve.wait_ge(ss_root, 1)
            dve.wait_ge(const1_in, 16 * N_CONST1)
            for t in range(NT):
                dve.scalar_tensor_tensor(vv[:, t, :], vv[:, t, :], ss[:, t:t + 1], g_sgu[:], ALU.mult, ALU.mult)\
                   .then_inc(vv_ready, 1)
            for first, tiles, t in ((0, 3, cq), (3, 2, ckv)):
                variance(tiles)
                for k in range(tiles):
                    dve.scalar_tensor_tensor(t[:, k, :], t[:, k, :], g_small[:, first + k:first + k + 1], rstd[:],
                                             ALU.mult, ALU.mult).then_inc(lat_norm, 1)
                dve.wait_ge(lat_norm, first + tiles)
            for c in range(2):
                has_taken(dve, IN[1] + 8 + c)
            for n in range(NT):
                dve.wait_ge(mix_done, n + 1)
                part = y[:, 4:8, n * P:(n + 1) * P]
                dve.tensor_tensor(part, part, aux[1][:, n % 2, :].rearrange("p (g t) -> p g t", g=4), ALU.mult)\
                   .then_inc(mix_read, 1)
                t, hi, lo, k = (cq, cq_hi, cq_lo, n) if n < 3 else (ckv, ckv_hi, ckv_lo, n - 3)
                dve.wait_ge(lat_hi, n + 1)
                parts = [(t[:, k, :], slice(0, T))] if n < 3 else \
                    [(t[:, k, 0:P], slice(0, P)), (ckv_old[:, k, :], slice(P, 2 * P)),
                     (t[:, k, P:T], slice(2 * P, 768))]
                for src, cols in parts:
                    ins = dve.tensor_tensor(lo[:, k, cols], src, hi[:, k, cols].bitcast(F), ALU.subtract)
                    if cols.stop < parts[-1][1].stop:
                        note(ins)
                ins.then_inc(lat_lo, 1)
            dve.wait_ge(cache1_in, 16 * 4)
            rotate(5, kr[:, NP_TOK:T], aux[1][0:32, 1, :], kr_rope, 32)
            for i in range(2):
                note(dve.tensor_copy(k_head[64:96, i, 0:P], kr[:, 0:P]))
                ins = dve.tensor_copy(k_head[64:96, i, 2 * P:768], kr[:, P:T])
                if i == 0:
                    note(ins)
            ins.then_inc(kr_ready, 1)
            flat0 = [b[:].rearrange("p a n -> p (a n)") for b in (aux[0], acc[0])]

            def turn_head(h):
                rotate(6 + h, q_head[:, h % 2, NP_TOK:T], acc[1][0:96, 0, :], rope[0:96], 96)

            turn_head(0)
            for u in range(NUNIT + 2):
                if u >= 2:
                    v = u - 2
                    h, b = divmod(v, NT)
                    n, st = (P if b == 0 else T), stat[:, v % 2, :]
                    dve.wait_ge(s_read, NUNIT + v + 1)
                    step(dve.reciprocal(st[:, 5:6], st[:, 2:3]))
                    dve.tensor_scalar(p_sb[:, v % 2, 0:n], p_sb[:, v % 2, 0:n], st[:, 5:6], None, ALU.mult)\
                       .then_inc(p_ready, 1)
                    if h + 1 < NH and b == 1:
                        turn_head(h + 1)
                if u < NUNIT:
                    n, st = (P if u % NT == 0 else T), stat[:, u % 2, :]
                    dve.wait_ge(s_done, NUNIT + u + 1)
                    step(dve.reduce_max(st[:, 0:1], flat0[u % 2][:, 0:n], AX.X))
                    dve.tensor_scalar(st[:, 1:2], st[:, 0:1], -SCALE_C, None, ALU.mult).then_inc(neg_ready, 1)
            out_and_route(1)
            route(1)
            experts(1)
            variance()
            for k in range(KD):
                dve.scalar_tensor_tensor(y[:, k, :], x[:, k, :], g_norm[:, 4, k:k + 1], rstd[:],
                                         ALU.mult, ALU.mult).then_inc(y_ready, 1)


def constants():
    import numpy as np
    f = np.float32
    out = {"ident": np.eye(P, dtype=f), "ones": np.ones((P, P), f),
           "iota": np.tile(np.arange(NKEY, dtype=f), (P, 1))}
    q, k = np.arange(P)[:, None], np.arange(3 * P)[None, :]
    out["mask"] = np.where(np.abs(k - P - q) <= P, 0.0, NEG).astype(f)

    def tables(dr):
        n = dr // 4
        freqs = np.power(f(10000.0), -np.arange(n, dtype=f) / f(n)).astype(f)
        t = np.arange(NL_TOK)
        row, col = (t // 64).astype(f), (t % 64).astype(f)
        ang = np.concatenate([row[:, None] * freqs, col[:, None] * freqs], axis=1).astype(f)
        cos, sin = np.cos(ang).astype(f).T, np.sin(ang).astype(f).T
        return np.concatenate([cos, cos]), np.concatenate([-sin, sin])

    def swap(dr):
        return np.roll(np.eye(dr, dtype=f), dr // 2, axis=0)

    cos, sin = tables(64)
    out["rope0"] = np.stack([np.tile(cos, (2, 1)), np.tile(sin, (2, 1))], axis=1)
    out["perm0"] = np.kron(np.eye(2, dtype=f), swap(64))
    cos, sin = tables(32)
    rope1, perm1 = np.zeros((P, 2, NL_TOK), f), np.zeros((P, P), f)
    rope1[0:64, 0] = 1.0
    rope1[64:96, 0], rope1[64:96, 1] = cos, sin
    perm1[64:96, 64:96] = swap(32)
    perm1[0:32, 96:128] = swap(32)
    out["rope1"], out["perm1"] = rope1, perm1
    out["rope_k"] = np.stack([cos, sin], axis=1)
    return {n: np.ascontiguousarray(v, dtype=f) for n, v in out.items()}


def layout(i):
    import numpy as np

    def chunks(w, n=None):
        k, m = w.shape[0] // P, w.shape[1] // P
        return w.reshape(k, P, m, P).transpose(2, 1, 0, 3).reshape(m, P, k * P)

    def columns(v):
        return v.reshape(-1, P).T

    def features(t):
        return t.T.reshape(t.shape[1] // P, P, t.shape[0]).transpose(1, 0, 2)

    o = {}
    o["x"] = features(np.concatenate([i["x_prompt"][0], i["x_sample"][0]]))
    o["c_all"] = np.broadcast_to(np.stack([i["c_ctx"], i["c"][0]]), (P, 2, D))
    o["w_mod"] = i["w_mod"].transpose(0, 2, 1).reshape(2, 48, P, D)
    o["w_mod0"] = chunks(i["w_mod"][0][:, 10 * P:16 * P])
    o["c_cols"] = np.stack([columns(i["c_ctx"]), columns(i["c"][0])], axis=2)
    o["b_mod"] = i["b_mod"].reshape(2, 48, P).transpose(2, 0, 1)
    norms = [i["g_norm1"][0], i["g_norm2"][0], i["g_norm1"][1], i["g_norm2"][1], i["g_final"]]
    o["g_norm"] = np.stack([columns(g) for g in norms], axis=1)
    o["sink"] = np.broadcast_to(i["ev_sink"][0], (P, NH))
    o["conv_w"] = i["ev_conv_w"][0].reshape(3, 4, P).transpose(2, 1, 0)
    o["g_small"] = np.concatenate([columns(i["od_g_qnorm"][0]), columns(i["od_g_kvnorm"][0])], axis=1)
    w = i["ev_w_in"][0]
    heads = [np.concatenate([w[:, 1536 + 64 * h:1600 + 64 * h] for h in (j, 4 + j)], axis=1) for j in range(4)]
    conv = [w[:, 512 * s + P * j:512 * s + P * j + P] for j in range(4) for s in range(3)]
    o["in0"] = chunks(np.concatenate(heads + [w[:, 2048:2304]] + conv, axis=1))
    w = i["ev_w_out"][0]
    rows = [w[512 + 64 * h:576 + 64 * h] for j in range(4) for h in (j, 4 + j)]
    o["out0"] = chunks(np.concatenate([w[0:512]] + rows))
    o["cache_k"] = i["cache_attn_k"][0, 0].reshape(P, P).T
    o["cache_v"] = i["cache_attn_v"][0, 0].reshape(P, P)
    w = i["od_w_in"][0]
    o["in1"] = chunks(np.concatenate([w[:, 1184:1696], w[:, 0:640], w[:, 640:768], w[:, 672:1184]], axis=1))
    uq, ukv = i["od_w_uq"][0], i["od_w_ukv"][0]
    q = uq.reshape(3, P, NH, 96).transpose(2, 1, 0, 3).reshape(NH, P, 288)
    kv = ukv.reshape(2, P, NH, P).transpose(2, 1, 0, 3).reshape(NH, P, 256)
    o["head"] = np.concatenate([q, kv], axis=2)
    o["ukv_v"] = ukv.reshape(2, P, NH, 2, 64)[:, :, :, 1].transpose(1, 0, 2, 3).reshape(P, 1024)
    o["out1"] = chunks(i["od_w_out"][0])
    o["cache_ckv"] = features(i["cache_mla_ckv"][0, 0])
    o["cache_kr"] = i["cache_mla_krope"][0, 0].T
    o["ws_t"] = i["od_w_spatial"][0].transpose(2, 0, 1)
    o["b_s"] = i["od_b_spatial"]
    o["g_sgu"] = np.broadcast_to(i["od_g_sgu"][0], (P, 512))
    o["wq"] = np.stack([chunks(i["peer_wq"][l]) for l in range(2)])
    o["subk"] = i["peer_subkeys"].reshape(2, 16, NKEY, P).transpose(0, 3, 1, 2)
    u = i["peer_u"].reshape(2, NKEY, NKEY, KD, P)
    o["u"] = u.transpose(0, 2, 4, 3, 1).reshape(2, NKEY, P, 1024)
    o["v"] = i["peer_v"].reshape(2, NKEY, NKEY, D).transpose(0, 2, 1, 3)
    return o


_OUTS = {"y": (P, KD, T), "new_k": (P, P), "new_v": (P, P), "new_ckv": (P, 2, P), "new_kr": (32, P)}


def kernel(**inputs):
    import numpy as _np
    import concourse.bacc as _bacc
    from concourse import mybir as _mybir
    from concourse.bass_utils import run_bass_kernel_spmd as _run

    f32 = _mybir.dt.float32
    nc = _bacc.Bacc("TRN2", target_bir_lowering=False, num_devices=1)
    arrays, args = {}, {}
    data = layout({n: _np.asarray(v) for n, v in inputs.items()})
    data.update(constants())
    for name, v in data.items():
        v = _np.ascontiguousarray(v)
        arrays[f"in_{name}"] = v
        args[name] = nc.dram_tensor(f"in_{name}", v.shape, _mybir.dt.from_np(v.dtype), kind="ExternalInput").ap()
    for name, shape in _OUTS.items():
        args[name] = nc.dram_tensor(f"out_{name}", shape, f32, kind="ExternalOutput").ap()
    for name in ("act_s", "gate_s"):
        args[name] = nc.dram_tensor(name, (2, NKEY, P, T), f32, kind="Internal").ap()
    build(nc, args)
    r = _run(nc, [arrays], core_ids=[0]).results[0]
    y = r["out_y"].transpose(2, 1, 0).reshape(T, D)
    new_ckv = r["out_new_ckv"].transpose(2, 1, 0).reshape(1, 1, NP_TOK, 256)
    return (_np.ascontiguousarray(y[None, 0:NP_TOK]), _np.ascontiguousarray(y[None, NP_TOK:T]),
            _np.ascontiguousarray(r["out_new_k"].T).reshape(1, 1, NP_TOK, 2, 64),
            _np.ascontiguousarray(r["out_new_v"]).reshape(1, 1, NP_TOK, 2, 64),
            _np.ascontiguousarray(new_ckv), _np.ascontiguousarray(r["out_new_kr"].T).reshape(1, 1, NP_TOK, 32))
```
